# Optimizing a Trainium2 kernel written in Bass

```python
import jax, jax.numpy as jnp
from jax import lax
import numpy as np

D_MODEL = 1024
BATCH = 1
SEQ = 512
DEPTH = 2

D_MIX = D_MODEL
RET_HEADS = 4
RET_DK = D_MIX // 16
RET_DV = D_MIX // 16
HG_HEADS = 4
HG_DK = D_MIX // 16
HG_DV = D_MIX // 16
GDN_HEADS = 4
GDN_DK = D_MIX // 8
GDN_DV = D_MIX // 8
GDN_CONV = 4
FFN_CONV = 3
D_FF = ((8 * D_MODEL // 3 + 127) // 128) * 128
RET_CHUNK = 64
HG_CHUNK = 16
GDN_CHUNK = 64
ROPE_BASE = 10000.0
NORM_EPS = 1e-6
EXP_CLIP = 80.0
PROJ_SPLITS = (
    RET_HEADS * RET_DK, RET_HEADS * RET_DK, RET_HEADS * RET_DV, RET_HEADS * RET_DV,
    HG_HEADS * HG_DK, HG_HEADS * HG_DK, HG_HEADS * HG_DV, HG_HEADS * HG_DV,
    GDN_HEADS * GDN_DK, GDN_HEADS * GDN_DK, GDN_HEADS * GDN_DV, GDN_HEADS, GDN_HEADS, GDN_HEADS * GDN_DV,
)
D_PROJ = sum(PROJ_SPLITS)

kernel_name = 'hybrid_retention_hgrn2_gdn_convffn'

def rmsnorm(x, w=None):
    xf = x.astype(jnp.float32)
    y = xf * lax.rsqrt(jnp.mean(xf * xf, axis=-1, keepdims=True) + NORM_EPS)
    if w is not None:
        y = y * w.astype(jnp.float32)
    return y.astype(x.dtype)

def l2norm(x):
    return x * lax.rsqrt(jnp.sum(x * x, axis=-1, keepdims=True) + NORM_EPS)

def causal_dwconv(x, w):
    K, C = w.shape
    return lax.conv_general_dilated(
        x, w[:, None, :].astype(x.dtype), window_strides=(1,), padding=[(K - 1, 0)],
        dimension_numbers=('NWC', 'WIO', 'NWC'), feature_group_count=C)

def rotary(x, positions):
    half = x.shape[-1] // 2
    inv_freq = ROPE_BASE ** (-jnp.arange(half, dtype=jnp.float32) / half)
    ang = positions.astype(jnp.float32)[..., None] * inv_freq
    cos, sin = jnp.cos(ang)[:, :, None, :], jnp.sin(ang)[:, :, None, :]
    x1, x2 = x[..., :half], x[..., half:]
    return jnp.concatenate([x1 * cos - x2 * sin, x1 * sin + x2 * cos], axis=-1)

def _chunks(x, C):
    B, H, T = x.shape[:3]
    return x.reshape((B, H, T // C, C) + x.shape[3:])

def masked_exp(diff, mask):
    return jnp.where(mask, jnp.exp(jnp.where(mask, diff, 0.0)), 0.0)

def diag_state_scan(U, w):
    def step(S, inp):
        U_n, w_n = inp
        return w_n * S + U_n, S
    S0 = jnp.zeros(U.shape[:2] + U.shape[3:], jnp.float32)
    _, S_prev = lax.scan(step, S0, (jnp.moveaxis(U, 2, 0), jnp.moveaxis(w, 2, 0)))
    return jnp.moveaxis(S_prev, 0, 2)

def retention_chunk(q, k, v, log_gamma):
    C = RET_CHUNK
    B, H, T, _ = q.shape
    qc, kc, vc = _chunks(q, C), _chunks(k, C), _chunks(v, C)
    idx = jnp.arange(C, dtype=jnp.float32)
    rel = idx[:, None] - idx[None, :]
    causal = rel >= 0
    lg = log_gamma[:, None, None]
    D = masked_exp(rel[None] * lg, causal[None])
    scores = jnp.einsum('bhnid,bhnjd->bhnij', qc, kc) * D[None, :, None]
    intra = jnp.einsum('bhnij,bhnje->bhnie', scores, vc)
    lg1 = log_gamma[:, None]
    q_in = qc * jnp.exp((idx + 1.0)[None] * lg1)[None, :, None, :, None]
    k_out = kc * jnp.exp((C - 1.0 - idx)[None] * lg1)[None, :, None, :, None]
    U = jnp.einsum('bhnjd,bhnje->bhnde', k_out, vc)
    N = qc.shape[2]
    w = jnp.broadcast_to(jnp.exp(C * log_gamma)[None, :, None, None, None], (1, H, N, 1, 1))
    S_prev = diag_state_scan(U, w)
    inter = jnp.einsum('bhnid,bhnde->bhnie', q_in, S_prev)
    return (intra + inter).reshape(B, H, T, -1)

def gla_chunk(q, k, v, g):
    C = HG_CHUNK
    B, H, T, _ = q.shape
    qc, kc, vc = _chunks(q, C), _chunks(k, C), _chunks(v, C)
    b = jnp.cumsum(_chunks(g, C), axis=3)
    idx = jnp.arange(C)
    causal = (idx[:, None] >= idx[None, :])[:, :, None]
    decay = masked_exp(b[:, :, :, :, None, :] - b[:, :, :, None, :, :], causal)
    scores = jnp.einsum('bhnid,bhnjd,bhnijd->bhnij', qc, kc, decay)
    intra = jnp.einsum('bhnij,bhnje->bhnie', scores, vc)
    b_last = b[:, :, :, -1:, :]
    q_in = qc * jnp.exp(b)
    k_out = kc * jnp.exp(b_last - b)
    U = jnp.einsum('bhnjd,bhnje->bhnde', k_out, vc)
    w = jnp.exp(b_last[:, :, :, 0, :])[..., None]
    S_prev = diag_state_scan(U, w)
    inter = jnp.einsum('bhnid,bhnde->bhnie', q_in, S_prev)
    return (intra + inter).reshape(B, H, T, -1)

def gated_delta_chunk(q, k, v, g, beta):
    C = GDN_CHUNK
    B, H, T, dk = q.shape
    dv = v.shape[-1]
    qc, kc, vc = _chunks(q, C), _chunks(k, C), _chunks(v, C)
    b = jnp.cumsum(_chunks(g, C), axis=-1)
    bc = _chunks(beta, C)[..., None]
    idx = jnp.arange(C)
    causal = idx[:, None] >= idx[None, :]
    strict = idx[:, None] > idx[None, :]
    decay = masked_exp(b[..., :, None] - b[..., None, :], causal)
    kb = kc * bc
    L = jnp.where(strict, jnp.einsum('bhnid,bhnjd->bhnij', kb, kc) * decay, 0.0)
    rhs = jnp.concatenate([vc * bc, kb * jnp.exp(b)[..., None]], axis=-1)
    sol = lax.linalg.triangular_solve(L, rhs, left_side=True, lower=True, unit_diagonal=True)
    u, kcd = sol[..., :dv], sol[..., dv:]
    attn = jnp.einsum('bhnid,bhnjd->bhnij', qc, kc) * decay
    q_in = qc * jnp.exp(b)[..., None]
    k_out = kc * jnp.exp(b[..., -1:] - b)[..., None]
    w = jnp.exp(b[..., -1])

    def step(S, inp):
        u_n, kcd_n, q_n, k_n, a_n, w_n = inp
        v_new = u_n - jnp.einsum('bhcd,bhde->bhce', kcd_n, S)
        o_n = jnp.einsum('bhcd,bhde->bhce', q_n, S) + jnp.einsum('bhij,bhje->bhie', a_n, v_new)
        S = S * w_n[..., None, None] + jnp.einsum('bhcd,bhce->bhde', k_n, v_new)
        return S, o_n

    xs = tuple(jnp.moveaxis(t, 2, 0) for t in (u, kcd, q_in, k_out, attn, w))
    S0 = jnp.zeros((B, H, dk, dv), jnp.float32)
    _, o = lax.scan(step, S0, xs)
    return jnp.moveaxis(o, 0, 2).reshape(B, H, T, dv)

def hybrid_mixer(h, positions, w_in, lb, conv_w, A_log, dt_bias, hg_norm_w, gdn_norm_w, w_out):
    B, T, _ = h.shape
    f32 = jnp.float32
    proj = h @ w_in
    split_at = np.cumsum(PROJ_SPLITS)[:-1].tolist()
    (rq, rk, rv, rg, hq, hf, hi, hg, gq, gk, gv, ga, gb, gg) = jnp.split(proj, split_at, axis=-1)

    def heads(t, H):
        return t.astype(f32).reshape(B, T, H, -1)

    def bhtd(t):
        return jnp.transpose(t, (0, 2, 1, 3))

    rq_h = rotary(heads(rq, RET_HEADS), positions)
    rk_h = rotary(heads(rk, RET_HEADS), positions) * RET_DK ** -0.5
    log_gamma = jnp.log1p(-jnp.exp2(-5.0 - jnp.arange(RET_HEADS, dtype=f32)))
    o = retention_chunk(bhtd(rq_h), bhtd(rk_h), bhtd(heads(rv, RET_HEADS)), log_gamma)
    o_ret = (rmsnorm(bhtd(o)) * jax.nn.silu(heads(rg, RET_HEADS))).reshape(B, T, -1)

    z = heads(hf, HG_HEADS)
    lb_h = lb.astype(f32).reshape(HG_HEADS, HG_DK)
    log_f = jax.nn.log_sigmoid(z) + jnp.log1p(lb_h * jnp.exp(jnp.minimum(-z, EXP_CLIP)))
    k_in = (1.0 - lb_h) * jax.nn.sigmoid(-z)
    o = gla_chunk(bhtd(jax.nn.silu(heads(hq, HG_HEADS))), bhtd(k_in), bhtd(heads(hi, HG_HEADS)), bhtd(log_f))
    o_hg = (rmsnorm(bhtd(o), hg_norm_w) * jax.nn.silu(heads(hg, HG_HEADS))).reshape(B, T, -1)

    qkv = jax.nn.silu(causal_dwconv(jnp.concatenate([gq, gk, gv], axis=-1), conv_w).astype(f32))
    cq, ck, cv = jnp.split(qkv, [GDN_HEADS * GDN_DK, 2 * GDN_HEADS * GDN_DK], axis=-1)
    q = l2norm(cq.reshape(B, T, GDN_HEADS, GDN_DK)) * GDN_DK ** -0.5
    k = l2norm(ck.reshape(B, T, GDN_HEADS, GDN_DK))
    v = cv.reshape(B, T, GDN_HEADS, GDN_DV)
    g = -jnp.exp(A_log.astype(f32)) * jax.nn.softplus(ga.astype(f32) + dt_bias.astype(f32))
    beta = jax.nn.sigmoid(gb.astype(f32))
    o = gated_delta_chunk(bhtd(q), bhtd(k), bhtd(v), jnp.transpose(g, (0, 2, 1)), jnp.transpose(beta, (0, 2, 1)))
    o_gdn = (rmsnorm(bhtd(o), gdn_norm_w) * jax.nn.silu(heads(gg, GDN_HEADS))).reshape(B, T, -1)

    mixed = jnp.concatenate([o_ret, o_hg, o_gdn], axis=-1).astype(h.dtype)
    return mixed @ w_out

def conv_ffn(h, w_up, conv_w, conv_b, w_down):
    u = causal_dwconv(h @ w_up, conv_w) + conv_b
    gate, val = jnp.split(u, 2, axis=-1)
    return (jax.nn.silu(gate) * val) @ w_down

def setup_inputs(seed: int = 0) -> dict:
    key = jax.random.key(seed)
    ks = jax.random.split(key, 18)
    f32 = jnp.float32
    nrm = lambda k, s: jax.random.normal(k, s, f32)
    dt = jnp.exp(jax.random.uniform(ks[6], (DEPTH, GDN_HEADS), f32, np.log(1e-3), np.log(1e-1)))
    return {
        'x': nrm(ks[0], (BATCH, SEQ, D_MODEL)),
        'positions': jnp.broadcast_to(jnp.arange(SEQ, dtype=jnp.int32), (BATCH, SEQ)),
        'norm1_w': 1.0 + 0.02 * nrm(ks[1], (DEPTH, D_MODEL)),
        'w_in': nrm(ks[2], (DEPTH, D_MODEL, D_PROJ)) * D_MODEL ** -0.5,
        'hg_lb_logits': 0.5 * nrm(ks[3], (DEPTH, HG_HEADS * HG_DK)),
        'gdn_conv_w': nrm(ks[4], (DEPTH, GDN_CONV, GDN_HEADS * (2 * GDN_DK + GDN_DV))) * GDN_CONV ** -0.5,
        'gdn_A_log': jnp.log(jax.random.uniform(ks[5], (DEPTH, GDN_HEADS), f32, 1.0, 16.0)),
        'gdn_dt_bias': dt + jnp.log(-jnp.expm1(-dt)),
        'hg_norm_w': 1.0 + 0.02 * nrm(ks[7], (DEPTH, HG_DV)),
        'gdn_norm_w': 1.0 + 0.02 * nrm(ks[8], (DEPTH, GDN_DV)),
        'w_out': nrm(ks[9], (DEPTH, D_MIX, D_MODEL)) * D_MIX ** -0.5,
        'norm2_w': 1.0 + 0.02 * nrm(ks[10], (DEPTH, D_MODEL)),
        'w_up': nrm(ks[11], (DEPTH, D_MODEL, 2 * D_FF)) * D_MODEL ** -0.5,
        'ffn_conv_w': nrm(ks[12], (DEPTH, FFN_CONV, 2 * D_FF)) * FFN_CONV ** -0.5,
        'ffn_conv_b': 0.01 * nrm(ks[13], (DEPTH, 2 * D_FF)),
        'w_down': nrm(ks[14], (DEPTH, D_FF, D_MODEL)) * D_FF ** -0.5,
        'final_norm_w': 1.0 + 0.02 * nrm(ks[15], (D_MODEL,)),
    }

def reference(x, positions, norm1_w, w_in, hg_lb_logits, gdn_conv_w, gdn_A_log, gdn_dt_bias,
              hg_norm_w, gdn_norm_w, w_out, norm2_w, w_up, ffn_conv_w, ffn_conv_b, w_down,
              final_norm_w):
    p = jax.nn.softmax(hg_lb_logits.astype(jnp.float32), axis=0)
    lower_bounds = jnp.maximum(jnp.cumsum(p, axis=0) - p[0:1], 0.0)
    for layer in range(DEPTH):
        h = rmsnorm(x, norm1_w[layer])
        x = x + hybrid_mixer(h, positions, w_in[layer], lower_bounds[layer], gdn_conv_w[layer],
                             gdn_A_log[layer], gdn_dt_bias[layer], hg_norm_w[layer],
                             gdn_norm_w[layer], w_out[layer])
        h = rmsnorm(x, norm2_w[layer])
        x = x + conv_ffn(h, w_up[layer], ffn_conv_w[layer], ffn_conv_b[layer], w_down[layer])
    return rmsnorm(x, final_norm_w)


_drawn_inputs = setup_inputs


def setup_inputs(seed=0):
    import zlib

    import numpy as np

    out = dict(_drawn_inputs(seed))
    spreads = {}
    factors = {'hg_lb_logits': 3.114,
     'hg_norm_w': 6.26,
     'gdn_norm_w': 5.162,
     'norm2_w': 2.802,
     'ffn_conv_b': 5.584,
     'final_norm_w': 2.861}
    for name, (base, spread) in spreads.items():
        noise = np.random.default_rng([zlib.crc32(name.encode()), seed]).standard_normal(out[name].shape)
        drawn = base * np.exp(spread * noise) if base else spread * noise
        out[name] = __import__('jax').numpy.asarray(drawn.astype(out[name].dtype))
    for name, factor in factors.items():
        out[name] = (out[name] * factor).astype(out[name].dtype)
    return out
```

```python
from contextlib import ExitStack

import numpy as np

import concourse.bass as bass
from concourse import mybir

F32 = mybir.dt.float32
F32R = mybir.dt.float32r
I32 = mybir.dt.int32
ACT = mybir.ActivationFunctionType
ALU = mybir.AluOpType

P = 128
D_MODEL = 1024
SEQ = 512
DEPTH = 2
C = 128
NC = SEQ // C
KT = D_MODEL // P
HEADS = 4
D_FF = 2816
FT = D_FF // P
EPS = 1e-6

COPY_UNITS, CONV_UNITS, GATE_UNITS = 10, 12, 10
IN_UNITS = COPY_UNITS + CONV_UNITS + GATE_UNITS
OUT_UNITS = KT
UP_UNITS = 2 * FT
DOWN_UNITS = FT
UNITS = IN_UNITS + OUT_UNITS + UP_UNITS + DOWN_UNITS
CONV0, GATE0 = COPY_UNITS, COPY_UNITS + CONV_UNITS
OUT0, UP0, DOWN0 = IN_UNITS, IN_UNITS + OUT_UNITS, IN_UNITS + OUT_UNITS + UP_UNITS

LEVELS = [1, 2, 4, 8, 16, 32, 64]

CONSTS = {}
_at = 0
for _name, _n in (("ident", C), ("mean_model", P), ("ones", P), ("mean64", P), ("mean128", P), ("causal", C),
                  ("lvl", len(LEVELS) * C), ("ret_decay", HEADS * C), ("ret_q", 2 * C), ("ret_k", 2 * P),
                  ("blocks", P), ("rot", P), ("ret_w", 2), ("inv_freq", 1)):
    CONSTS[_name] = (_at, _n)
    _at += _n
N_CONST = _at
PARAMS = {}
_at = 0
for _name, _n in (("norm1", KT), ("norm2", KT), ("gdn_conv", CONV_UNITS * 4), ("ffn_conv", UP_UNITS * 3),
                  ("ffn_bias", UP_UNITS), ("onorm", KT), ("a_log", HEADS), ("dt_bias", HEADS), ("w_ab", KT * 8)):
    PARAMS[_name] = (_at, _n)
    _at += _n
N_PARAM = _at

PER_LAYER = dict(
    x_after_mixer=8, x_after_ffn=8, x_squared=16, x_mean_square=2, rstd_log=2, rstd_ready=2, x_normed=16, h_hi_ready=16, h_lo_ready=16,
    params_copied=1, wab_hi_ready=1, wab_lo_ready=1, ab_projected=1, ab_copied=1, ab_turned=1, gate_dve_step=14, gate_act_step=8, b_token_major=1, b_spread=4, b_diff_ready=4, exp_b_ready=4, decay_exp=4, decay_masked=4,
    hi_ready=UNITS, lo_ready=UNITS, unit_used=UNITS,
    conv_last_tap=12, conv_mid_taps=24, conv_done=12, qkv_silu=12, bank_copied=20,
    kv_turned=8, kv_turned_read=8, k_out_ready=4, l2_squared=8, l2_summed=8, l2_log=8, l2_rnorm=8, qk_normed=8,
    kk_qk_products=4, kk_decayed=4, g_attn_ready=4, q_in_ready=4, g_smallest=4, inv_first=4, inv_first_turned=4, inv_t_first=4,
    g_level=24, gt_product=24, gt_copied=24, tgt_product=24, inv_t_updated=24, inv_turned=24, inv_r_updated=24, kcd_product=4, kcd_ready=4,
    v_new_product=4, v_new_ready=4, state_sum=3, delta_out=4, state_ready=3, delta_out_copied=4,
    rotated=4, rot_sin=4, rot_cos=4, rot_done=4, ret_scores=4, ret_decayed=4, ret_q_in=2, ret_turned=4, ret_k_out=2, ret_v_copied=2, ret_sums=2, ret_states=6, ret_out=2, ret_out_copied=2,
    hg_dve_step=15, hg_act_step=8, hg_q_in=1, level_diff=7, level_exp=7, level_qk=7, hg_scores=32, hg_scores_placed=32, hg_turned=4, hg_turned_copied=4, hg_sums=2, hg_states=6, hg_out=2, hg_out_copied=2,
    out_squared=8, out_mean_square=8, out_log=8, out_rstd=8, out_normed=8, out_gated=8, mix_hi_ready=8, mix_lo_ready=8,
    out_projected=7, ffn_last_tap=UP_UNITS, ffn_mid_tap=UP_UNITS, ffn_conv_done=UP_UNITS, ffn_silu=FT, ffn_product=FT, g_hi_ready=FT, g_lo_ready=FT, down_projected=7,
)


def build(nc, x_in, pos_in, const_in, par_in, lb_in, fin_in, w_in, out):
    ctx = ExitStack()
    with ctx:
        def sb(name, shape, dt=F32, where=ctx):
            return where.enter_context(nc.sbuf_tensor(name, shape, dt))

        s = {name: ctx.enter_context(nc.semaphore(name)) for name in PER_LAYER}
        per = PER_LAYER
        setup_loaded = ctx.enter_context(nc.semaphore("setup_loaded"))
        x_loaded = ctx.enter_context(nc.semaphore("x_loaded"))
        loaded = ctx.enter_context(nc.semaphore("loaded"))
        raw_loaded = [ctx.enter_context(nc.semaphore(f"raw_loaded{i}")) for i in range(2)]
        setup_dve = ctx.enter_context(nc.semaphore("setup_dve"))
        SETUP_LB, SETUP_ANGLES = 2, 26
        setup_act = ctx.enter_context(nc.semaphore("setup_act"))
        stored = ctx.enter_context(nc.semaphore("stored"))
        carrier = ctx.enter_context(nc.semaphore("carrier"))

        def apart(eng):
            eng.sem_inc(carrier)

        cst = sb("cst", [P, N_CONST])
        par = sb("par", [P, DEPTH, N_PARAM])
        cur = sb("cur", [P, N_PARAM])
        lb = sb("lb", [P, DEPTH, 4])
        lb_cur = sb("lb_cur", [P, 4])
        fin = sb("fin", [P, KT])
        sin_t = sb("sin_t", [P, SEQ])
        cos_t = sb("cos_t", [P, SEQ])
        x = sb("x", [P, KT, SEQ])
        rstd = sb("rstd", [P, SEQ])
        h_hi = sb("h_hi", [P, KT, SEQ], F32R)
        h_lo = sb("h_lo", [P, KT, SEQ], F32R)
        raw = sb("raw", [P, 2, KT * P])
        w_hi = sb("w_hi", [P, 2, KT * P], F32R)
        w_lo = sb("w_lo", [P, 2, KT * P], F32R)
        wab_hi = sb("wab_hi", [P, KT, 8], F32R)
        wab_lo = sb("wab_lo", [P, KT, 8], F32R)
        small = sb("small", [P, 16, 16])
        abc = sb("abc", [P, NC, 8])
        lbw = sb("lbw", [P, 8])
        bank = [ctx.enter_context(nc.psum_tensor(f"bank{i}", [P, 512], F32)) for i in range(8)]

        with ExitStack() as mixer_mem:
            gqkv = sb("gqkv", [P, 12, SEQ], F32, mixer_mem)
            gate = sb("gate", [P, GATE_UNITS, SEQ], F32, mixer_mem)
            cp = sb("cp", [P, COPY_UNITS, SEQ], F32, mixer_mem)
            area_a = sb("area_a", [P, 12, SEQ], F32, mixer_mem)
            area_b = sb("area_b", [P, 12, SEQ], F32, mixer_mem)
        with ExitStack() as ffn_mem:
            g_hi = sb("g_hi", [P, FT, SEQ], F32R, ffn_mem)
            g_lo = sb("g_lo", [P, FT, SEQ], F32R, ffn_mem)
            cg = sb("cg", [P, SEQ], F32, ffn_mem)
            cv = sb("cv", [P, SEQ], F32, ffn_mem)
            gt = sb("gt", [P, SEQ], F32, ffn_mem)

        def const(name, i=0, n=None):
            a, _n = CONSTS[name]
            n = _n if n is None else n
            return cst[:, a + i * n:a + (i + 1) * n]

        def param(name, i=0, n=1):
            a, _ = PARAMS[name]
            return cur[:, bass.ds(a + i * n, n)] if not isinstance(i, int) else cur[:, a + i * n:a + (i + 1) * n]

        def chunks(ap):
            return ap.rearrange("p (c i) -> p c i", c=NC)

        def per_chunk(ap):
            return ap.unsqueeze(1).broadcast_to([P, NC, C])

        def per_token(ap):
            return ap.unsqueeze(2).broadcast_to([P, ap.shape[1], C])

        ident, causal = const("ident"), const("causal")
        k_out, k_be, v_b = (area_a[:, 4 * i:4 * i + 4, :] for i in range(3))
        T, R, attn = (area_b[:, 4 * i:4 * i + 4, :] for i in range(3))
        decay, e_b, kcd = T, R, T
        G = gqkv[:, 4:8, :]
        ab_rows = area_a[0:8, 11, :]
        ml_ring, p_ring = gqkv[:, 8:10, :], gqkv[:, 10:12, :]
        vn_ring, S_ring = ml_ring, p_ring
        oT = gqkv[:, 0:8, :]
        scratch = gqkv[:, 2:4, :]
        PT = area_a[:, 0:4, :]
        k_tok, v_tok = area_a[:, 4:6, :], area_a[:, 6:8, :]
        SU = area_a[:, 8:10, :]
        slot = [area_b[:, 2 * i:2 * i + 2, :].rearrange("p t n -> p (t n)") for i in range(6)]
        hz = cp[:, 6:8, :].rearrange("p t n -> p (t n)")
        hq = gate[:, 8:10, :].rearrange("p t n -> p (t n)")

        za, sp, g_tok, nb, beta, btok, bl, dko, e_tok, ko, w_dec, be, hbl, hw, e_a, abt = (
            small[:, i, :] for i in range(16))

        def hc(ap):
            return ap.rearrange("p (h c) -> p h c", h=HEADS)


        block = ctx.enter_context(nc.Block())

        @block.sync
        def _(sp_):
            freq = CONSTS["ret_w"][0]
            for dst, src in ((slot[0][:, 0:SEQ].bitcast(I32), pos_in), (cst[:, freq:], const_in[:, freq:]),
                             (lb[:, :, 0:2], lb_in)):
                sp_.dma_start(dst, src).then_inc(setup_loaded, 16)
            for k in range(KT):
                sp_.dma_start(x[:, k, :], x_in[:, k, :]).then_inc(x_loaded, 16)
            for dst, src in ((par[:, :, :], par_in), (fin[:, :], fin_in), (cst[:, :freq], const_in[:, :freq])):
                sp_.dma_start(dst, src).then_inc(loaded, 16)
            for u in range(2):
                sp_.dma_start(raw[:, u, :], w_in[u]).then_inc(raw_loaded[u], 16)
            with sp_.Fori(1, DEPTH * UNITS // 2) as q:
                for u in range(2):
                    sp_.wait_ge(s["lo_ready"], 2 * q + u - 1)
                    sp_.dma_start(raw[:, u, :], w_in[2 * q + u]).then_inc(raw_loaded[u], 16)
            for k in range(KT):
                sp_.wait_ge(s["x_normed"], DEPTH * 16 + k + 1)
                sp_.dma_start(out[:, k, :], gqkv[:, k, :]).then_inc(stored, 16)
            sp_.wait_ge(stored, 16 * KT)

        @block.gpsimd
        def _(pool):
            tt = nc.gpsimd.tensor_tensor

            def norm_lo(L, which):
                for k in range(KT):
                    pool.wait_ge(s["h_hi_ready"], L * per["h_hi_ready"] + 8 * which + k + 1)
                    tt(h_lo[:, k, :], gqkv[:, k, :], h_hi[:, k, :].bitcast(F32),
                       ALU.subtract).then_inc(s["h_lo_ready"], 1)

            with pool.Fori(0, DEPTH) as L:
                norm_lo(L, 0)
                for h in range(HEADS):
                    pool.wait_ge(s["decay_exp"], L * per["decay_exp"] + h + 1)
                    tt(chunks(decay[:, h, :]), chunks(decay[:, h, :]), per_chunk(causal),
                       ALU.mult).then_inc(s["decay_masked"], 1)
                for h in range(HEADS):
                    pool.wait_ge(s["kk_qk_products"], L * per["kk_qk_products"] + h + 1)
                    pool.wait_ge(s["exp_b_ready"], L * per["exp_b_ready"] + h + 1)
                    tt(gqkv[:, h, :], gqkv[:, h, :], e_b[:, h, :], ALU.mult).then_inc(s["q_in_ready"], 1)
                for h in range(HEADS):
                    pool.wait_ge(s["g_attn_ready"], L * per["g_attn_ready"] + h + 1)
                    pool.wait_ge(s["q_in_ready"], L * per["q_in_ready"] + h + 1)
                    tt(chunks(R[:, h, :]), chunks(G[:, h, :]), per_chunk(const("lvl", 0, C)),
                       ALU.mult).then_inc(s["g_smallest"], 1)
                    pool.wait_ge(s["g_smallest"], L * per["g_smallest"] + h + 1)
                    tt(chunks(R[:, h, :]), per_chunk(ident), chunks(R[:, h, :]),
                       ALU.subtract).then_inc(s["inv_first"], 1)
                for k in range(24):
                    if k >= 2:
                        pool.wait_ge(s["gt_product"], L * per["gt_product"] + k - 1)
                    else:
                        pool.wait_ge(s["g_attn_ready"], L * per["g_attn_ready"] + 4)
                        pool.wait_ge(s["kv_turned"], L * per["kv_turned"] + 4)
                    tt(chunks(ml_ring[:, k % 2, :]), chunks(G[:, k % 4, :]), per_chunk(const("lvl", 1 + k // 4, C)),
                       ALU.mult).then_inc(s["g_level"], 1)
                for t in range(4):
                    pool.wait_ge(s["rotated"], L * per["rotated"] + t + 1)
                    tt(cp[:, t, :], cp[:, t, :], cos_t[:, :], ALU.mult).then_inc(s["rot_cos"], 1)
                for t in range(2):
                    pool.wait_ge(s["ret_scores"], L * per["ret_scores"] + 2 * t + 2)
                    tt(chunks(cp[:, t, :]), chunks(cp[:, t, :]), per_chunk(const("ret_q", t, C)),
                       ALU.mult).then_inc(s["ret_q_in"], 1)
                pool.wait_ge(s["hg_act_step"], L * per["hg_act_step"] + 7)
                tt(slot[2], slot[2], hq, ALU.mult).then_inc(s["hg_q_in"], 1)
                for n, half in enumerate(LEVELS):
                    X = slot[3 + 2 * (n % 2)].rearrange("p (g s) -> p g s", s=2 * half)
                    b = slot[0].rearrange("p (g s) -> p g s", s=2 * half)
                    ref = b[:, :, half - 1:half].broadcast_to([P, 2 * SEQ // (2 * half), half])
                    if n >= 2:
                        pool.wait_ge(s["hg_scores"], L * per["hg_scores"] + 4 * (n - 1))
                    else:
                        pool.wait_ge(s["hg_dve_step"], L * per["hg_dve_step"] + 12)
                    tt(X[:, :, 0:half], ref, b[:, :, 0:half], ALU.subtract)
                    tt(X[:, :, half:], b[:, :, half:], ref, ALU.subtract).then_inc(s["level_diff"], 1)
                norm_lo(L, 1)

        @block.scalar
        def _(act):
            A = nc.scalar.activation

            def split_hi(q, u):
                act.wait_ge(raw_loaded[u], 16 * q + 16)
                A(w_hi[:, u, :], raw[:, u, :], ACT.Copy).then_inc(s["hi_ready"], 1)

            def norm(L, which, meanwhile=None):
                nc.scalar.preload_act_table_set("natural_log_exp_and_others")
                for k in range(KT):
                    if which == 0:
                        act.wait_ge(s["x_after_ffn"], L * per["x_after_ffn"] + k + 1)
                    else:
                        act.wait_ge(s["x_after_mixer"], L * per["x_after_mixer"] + k + 1)
                    A(gqkv[:, k, :], x[:, k, :], ACT.Square).then_inc(s["x_squared"], 1)
                if meanwhile:
                    meanwhile()
                act.wait_ge(s["x_mean_square"], L * per["x_mean_square"] + which + 1)
                A(rstd[:, :], bank[2][:, :], ACT.Ln, bias=EPS).then_inc(s["rstd_log"], 1)
                act.wait_ge(s["rstd_log"], L * per["rstd_log"] + which + 1)
                A(rstd[:, :], rstd[:, :], ACT.Exp, scale=-0.5).then_inc(s["rstd_ready"], 1)

            def norm_hi(L, which):
                for k in range(KT):
                    act.wait_ge(s["x_normed"], L * per["x_normed"] + 8 * which + k + 1)
                    A(h_hi[:, k, :], gqkv[:, k, :], ACT.Copy).then_inc(s["h_hi_ready"], 1)

            act.wait_ge(setup_dve, SETUP_LB)
            A(lbw[:, 0:4], lbw[:, 0:4], ACT.Exp).then_inc(setup_act, 1)
            act.wait_ge(setup_dve, SETUP_ANGLES)
            A(sin_t[:, :], sin_t[:, :], ACT.Sin).then_inc(setup_act, 1)
            A(cos_t[:, :], cos_t[:, :], ACT.Sin).then_inc(setup_act, 1)

            with act.Fori(0, DEPTH) as L:
                norm(L, 0, lambda: [split_hi(L * (UNITS // 2), u) for u in range(2)])
                norm_hi(L, 0)
                act.wait_ge(s["params_copied"], L * per["params_copied"] + 1)
                A(wab_hi[:, :, :], param("w_ab", 0, KT * 8).rearrange("p (k n) -> p k n", k=KT),
                  ACT.Copy).then_inc(s["wab_hi_ready"], 1)

                q0 = L * (UNITS // 2)

                def copy_unit(i, u):
                    act.wait_ge(s["unit_used"], L * per["unit_used"] + 2 * i + u + 1)
                    split_hi(q0 + i + 1, u)
                    A(cp[:, 2 * i + u, :], bank[u][:, :], ACT.Copy).then_inc(s["bank_copied"], 1)

                def spread_exps(h):
                    act.wait_ge(s["b_diff_ready"], L * per["b_diff_ready"] + h + 1)
                    A(e_b[:, h, :], bank[2 + h][:, :], ACT.Exp).then_inc(s["exp_b_ready"], 1)
                    A(decay[:, h, :], decay[:, h, :], ACT.Exp).then_inc(s["decay_exp"], 1)

                copy_unit(0, 0)
                copy_unit(0, 1)
                act.wait_ge(s["gate_dve_step"], L * per["gate_dve_step"] + 2)
                A(sp, za, ACT.Abs).then_inc(s["gate_act_step"], 1)
                act.wait_ge(s["gate_act_step"], L * per["gate_act_step"] + 1)
                A(sp, sp, ACT.Exp, scale=-1.0).then_inc(s["gate_act_step"], 1)
                act.wait_ge(s["gate_act_step"], L * per["gate_act_step"] + 2)
                A(sp, sp, ACT.Ln, bias=1.0).then_inc(s["gate_act_step"], 1)
                A(e_a[:, 0:4], param("a_log", 0, 4), ACT.Exp).then_inc(s["gate_act_step"], 1)
                act.wait_ge(s["gate_dve_step"], L * per["gate_dve_step"] + 3)
                A(nb, nb, ACT.Exp).then_inc(s["gate_act_step"], 1)
                copy_unit(1, 0)
                act.wait_ge(s["gate_dve_step"], L * per["gate_dve_step"] + 8)
                A(e_tok, btok, ACT.Exp).then_inc(s["gate_act_step"], 1)
                spread_exps(0)
                spread_exps(1)
                copy_unit(1, 1)
                spread_exps(2)
                spread_exps(3)
                act.wait_ge(s["gate_dve_step"], L * per["gate_dve_step"] + 13)
                A(ko, dko, ACT.Exp).then_inc(s["gate_act_step"], 1)
                A(w_dec, bl, ACT.Exp).then_inc(s["gate_act_step"], 1)
                with act.Fori(2, COPY_UNITS // 2) as i:
                    for u in range(2):
                        copy_unit(i, u)

                nc.scalar.preload_act_table_set("silu_and_others")
                with act.Fori(0, CONV_UNITS // 2) as i:
                    for u in range(2):
                        act.wait_ge(s["unit_used"], L * per["unit_used"] + CONV0 + 2 * i + u + 1)
                        apart(act)
                        A(gqkv[:, 2 * i + u, :], bank[u][:, :], ACT.Copy,
                          scale=param("gdn_conv", (2 * i + u) * 4 + 3)).then_inc(s["conv_last_tap"], 1)
                        split_hi(q0 + CONV0 // 2 + i + 1, u)
                        act.wait_ge(s["conv_done"], L * per["conv_done"] + 2 * i + u + 1)
                        apart(act)
                        A(gqkv[:, 2 * i + u, :], gqkv[:, 2 * i + u, :], ACT.Silu).then_inc(s["qkv_silu"], 1)
                with act.Fori(0, GATE_UNITS // 2) as i:
                    for u in range(2):
                        act.wait_ge(s["unit_used"], L * per["unit_used"] + GATE0 + 2 * i + u + 1)
                        split_hi(q0 + GATE0 // 2 + i + 1, u)
                        A(gate[:, 2 * i + u, :], bank[u][:, :], ACT.Silu).then_inc(s["bank_copied"], 1)

                nc.scalar.preload_act_table_set("natural_log_exp_and_others")
                act.wait_ge(s["qkv_silu"], L * per["qkv_silu"] + 12)
                act.wait_ge(s["x_normed"], L * per["x_normed"] + 8)
                for t in range(8):
                    A(area_a[:, t, :], gqkv[:, t, :], ACT.Square).then_inc(s["l2_squared"], 1)
                for t in range(8):
                    act.wait_ge(s["l2_summed"], L * per["l2_summed"] + t + 1)
                    A(area_a[:, t, :], bank[t % 2][:, :], ACT.Ln, bias=EPS).then_inc(s["l2_log"], 1)
                    act.wait_ge(s["l2_log"], L * per["l2_log"] + t + 1)
                    A(area_a[:, t, :], area_a[:, t, :], ACT.Exp, scale=-0.5).then_inc(s["l2_rnorm"], 1)
                for h in range(HEADS):
                    act.wait_ge(s["inv_first_turned"], L * per["inv_first_turned"] + h + 1)
                    A(T[:, h, :], bank[4 + h % 2][:, :], ACT.Copy).then_inc(s["inv_t_first"], 1)
                for k in range(24 + 2):
                    if k < 24:
                        act.wait_ge(s["gt_product"], L * per["gt_product"] + k + 1)
                        if k >= 2:
                            act.wait_ge(s["tgt_product"], L * per["tgt_product"] + k - 1)
                        A(p_ring[:, k % 2, :], bank[k % 2][:, :], ACT.Copy).then_inc(s["gt_copied"], 1)
                    if k >= 2:
                        act.wait_ge(s["inv_turned"], L * per["inv_turned"] + k - 1)
                        A(R[:, (k - 2) % 4, :], bank[4 + k % 2][:, :], ACT.Copy).then_inc(s["inv_r_updated"], 1)
                for h in range(HEADS):
                    act.wait_ge(s["kcd_product"], L * per["kcd_product"] + h + 1)
                    A(kcd[:, h, :], bank[6 + h % 2][:, :], ACT.Copy, scale=-1.0).then_inc(s["kcd_ready"], 1)
                for c in range(NC):
                    act.wait_ge(s["v_new_product"], L * per["v_new_product"] + c + 1)
                    if c >= 2:
                        act.wait_ge(s["delta_out"], L * per["delta_out"] + c - 1)
                    A(vn_ring[:, c % 2, :], bank[c % 2][:, :], ACT.Copy).then_inc(s["v_new_ready"], 1)
                act.wait_ge(s["delta_out"], L * per["delta_out"] + 4)
                for h in range(HEADS):
                    A(oT[:, 4 + h, :], bank[2 + h][:, :], ACT.Copy).then_inc(s["delta_out_copied"], 1)

                for t in range(2):
                    act.wait_ge(s["ret_turned"], L * per["ret_turned"] + 3 + t)
                    A(v_tok[:, t, :], bank[6 + t][:, :], ACT.Copy).then_inc(s["ret_v_copied"], 1)
                for t in range(2):
                    act.wait_ge(s["ret_out"], L * per["ret_out"] + t + 1)
                    A(oT[:, t, :], bank[6 + t][:, :], ACT.Copy).then_inc(s["ret_out_copied"], 1)

                act.wait_ge(s["hg_dve_step"], L * per["hg_dve_step"] + 1)
                A(slot[0], slot[0], ACT.Exp).then_inc(s["hg_act_step"], 1)
                act.wait_ge(s["hg_act_step"], L * per["hg_act_step"] + 1)
                A(slot[2], slot[0], ACT.Ln, bias=1.0).then_inc(s["hg_act_step"], 1)
                act.wait_ge(s["hg_dve_step"], L * per["hg_dve_step"] + 3)
                A(slot[3], slot[1], ACT.Exp, scale=-1.0).then_inc(s["hg_act_step"], 1)
                act.wait_ge(s["hg_dve_step"], L * per["hg_dve_step"] + 4)
                A(slot[3], slot[3], ACT.Ln).then_inc(s["hg_act_step"], 1)
                act.wait_ge(s["hg_dve_step"], L * per["hg_dve_step"] + 6)
                A(slot[4], slot[4], ACT.Exp).then_inc(s["hg_act_step"], 1)
                act.wait_ge(s["hg_dve_step"], L * per["hg_dve_step"] + 13)
                A(slot[1], slot[1], ACT.Exp).then_inc(s["hg_act_step"], 1)
                A(slot[2], slot[0], ACT.Exp).then_inc(s["hg_act_step"], 1)
                A(hw[:, 0:8], hbl[:, 0:8], ACT.Exp).then_inc(s["hg_act_step"], 1)
                for n in range(len(LEVELS)):
                    act.wait_ge(s["level_diff"], L * per["level_diff"] + n + 1)
                    A(slot[3 + 2 * (n % 2)], slot[3 + 2 * (n % 2)], ACT.Exp).then_inc(s["level_exp"], 1)
                    if n == 2:
                        for t in range(4):
                            act.wait_ge(s["hg_turned"], L * per["hg_turned"] + t + 1)
                            dst = k_tok if t < 2 else v_tok
                            A(dst[:, t % 2, :], bank[4 + t][:, :], ACT.Copy).then_inc(s["hg_turned_copied"], 1)
                for t in range(2):
                    act.wait_ge(s["hg_out"], L * per["hg_out"] + t + 1)
                    A(oT[:, 2 + t, :], bank[6 + t][:, :], ACT.Copy).then_inc(s["hg_out_copied"], 1)

                for t in range(8):
                    if t == 0:
                        act.wait_ge(s["ret_out_copied"], L * per["ret_out_copied"] + 2)
                        act.wait_ge(s["delta_out_copied"], L * per["delta_out_copied"] + 4)
                        act.wait_ge(s["hg_out_copied"], L * per["hg_out_copied"] + 2)
                        act.wait_ge(s["hg_out"], L * per["hg_out"] + 2)
                    A(area_a[:, t, :], oT[:, t, :], ACT.Square).then_inc(s["out_squared"], 1)
                for t in range(8):
                    act.wait_ge(s["out_mean_square"], L * per["out_mean_square"] + t + 1)
                    A(area_a[:, t, :], bank[t % 2][:, :], ACT.Ln, bias=EPS).then_inc(s["out_log"], 1)
                    act.wait_ge(s["out_log"], L * per["out_log"] + t + 1)
                    A(area_a[:, t, :], area_a[:, t, :], ACT.Exp, scale=-0.5).then_inc(s["out_rstd"], 1)
                for t in range(8):
                    act.wait_ge(s["out_gated"], L * per["out_gated"] + t + 1)
                    A(h_hi[:, t, :], oT[:, t, :], ACT.Copy).then_inc(s["mix_hi_ready"], 1)

                with act.Fori(0, OUT_UNITS // 2) as i:
                    for u in range(2):
                        act.wait_ge(s["unit_used"], L * per["unit_used"] + OUT0 + 2 * i + u + 1)
                        split_hi(q0 + OUT0 // 2 + i + 1, u)

                norm(L, 1)
                norm_hi(L, 1)

                nc.scalar.preload_act_table_set("silu_and_others")
                with act.Fori(0, FT) as i:
                    for u, dst in ((0, cg), (1, cv)):
                        act.wait_ge(s["unit_used"], L * per["unit_used"] + UP0 + 2 * i + u + 1)
                        split_hi(q0 + UP0 // 2 + i + 1, u)
                        A(dst[:, :], bank[u][:, :], ACT.Identity,
                          scale=param("ffn_conv", (2 * i + u) * 3 + 2),
                          bias=param("ffn_bias", 2 * i + u)).then_inc(s["ffn_last_tap"], 1)
                        if u == 0:
                            act.wait_ge(s["ffn_conv_done"], L * per["ffn_conv_done"] + 2 * i + 1)
                            A(cg[:, :], cg[:, :], ACT.Silu).then_inc(s["ffn_silu"], 1)
                    act.wait_ge(s["ffn_product"], L * per["ffn_product"] + i + 1)
                    A(g_hi[:, bass.ds(i, 1), :], gt[:, :].unsqueeze(1), ACT.Copy).then_inc(s["g_hi_ready"], 1)

                with act.Fori(0, DOWN_UNITS // 2 - 1) as i:
                    for u in range(2):
                        act.wait_ge(s["unit_used"], L * per["unit_used"] + DOWN0 + 2 * i + u + 1)
                        split_hi(q0 + DOWN0 // 2 + i + 1, u)
            norm(DEPTH, 0)

        @block.vector
        def _(dve):
            tt, ts, stt = nc.vector.tensor_tensor, nc.vector.tensor_scalar, nc.vector.scalar_tensor_tensor

            def split_lo(L, k, u):
                dve.wait_ge(s["hi_ready"], L * per["hi_ready"] + k + 1)
                tt(w_lo[:, u, :], raw[:, u, :], w_hi[:, u, :].bitcast(F32),
                   ALU.subtract).then_inc(s["lo_ready"], 1)

            def norm(L, which, weight):
                dve.wait_ge(s["rstd_ready"], L * per["rstd_ready"] + which + 1)
                for k in range(KT):
                    stt(gqkv[:, k, :], x[:, k, :], weight(k), rstd[:, :], ALU.mult,
                        ALU.mult).then_inc(s["x_normed"], 1)

            steps = [0]
            dve.wait_ge(setup_loaded, 48)

            def once(ins):
                ins.then_inc(setup_dve, 1)
                steps[0] += 1
                dve.wait_ge(setup_dve, steps[0])

            l0, l1 = lb[:, 0, 0:2], lb[:, 1, 0:2]
            once(tt(lbw[:, 4:6], l0, l1, ALU.max))
            once(tt(lbw[:, 0:4].rearrange("p (l t) -> p l t", l=DEPTH), lb[:, :, 0:2],
                    lbw[:, 4:6].unsqueeze(1).broadcast_to([P, DEPTH, 2]), ALU.subtract))
            dve.wait_ge(setup_act, 1)
            once(tt(lbw[:, 4:6], lbw[:, 0:2], lbw[:, 2:4], ALU.add))
            once(nc.vector.reciprocal(lbw[:, 6:8], lbw[:, 4:6]))
            once(tt(lbw[:, 0:4].rearrange("p (l t) -> p l t", l=DEPTH),
                    lbw[:, 0:4].rearrange("p (l t) -> p l t", l=DEPTH),
                    lbw[:, 6:8].unsqueeze(1).broadcast_to([P, DEPTH, 2]), ALU.mult))
            once(tt(lbw[:, 2:4], lbw[:, 0:2], lbw[:, 2:4], ALU.add))
            for layer in range(DEPTH):
                once(tt(lb[:, layer, 0:2], lbw[:, 2 * layer:2 * layer + 2], lbw[:, 0:2], ALU.subtract))
            once(ts(lb[:, :, 0:2], lb[:, :, 0:2], 0.0, None, ALU.max))
            once(ts(lb[:, :, 2:4], lb[:, :, 0:2], -1.0, 1.0, ALU.mult, ALU.add))
            posf, ang, turns, n_turns = (slot[1 + i][:, 0:SEQ] for i in range(4))
            magic = 12582912.0
            two_pi = [6.28125, float(np.float32(2 * np.pi - 6.28125))]
            two_pi.append(float(2 * np.pi - two_pi[0] - two_pi[1]))
            once(nc.vector.tensor_copy(posf, slot[0][:, 0:SEQ].bitcast(I32)))
            once(ts(ang, posf, const("inv_freq"), None, ALU.mult))
            for dst, quarter in ((sin_t, 0.0), (cos_t, 0.25)):
                once(ts(turns, ang, float(1 / (2 * np.pi)), quarter, ALU.mult, ALU.add))
                once(ts(n_turns, turns, magic, -magic, ALU.add, ALU.add))
                once(stt(turns, n_turns, -two_pi[0], ang, ALU.mult, ALU.add))
                once(stt(turns, n_turns, -two_pi[1], turns, ALU.mult, ALU.add))
                once(stt(turns, n_turns, -two_pi[2], turns, ALU.mult, ALU.add))
                once(ts(turns, turns, float(2 * np.pi * quarter), 3.1415925, ALU.add, ALU.min))
                once(ts(dst[:, :], turns, -3.1415925, None, ALU.max))
            assert steps[0] == SETUP_ANGLES
            dve.wait_ge(setup_act, 3)
            dve.wait_ge(x_loaded, 16 * KT)
            dve.sem_inc(s["x_after_ffn"], KT)
            dve.wait_ge(loaded, 48)

            with dve.Fori(0, DEPTH) as L:
                nc.vector.tensor_copy(lb_cur[:, :].unsqueeze(1), lb[:, bass.ds(L, 1), :])
                nc.vector.tensor_copy(cur[:, :].unsqueeze(1), par[:, bass.ds(L, 1), :]).then_inc(s["params_copied"], 1)
                dve.wait_ge(s["params_copied"], L * per["params_copied"] + 1)
                norm(L, 0, lambda k: param("norm1", k))
                for u in range(2):
                    split_lo(L, u, u)
                dve.wait_ge(s["wab_hi_ready"], L * per["wab_hi_ready"] + 1)
                tt(wab_lo[:, :, :], param("w_ab", 0, KT * 8).rearrange("p (k n) -> p k n", k=KT),
                   wab_hi[:, :, :].bitcast(F32), ALU.subtract).then_inc(s["wab_lo_ready"], 1)

                dve.wait_ge(s["ab_projected"], L * per["ab_projected"] + 1)
                gd = s["gate_dve_step"]
                nc.vector.tensor_copy(ab_rows, bank[6][0:8, :]).then_inc(s["ab_copied"], 1)
                split_lo(L, 2, 0)
                split_lo(L, 3, 1)
                dve.wait_ge(s["ab_turned"], L * per["ab_turned"] + 1)
                nc.vector.tensor_copy(abc[:, :, :], bank[7][:, 0:32].rearrange("p (c n) -> p c n", c=NC)).then_inc(gd, 1)
                dve.wait_ge(s["gate_dve_step"], L * per["gate_dve_step"] + 1)
                tt(hc(za), abc[:, :, 0:4].rearrange("p c h -> p h c"),
                   param("dt_bias", 0, 4).unsqueeze(2).broadcast_to([P, HEADS, NC]), ALU.add).then_inc(gd, 1)
                ts(hc(nb), abc[:, :, 4:8].rearrange("p c h -> p h c"), -1.0, 80.0, ALU.mult, ALU.min).then_inc(gd, 1)
                dve.wait_ge(s["gate_act_step"], L * per["gate_act_step"] + 3)
                stt(sp, za, 0.0, sp, ALU.max, ALU.add).then_inc(gd, 1)
                dve.wait_ge(s["gate_act_step"], L * per["gate_act_step"] + 4)
                dve.wait_ge(s["gate_dve_step"], L * per["gate_dve_step"] + 4)
                stt(hc(g_tok), hc(sp), -1.0, e_a[:, 0:4].unsqueeze(2).broadcast_to([P, HEADS, NC]),
                    ALU.mult, ALU.mult).then_inc(gd, 1)
                dve.wait_ge(s["gate_act_step"], L * per["gate_act_step"] + 5)
                ts(nb, nb, 1.0, None, ALU.add).then_inc(gd, 1)
                dve.wait_ge(s["gate_dve_step"], L * per["gate_dve_step"] + 6)
                nc.vector.reciprocal(beta, nb).then_inc(gd, 1)
                split_lo(L, 4, 0)
                dve.wait_ge(s["b_token_major"], L * per["b_token_major"] + 1)
                nc.vector.tensor_copy(btok, bank[6][:, 64:80]).then_inc(gd, 1)
                dve.wait_ge(s["gate_dve_step"], L * per["gate_dve_step"] + 8)
                for h in range(HEADS):
                    dve.wait_ge(s["b_spread"], L * per["b_spread"] + h + 1)
                    nc.vector.tensor_copy(hc(bl)[:, h, :], chunks(bank[2 + h][:, :])[:, :, C - 1]).then_inc(gd, 1)
                    for c in range(NC):
                        ins = ts(decay[:, h, c * C:(c + 1) * C], bank[2 + h][:, c * C:(c + 1) * C],
                                 btok[:, h * NC + c:h * NC + c + 1], 0.0, ALU.subtract, ALU.min)
                    ins.then_inc(s["b_diff_ready"], 1)
                    if h == 1:
                        split_lo(L, 5, 1)
                dve.wait_ge(s["gate_dve_step"], L * per["gate_dve_step"] + 12)
                tt(dko, bl, btok, ALU.subtract).then_inc(gd, 1)
                dve.wait_ge(s["gate_act_step"], L * per["gate_act_step"] + 6)
                tt(be, beta, e_tok, ALU.mult).then_inc(gd, 1)

                with dve.Fori(2, COPY_UNITS // 2) as i:
                    for u in range(2):
                        split_lo(L, 2 * i + 2 + u, u)
                with dve.Fori(0, CONV_UNITS // 2) as i:
                    for u in range(2):
                        n = 2 * i + u
                        for tap in range(1, 4):
                            if tap == 1:
                                dve.wait_ge(s["conv_last_tap"], L * per["conv_last_tap"] + n + 1)
                            else:
                                dve.wait_ge(s["conv_mid_taps"], L * per["conv_mid_taps"] + 2 * n + tap - 1)
                            o = gqkv[:, bass.ds(n, 1), tap:SEQ]
                            stt(o, bank[u][:, 0:SEQ - tap].unsqueeze(1), param("gdn_conv", n * 4 + 3 - tap), o,
                                ALU.mult, ALU.add).then_inc(s["conv_mid_taps"] if tap < 3 else s["conv_done"], 1)
                        split_lo(L, CONV0 + n + 2, u)
                with dve.Fori(0, GATE_UNITS // 2) as i:
                    for u in range(2):
                        split_lo(L, GATE0 + 2 * i + 2 + u, u)

                dve.wait_ge(s["gate_dve_step"], L * per["gate_dve_step"] + 14)
                for h in range(HEADS):
                    dve.wait_ge(s["kv_turned"], L * per["kv_turned"] + h + 1)
                    tt(chunks(v_b[:, h, :]), chunks(bank[6 + h % 2][:, :]), per_token(hc(beta)[:, h, :]),
                       ALU.mult).then_inc(s["kv_turned_read"], 1)
                for t in range(8):
                    dve.wait_ge(s["l2_rnorm"], L * per["l2_rnorm"] + t + 1)
                    stt(gqkv[:, t, :], gqkv[:, t, :], float(P) ** -0.5 if t < 4 else 1.0, area_a[:, t, :],
                        ALU.mult, ALU.mult).then_inc(s["qk_normed"], 1)
                dve.wait_ge(s["qk_normed"], L * per["qk_normed"] + 8)
                dve.wait_ge(s["gate_act_step"], L * per["gate_act_step"] + 8)
                for h in range(HEADS):
                    dve.wait_ge(s["kv_turned"], L * per["kv_turned"] + 4 + h + 1)
                    tt(chunks(k_out[:, h, :]), chunks(bank[6 + h % 2][:, :]), per_token(hc(ko)[:, h, :]),
                       ALU.mult).then_inc(s["k_out_ready"], 1)
                    tt(chunks(k_be[:, h, :]), chunks(bank[6 + h % 2][:, :]), per_token(hc(be)[:, h, :]),
                       ALU.mult).then_inc(s["kv_turned_read"], 1)
                dve.wait_ge(s["decay_masked"], L * per["decay_masked"] + 4)
                for h in range(HEADS):
                    e = h % 2
                    dve.wait_ge(s["kk_qk_products"], L * per["kk_qk_products"] + h + 1)
                    tt(attn[:, h, :], bank[2 + e][:, :], decay[:, h, :], ALU.mult)
                    tt(G[:, h, :], bank[e][:, :], decay[:, h, :], ALU.mult).then_inc(s["kk_decayed"], 1)
                    dve.wait_ge(s["kk_decayed"], L * per["kk_decayed"] + h + 1)
                    tt(G[:, h, :], bank[4 + e][:, :], G[:, h, :], ALU.mult).then_inc(s["g_attn_ready"], 1)
                for k in range(24):
                    dve.wait_ge(s["tgt_product"], L * per["tgt_product"] + k + 1)
                    if k < 4:
                        dve.wait_ge(s["inv_t_first"], L * per["inv_t_first"] + k + 1)
                    else:
                        dve.wait_ge(s["inv_t_updated"], L * per["inv_t_updated"] + k - 3)
                    tt(T[:, k % 4, :], T[:, k % 4, :], bank[2 + k % 2][:, :], ALU.subtract).then_inc(s["inv_t_updated"], 1)
                for c in range(NC - 1):
                    dve.wait_ge(s["state_sum"], L * per["state_sum"] + c + 1)
                    if c == 0:
                        nc.vector.tensor_copy(S_ring[:, 0, :], bank[6][:, :]).then_inc(s["state_ready"], 1)
                        continue
                    dve.wait_ge(s["state_ready"], L * per["state_ready"] + c)
                    if c >= 2:
                        dve.wait_ge(s["delta_out"], L * per["delta_out"] + c)
                    for h in range(HEADS):
                        o = slice(h * P, (h + 1) * P)
                        ins = stt(S_ring[:, c % 2, o], S_ring[:, (c - 1) % 2, o], w_dec[:, h * NC + c:h * NC + c + 1],
                                  bank[6 + c % 2][:, o], ALU.mult, ALU.add)
                    ins.then_inc(s["state_ready"], 1)

                def states(w_of, summed, per_sum, done, per_done):
                    for t in range(2):
                        dve.wait_ge(summed, L * per_sum + t + 1)
                        st = SU[:, t, 0:3 * P].rearrange("p (c n) -> p c n", c=3)
                        tt(st, bank[4 + t][:, 0:3 * P].rearrange("p (c n) -> p c n", c=3),
                           const("blocks").unsqueeze(1).broadcast_to([P, 3, P]), ALU.mult).then_inc(done, 1)
                        for c in range(1, 3):
                            dve.wait_ge(done, L * per_done + 3 * t + c)
                            stt(st[:, c, :], st[:, c - 1, :], w_of(t, c), st[:, c, :], ALU.mult,
                                ALU.add).then_inc(done, 1)

                for t in range(4):
                    dve.wait_ge(s["rotated"], L * per["rotated"] + t + 1)
                    if t >= 2:
                        dve.wait_ge(s["rot_done"], L * per["rot_done"] + t - 1)
                    tt(scratch[:, t % 2, :], bank[t % 2][:, :], sin_t[:, :], ALU.mult).then_inc(s["rot_sin"], 1)
                    dve.wait_ge(s["rot_sin"], L * per["rot_sin"] + t + 1)
                    dve.wait_ge(s["rot_cos"], L * per["rot_cos"] + t + 1)
                    tt(cp[:, t, :], cp[:, t, :], scratch[:, t % 2, :], ALU.add).then_inc(s["rot_done"], 1)
                for t in range(2):
                    dve.wait_ge(s["ret_turned"], L * per["ret_turned"] + t + 1)
                    tt(chunks(k_tok[:, t, :]), chunks(bank[4 + t][:, :]), per_chunk(const("ret_k", t, P)),
                       ALU.mult).then_inc(s["ret_k_out"], 1)
                for h in range(HEADS):
                    dve.wait_ge(s["ret_scores"], L * per["ret_scores"] + h + 1)
                    tt(chunks(PT[:, h, :]), chunks(bank[2 + h % 2][:, :]), per_chunk(const("ret_decay", h, C)),
                       ALU.mult).then_inc(s["ret_decayed"], 1)
                states(lambda t, c: const("ret_w", t, 1), s["ret_sums"], per["ret_sums"], s["ret_states"], per["ret_states"])

                hd = s["hg_dve_step"]
                dve.wait_ge(s["ret_out"], L * per["ret_out"] + 2)
                ts(slot[0], hz, -1.0, 40.0, ALU.mult, ALU.min).then_inc(hd, 1)
                ts(slot[1], hz, -1.0, -40.0, ALU.mult, ALU.add).then_inc(hd, 1)
                dve.wait_ge(s["hg_dve_step"], L * per["hg_dve_step"] + 2)
                ts(slot[1], slot[1], 0.0, 40.0, ALU.max, ALU.min).then_inc(hd, 1)
                dve.wait_ge(s["hg_act_step"], L * per["hg_act_step"] + 3)
                for t in range(2):
                    o = slice(t * SEQ, (t + 1) * SEQ)
                    ins = stt(slot[3][:, o], slot[0][:, o], lb_cur[:, t:t + 1], slot[3][:, o], ALU.mult, ALU.add)
                ins.then_inc(hd, 1)
                tt(slot[4], hz, slot[2], ALU.add).then_inc(hd, 1)
                dve.wait_ge(s["hg_dve_step"], L * per["hg_dve_step"] + 5)
                ts(slot[4], slot[4], -1.0, 0.0, ALU.mult, ALU.min).then_inc(hd, 1)
                ts(slot[5], hz, 40.0, 0.0, ALU.add, ALU.min).then_inc(hd, 1)
                dve.wait_ge(s["hg_dve_step"], L * per["hg_dve_step"] + 7)
                tt(slot[5], slot[5], slot[2], ALU.subtract).then_inc(hd, 1)
                dve.wait_ge(s["hg_dve_step"], L * per["hg_dve_step"] + 8)
                tt(slot[5], slot[5], slot[1], ALU.add).then_inc(hd, 1)
                dve.wait_ge(s["hg_dve_step"], L * per["hg_dve_step"] + 9)
                dve.wait_ge(s["hg_act_step"], L * per["hg_act_step"] + 4)
                tt(slot[5], slot[5], slot[3], ALU.add).then_inc(hd, 1)
                dve.wait_ge(s["hg_act_step"], L * per["hg_act_step"] + 5)
                for t in range(2):
                    o = slice(t * SEQ, (t + 1) * SEQ)
                    ins = ts(slot[4][:, o], slot[4][:, o], lb_cur[:, 2 + t:3 + t], None, ALU.mult)
                ins.then_inc(hd, 1)
                dve.wait_ge(s["hg_dve_step"], L * per["hg_dve_step"] + 10)
                for c in range(2 * NC):
                    o = slice(c * C, (c + 1) * C)
                    ins = nc.vector.tensor_tensor_scan(slot[0][:, o], const("ones"), slot[5][:, o], 0.0,
                                                       ALU.mult, ALU.add)
                ins.then_inc(hd, 1)
                dve.wait_ge(s["hg_dve_step"], L * per["hg_dve_step"] + 12)
                bc = slot[0].rearrange("p (c i) -> p c i", i=C)
                nc.vector.tensor_copy(hbl[:, 0:8].unsqueeze(2), bc[:, :, C - 1:C])
                tt(slot[1].rearrange("p (c i) -> p c i", i=C), bc[:, :, C - 1:C].broadcast_to([P, 2 * NC, C]), bc,
                   ALU.subtract).then_inc(hd, 1)
                dve.wait_ge(s["hg_act_step"], L * per["hg_act_step"] + 6)
                tt(slot[1], slot[1], slot[4], ALU.mult).then_inc(hd, 1)
                nc.vector.memset(PT[:, :, :], 0.0).then_inc(hd, 1)
                dve.wait_ge(s["hg_dve_step"], L * per["hg_dve_step"] + 15)

                def scores_of(n):
                    mask = const("lvl", n, C) if n < len(LEVELS) else ident
                    for h in range(HEADS):
                        dve.wait_ge(s["hg_scores"], L * per["hg_scores"] + 4 * n + h + 1)
                        if n:
                            dve.wait_ge(s["hg_scores_placed"], L * per["hg_scores_placed"] + 4 * (n - 1) + h + 1)
                        apart(dve)
                        nc.vector.copy_predicated(chunks(PT[:, h, :]), per_chunk(mask.bitcast(I32)),
                                                  chunks(bank[h][:, :])).then_inc(s["hg_scores_placed"], 1)

                for n, half in enumerate(LEVELS):
                    X, k3, q3 = (a.rearrange("p (g s) -> p g s", s=2 * half) for a in
                                 (slot[3 + 2 * (n % 2)], slot[4], hq))
                    dve.wait_ge(s["level_exp"], L * per["level_exp"] + n + 1)
                    tt(X[:, :, 0:half], X[:, :, 0:half], k3[:, :, 0:half], ALU.mult)
                    tt(X[:, :, half:], X[:, :, half:], q3[:, :, half:], ALU.mult).then_inc(s["level_qk"], 1)
                    if n:
                        scores_of(n - 1)
                scores_of(6)
                scores_of(7)
                states(lambda t, c: hw[:, t * NC + c:t * NC + c + 1], s["hg_sums"], per["hg_sums"], s["hg_states"], per["hg_states"])

                for t in range(8 + 1):
                    if t < 8:
                        dve.wait_ge(s["out_rstd"], L * per["out_rstd"] + t + 1)
                        stt(oT[:, t, :], oT[:, t, :], param("onorm", t), area_a[:, t, :], ALU.mult,
                            ALU.mult).then_inc(s["out_normed"], 1)
                        dve.wait_ge(s["out_normed"], L * per["out_normed"] + t + 1)
                        tt(oT[:, t, :], oT[:, t, :], gate[:, t, :], ALU.mult).then_inc(s["out_gated"], 1)
                    if t:
                        dve.wait_ge(s["mix_hi_ready"], L * per["mix_hi_ready"] + t)
                        tt(h_lo[:, t - 1, :], oT[:, t - 1, :], h_hi[:, t - 1, :].bitcast(F32),
                           ALU.subtract).then_inc(s["mix_lo_ready"], 1)

                with dve.Fori(0, OUT_UNITS // 2) as i:
                    for u in range(2):
                        split_lo(L, OUT0 + 2 + 2 * i + u, u)
                for m in range(KT):
                    if m < KT - 1:
                        dve.wait_ge(s["out_projected"], L * per["out_projected"] + m + 1)
                    else:
                        dve.wait_ge(s["unit_used"], L * per["unit_used"] + OUT0 + 8)
                    tt(x[:, m, :], x[:, m, :], bank[(m + 2) % 8][:, :], ALU.add).then_inc(s["x_after_mixer"], 1)
                dve.wait_ge(s["x_after_mixer"], L * per["x_after_mixer"] + 8)
                norm(L, 1, lambda k: param("norm2", k))

                with dve.Fori(0, FT) as i:
                    for u, dst in ((0, cg), (1, cv)):
                        split_lo(L, UP0 + 2 + 2 * i + u, u)
                        n = 2 * i + u
                        dve.wait_ge(s["ffn_last_tap"], L * per["ffn_last_tap"] + n + 1)
                        stt(dst[:, 1:SEQ], bank[u][:, 0:SEQ - 1], param("ffn_conv", n * 3 + 1), dst[:, 1:SEQ],
                            ALU.mult, ALU.add).then_inc(s["ffn_mid_tap"], 1)
                        dve.wait_ge(s["ffn_mid_tap"], L * per["ffn_mid_tap"] + n + 1)
                        stt(dst[:, 2:SEQ], bank[u][:, 0:SEQ - 2], param("ffn_conv", n * 3), dst[:, 2:SEQ],
                            ALU.mult, ALU.add).then_inc(s["ffn_conv_done"], 1)
                    dve.wait_ge(s["ffn_conv_done"], L * per["ffn_conv_done"] + 2 * i + 2)
                    dve.wait_ge(s["ffn_silu"], L * per["ffn_silu"] + i + 1)
                    tt(gt[:, :], cg[:, :], cv[:, :], ALU.mult).then_inc(s["ffn_product"], 1)
                    dve.wait_ge(s["g_hi_ready"], L * per["g_hi_ready"] + i + 1)
                    tt(g_lo[:, bass.ds(i, 1), :], gt[:, :].unsqueeze(1), g_hi[:, bass.ds(i, 1), :].bitcast(F32),
                       ALU.subtract).then_inc(s["g_lo_ready"], 1)

                with dve.Fori(0, DOWN_UNITS // 2 - 1) as i:
                    for u in range(2):
                        split_lo(L, DOWN0 + 2 + 2 * i + u, u)
                for m in range(KT):
                    if m < KT - 1:
                        dve.wait_ge(s["down_projected"], L * per["down_projected"] + m + 1)
                    else:
                        dve.wait_ge(s["unit_used"], L * per["unit_used"] + UNITS)
                    tt(x[:, m, :], x[:, m, :], bank[(m + 2) % 8][:, :], ALU.add).then_inc(s["x_after_ffn"], 1)
                dve.wait_ge(s["x_after_ffn"], 8 * L + 16)

            norm(DEPTH, 0, lambda k: fin[:, k:k + 1])

        @block.tensor
        def _(pe):
            mm = nc.tensor.matmul

            def norm(L, which):
                for k in range(KT):
                    pe.wait_ge(s["x_squared"], L * per["x_squared"] + 8 * which + k + 1)
                    ins = mm(bank[2][:, :], const("mean_model"), gqkv[:, k, :], start=k == 0, stop=k == KT - 1)
                ins.then_inc(s["x_mean_square"], 1)

            def three(dst, hi, lo, b_hi, b_lo, start, stop):
                mm(dst, hi, b_hi, start=start, stop=False)
                mm(dst, hi, b_lo, start=False, stop=False)
                return mm(dst, lo, b_hi, start=False, stop=stop)

            def unit(L, k, u, normed_before=None):
                pe.wait_ge(s["lo_ready"], L * per["lo_ready"] + k + 1)
                for kt in range(KT):
                    if normed_before is not None:
                        pe.wait_ge(s["h_lo_ready"], L * per["h_lo_ready"] + normed_before + kt + 1)
                    o = slice(kt * P, (kt + 1) * P)
                    ins = three(bank[u][:, :], w_hi[:, u, o], w_lo[:, u, o], h_hi[:, kt, :], h_lo[:, kt, :],
                                kt == 0, kt == KT - 1)
                ins.then_inc(s["unit_used"], 1)
                return ins

            def rows(L, k, u, b_hi, b_lo, start, stop, last=None, over_up=False):
                pe.wait_ge(s["lo_ready"], L * per["lo_ready"] + k + 1)
                for m in range(KT):
                    if over_up and m >= KT - 2:
                        pe.wait_ge(s["ffn_conv_done"], L * per["ffn_conv_done"] + UP_UNITS - (KT - 1 - m))
                    o = slice(m * P, (m + 1) * P)
                    ins = three(bank[(m + 2) % 8][:, :], w_hi[:, u, o], w_lo[:, u, o], b_hi, b_lo, start, stop)
                    if last and m < KT - 1:
                        ins.then_inc(last, 1)
                ins.then_inc(s["unit_used"], 1)

            pe.wait_ge(loaded, 48)
            with pe.Fori(0, DEPTH) as L:
                norm(L, 0)
                unit(L, 0, 0, normed_before=0)
                pe.wait_ge(s["wab_lo_ready"], L * per["wab_lo_ready"] + 1)
                for kt in range(KT):
                    ins = three(bank[6][0:8, :], wab_hi[:, kt, :], wab_lo[:, kt, :], h_hi[:, kt, :], h_lo[:, kt, :],
                                kt == 0, kt == KT - 1)
                ins.then_inc(s["ab_projected"], 1)
                unit(L, 1, 1)
                pe.wait_ge(s["ab_copied"], L * per["ab_copied"] + 1)
                apart(pe)
                for c in range(NC):
                    ins = nc.tensor.transpose(bank[7][:, c * 8:c * 8 + 8], ab_rows[:, c * C:(c + 1) * C], ident[0:8, 0:8])
                ins.then_inc(s["ab_turned"], 1)
                pe.wait_ge(s["bank_copied"], L * per["bank_copied"] + 1)
                unit(L, 2, 0)
                pe.wait_ge(s["gate_dve_step"], L * per["gate_dve_step"] + 5)
                mm(bank[6][:, 64:80], causal, g_tok, start=True, stop=True).then_inc(s["b_token_major"], 1)
                for h in range(HEADS):
                    for c in range(NC):
                        ins = mm(bank[2 + h][:, c * C:(c + 1) * C],
                                 g_tok[:, h * NC + c:h * NC + c + 1].broadcast_to([P, C]), causal,
                                 start=True, stop=True)
                    ins.then_inc(s["b_spread"], 1)
                pe.wait_ge(s["bank_copied"], L * per["bank_copied"] + 2)
                unit(L, 3, 1)
                with pe.Fori(2, COPY_UNITS // 2) as i:
                    for u in range(2):
                        pe.wait_ge(s["bank_copied"], L * per["bank_copied"] + 2 * i + u - 1)
                        unit(L, 2 * i + u, u)
                for u in range(2):
                    pe.wait_ge(s["bank_copied"], L * per["bank_copied"] + COPY_UNITS - 1 + u)
                    unit(L, CONV0 + u, u)
                with pe.Fori(1, CONV_UNITS // 2) as i:
                    for u in range(2):
                        pe.wait_ge(s["conv_done"], L * per["conv_done"] + 2 * i + u - 1)
                        unit(L, CONV0 + 2 * i + u, u)
                for u in range(2):
                    pe.wait_ge(s["conv_done"], L * per["conv_done"] + CONV_UNITS - 1 + u)
                    unit(L, GATE0 + u, u)
                with pe.Fori(1, GATE_UNITS // 2) as i:
                    for u in range(2):
                        pe.wait_ge(s["bank_copied"], L * per["bank_copied"] + COPY_UNITS + 2 * i + u - 1)
                        unit(L, GATE0 + 2 * i + u, u)

                def turn(dst, src):
                    for c in range(NC):
                        o = slice(c * C, (c + 1) * C)
                        ins = nc.tensor.transpose(dst[:, o], src[:, o], ident)
                    return ins

                pe.wait_ge(s["qkv_silu"], L * per["qkv_silu"] + 12)
                pe.wait_ge(s["gate_dve_step"], L * per["gate_dve_step"] + 8)
                for h in range(HEADS):
                    if h >= 2:
                        pe.wait_ge(s["kv_turned_read"], L * per["kv_turned_read"] + h - 1)
                    turn(bank[6 + h % 2], gqkv[:, 8 + h, :]).then_inc(s["kv_turned"], 1)
                pe.wait_ge(s["bank_copied"], L * per["bank_copied"] + GATE_UNITS + COPY_UNITS)
                for t in range(8):
                    pe.wait_ge(s["l2_squared"], L * per["l2_squared"] + t + 1)
                    if t >= 2:
                        pe.wait_ge(s["l2_log"], L * per["l2_log"] + t - 1)
                    mm(bank[t % 2][:, :], const("ones"), area_a[:, t, :], start=True,
                       stop=True).then_inc(s["l2_summed"], 1)
                for h in range(HEADS):
                    pe.wait_ge(s["qk_normed"], L * per["qk_normed"] + 4 + h + 1)
                    pe.wait_ge(s["kv_turned_read"], L * per["kv_turned_read"] + 4 + h - 1)
                    turn(bank[6 + h % 2], gqkv[:, 4 + h, :]).then_inc(s["kv_turned"], 1)
                pe.wait_ge(s["l2_log"], L * per["l2_log"] + 8)
                pe.wait_ge(s["exp_b_ready"], L * per["exp_b_ready"] + 4)
                pe.wait_ge(s["gate_dve_step"], L * per["gate_dve_step"] + 12)
                for h in range(HEADS):
                    e = h % 2
                    if h >= 2:
                        pe.wait_ge(s["g_attn_ready"], L * per["g_attn_ready"] + h - 1)
                    for c in range(NC):
                        o = slice(c * C, (c + 1) * C)
                        mm(bank[2 + e][:, o], gqkv[:, 4 + h, o], gqkv[:, h, o], start=True, stop=True)
                        mm(bank[e][:, o], gqkv[:, 4 + h, o], gqkv[:, 4 + h, o], start=True, stop=True)
                        ins = mm(bank[4 + e][:, o], beta[:, h * NC + c:h * NC + c + 1].broadcast_to([P, C]), ident,
                                 start=True, stop=True)
                    ins.then_inc(s["kk_qk_products"], 1)
                pe.wait_ge(s["g_attn_ready"], L * per["g_attn_ready"] + 4)
                for h in range(HEADS):
                    pe.wait_ge(s["inv_first"], L * per["inv_first"] + h + 1)
                    if h >= 2:
                        pe.wait_ge(s["inv_t_first"], L * per["inv_t_first"] + h - 1)
                    turn(bank[4 + h % 2], R[:, h, :]).then_inc(s["inv_first_turned"], 1)

                def join_p(k):
                    h = k % 4
                    pe.wait_ge(s["g_level"], L * per["g_level"] + k + 1)
                    if k < 4:
                        pe.wait_ge(s["inv_t_first"], L * per["inv_t_first"] + h + 1)
                    else:
                        pe.wait_ge(s["inv_t_updated"], L * per["inv_t_updated"] + k - 3)
                    if k >= 2:
                        pe.wait_ge(s["gt_copied"], L * per["gt_copied"] + k - 1)
                    for c in range(NC):
                        o = slice(c * C, (c + 1) * C)
                        ins = mm(bank[k % 2][:, o], ml_ring[:, k % 2, o], T[:, h, o], start=True, stop=True)
                    ins.then_inc(s["gt_product"], 1)

                def join_tp(k):
                    h = k % 4
                    pe.wait_ge(s["gt_copied"], L * per["gt_copied"] + k + 1)
                    if k >= 4:
                        pe.wait_ge(s["inv_r_updated"], L * per["inv_r_updated"] + k - 3)
                    if k >= 2:
                        pe.wait_ge(s["inv_t_updated"], L * per["inv_t_updated"] + k - 1)
                    for c in range(NC):
                        o = slice(c * C, (c + 1) * C)
                        ins = mm(bank[2 + k % 2][:, o], R[:, h, o], p_ring[:, k % 2, o], start=True, stop=True)
                    ins.then_inc(s["tgt_product"], 1)

                def join_x(k):
                    pe.wait_ge(s["inv_t_updated"], L * per["inv_t_updated"] + k + 1)
                    if k >= 2:
                        pe.wait_ge(s["inv_r_updated"], L * per["inv_r_updated"] + k - 1)
                    else:
                        pe.wait_ge(s["inv_t_first"], L * per["inv_t_first"] + 4)
                    turn(bank[4 + k % 2], T[:, k % 4, :]).then_inc(s["inv_turned"], 1)

                for k in range(24 + 2):
                    if k < 24:
                        join_p(k)
                    if 1 <= k < 25:
                        join_tp(k - 1)
                    if k >= 2:
                        join_x(k - 2)
                pe.wait_ge(s["kv_turned_read"], L * per["kv_turned_read"] + 8)
                for h in range(HEADS):
                    pe.wait_ge(s["inv_r_updated"], L * per["inv_r_updated"] + 20 + h + 1)
                    if h >= 2:
                        pe.wait_ge(s["kcd_ready"], L * per["kcd_ready"] + h - 1)
                    for c in range(NC):
                        o = slice(c * C, (c + 1) * C)
                        ins = mm(bank[6 + h % 2][:, o], k_be[:, h, o], R[:, h, o], start=True, stop=True)
                    ins.then_inc(s["kcd_product"], 1)
                pe.wait_ge(s["gt_copied"], L * per["gt_copied"] + 24)
                pe.wait_ge(s["kcd_ready"], L * per["kcd_ready"] + 4)
                pe.wait_ge(s["inv_t_updated"], L * per["inv_t_updated"] + 24)
                pe.wait_ge(s["q_in_ready"], L * per["q_in_ready"] + 4)
                for c in range(NC):
                    o = slice(c * C, (c + 1) * C)
                    before = S_ring[:, (c - 1) % 2, :]
                    if c:
                        pe.wait_ge(s["state_ready"], L * per["state_ready"] + c)
                    if c >= 2:
                        pe.wait_ge(s["v_new_ready"], L * per["v_new_ready"] + c - 1)
                    for h in range(HEADS):
                        ho = slice(h * P, (h + 1) * P)
                        ins = mm(bank[c % 2][:, ho], R[:, h, o], v_b[:, h, o], start=True, stop=c == 0)
                        if c:
                            ins = mm(bank[c % 2][:, ho], kcd[:, h, o], before[:, ho], start=False, stop=True)
                    ins.then_inc(s["v_new_product"], 1)
                    pe.wait_ge(s["v_new_ready"], L * per["v_new_ready"] + c + 1)
                    if c < NC - 1:
                        if c >= 2:
                            pe.wait_ge(s["state_ready"], L * per["state_ready"] + c - 1)
                        for h in range(HEADS):
                            ho = slice(h * P, (h + 1) * P)
                            ins = mm(bank[6 + c % 2][:, ho], k_out[:, h, o], vn_ring[:, c % 2, ho],
                                     start=True, stop=True)
                        ins.then_inc(s["state_sum"], 1)
                    for h in range(HEADS):
                        ho = slice(h * P, (h + 1) * P)
                        if c:
                            mm(bank[2 + h][:, o], before[:, ho], gqkv[:, h, o], start=True, stop=False)
                        ins = mm(bank[2 + h][:, o], vn_ring[:, c % 2, ho], attn[:, h, o], start=c == 0, stop=True)
                    ins.then_inc(s["delta_out"], 1)

                def sums(done):
                    for t in range(2):
                        for c in range(NC - 1):
                            o = slice(c * C, (c + 1) * C)
                            ins = mm(bank[4 + t][:, c * P:(c + 1) * P], k_tok[:, t, o], v_tok[:, t, o],
                                     start=True, stop=True)
                        ins.then_inc(done, 1)

                def outputs(q_of, ready, per_ready, done):
                    for t in range(2):
                        pe.wait_ge(ready, L * per_ready + 3 * t + 3)
                        for c in range(NC):
                            o = slice(c * C, (c + 1) * C)
                            if c:
                                mm(bank[6 + t][:, o], SU[:, t, (c - 1) * P:c * P], q_of(t, o), start=True, stop=False,
                                   skip_group_check=True)
                            for e in range(2):
                                ins = mm(bank[6 + t][64 * e:64 * e + 64, o],
                                         v_tok[:, t, c * C + 64 * e:c * C + 64 * e + 64],
                                         PT[:, 2 * t + e, o], start=c == 0, stop=True, skip_group_check=True)
                        ins.then_inc(done, 1)

                pe.wait_ge(s["v_new_ready"], L * per["v_new_ready"] + 4)
                for t in range(4):
                    if t >= 2:
                        pe.wait_ge(s["rot_sin"], L * per["rot_sin"] + t - 1)
                    mm(bank[t % 2][:, :], const("rot"), cp[:, t, :], start=True, stop=True).then_inc(s["rotated"], 1)
                pe.wait_ge(s["state_ready"], L * per["state_ready"] + 3)
                pe.wait_ge(s["delta_out_copied"], L * per["delta_out_copied"] + 4)
                pe.wait_ge(s["rot_done"], L * per["rot_done"] + 4)
                for t in range(4):
                    turn(bank[4 + t], cp[:, 2 + t, :]).then_inc(s["ret_turned"], 1)
                for h in range(HEADS):
                    if h >= 2:
                        pe.wait_ge(s["ret_decayed"], L * per["ret_decayed"] + h - 1)
                    r = slice(64 * (h % 2), 64 * (h % 2) + 64)
                    for c in range(NC):
                        o = slice(c * C, (c + 1) * C)
                        ins = mm(bank[2 + h % 2][:, o], cp[r, 2 + h // 2, o], cp[r, h // 2, o], start=True, stop=True)
                    ins.then_inc(s["ret_scores"], 1)
                pe.wait_ge(s["ret_k_out"], L * per["ret_k_out"] + 2)
                pe.wait_ge(s["ret_v_copied"], L * per["ret_v_copied"] + 2)
                sums(s["ret_sums"])
                pe.wait_ge(s["ret_decayed"], L * per["ret_decayed"] + 4)
                pe.wait_ge(s["ret_q_in"], L * per["ret_q_in"] + 2)
                outputs(lambda t, o: cp[:, t, o], s["ret_states"], per["ret_states"], s["ret_out"])

                pe.wait_ge(s["hg_dve_step"], L * per["hg_dve_step"] + 15)
                pe.wait_ge(s["ret_states"], L * per["ret_states"] + 6)
                pe.wait_ge(s["ret_out_copied"], L * per["ret_out_copied"] + 2)
                for t in range(4):
                    turn(bank[4 + t], slot[1][:, t * SEQ:(t + 1) * SEQ] if t < 2 else
                         cp[:, 6 + t, :]).then_inc(s["hg_turned"], 1)
                pe.wait_ge(s["rot_sin"], L * per["rot_sin"] + 4)
                pe.wait_ge(s["ret_decayed"], L * per["ret_decayed"] + 4)
                for n in range(len(LEVELS) + 1):
                    if n < len(LEVELS):
                        pe.wait_ge(s["level_qk"], L * per["level_qk"] + n + 1)
                    X = slot[3 + 2 * (n % 2)]
                    for h in range(HEADS):
                        if n:
                            pe.wait_ge(s["hg_scores_placed"], L * per["hg_scores_placed"] + 4 * (n - 1) + h + 1)
                        r = slice(64 * (h % 2), 64 * (h % 2) + 64)
                        for c in range(NC):
                            a = (h // 2) * SEQ + c * C
                            lhs, rhs = (X, X) if n < len(LEVELS) else (slot[4], hq)
                            ins = mm(bank[h][:, c * C:(c + 1) * C], lhs[r, a:a + C], rhs[r, a:a + C],
                                     start=True, stop=True)
                        ins.then_inc(s["hg_scores"], 1)
                pe.wait_ge(s["hg_turned_copied"], L * per["hg_turned_copied"] + 4)
                sums(s["hg_sums"])
                pe.wait_ge(s["hg_scores_placed"], L * per["hg_scores_placed"] + 32)
                pe.wait_ge(s["hg_q_in"], L * per["hg_q_in"] + 1)
                outputs(lambda t, o: slot[2][:, t * SEQ + o.start:t * SEQ + o.stop], s["hg_states"], per["hg_states"], s["hg_out"])

                for t in range(8):
                    pe.wait_ge(s["out_squared"], L * per["out_squared"] + t + 1)
                    if t >= 2:
                        pe.wait_ge(s["out_log"], L * per["out_log"] + t - 1)
                    mm(bank[t % 2][:, :], const("mean64" if t < 4 else "mean128"), area_a[:, t, :], start=True,
                       stop=True).then_inc(s["out_mean_square"], 1)

                pe.wait_ge(s["out_log"], L * per["out_log"] + 8)
                for u in range(2):
                    pe.wait_ge(s["mix_lo_ready"], L * per["mix_lo_ready"] + u + 1)
                    rows(L, OUT0 + u, u, h_hi[:, u, :], h_lo[:, u, :], u == 0, False)
                pe.wait_ge(s["mix_lo_ready"], L * per["mix_lo_ready"] + 8)
                apart(pe)
                with pe.Fori(1, OUT_UNITS // 2 - 1) as i:
                    for u in range(2):
                        rows(L, OUT0 + 2 * i + u, u, h_hi[:, bass.ds(2 * i + u, 1), :],
                             h_lo[:, bass.ds(2 * i + u, 1), :], False, False)
                rows(L, OUT0 + 6, 0, h_hi[:, 6, :], h_lo[:, 6, :], False, False)
                rows(L, OUT0 + 7, 1, h_hi[:, 7, :], h_lo[:, 7, :], False, True, s["out_projected"])

                pe.wait_ge(s["x_after_mixer"], L * per["x_after_mixer"] + 8)
                norm(L, 1)

                unit(L, UP0, 0, normed_before=8)
                unit(L, UP0 + 1, 1)
                with pe.Fori(1, FT) as i:
                    for u in range(2):
                        pe.wait_ge(s["ffn_conv_done"], L * per["ffn_conv_done"] + 2 * i + u - 1)
                        unit(L, UP0 + 2 * i + u, u)

                pe.wait_ge(s["g_lo_ready"], L * per["g_lo_ready"] + 2)
                for u in range(2):
                    rows(L, DOWN0 + u, u, g_hi[:, u, :], g_lo[:, u, :], u == 0, False, over_up=u == 0)
                pe.wait_ge(s["g_lo_ready"], L * per["g_lo_ready"] + FT)
                apart(pe)
                with pe.Fori(1, DOWN_UNITS // 2 - 1) as i:
                    for u in range(2):
                        rows(L, DOWN0 + 2 * i + u, u, g_hi[:, bass.ds(2 * i + u, 1), :],
                             g_lo[:, bass.ds(2 * i + u, 1), :], False, False)
                rows(L, DOWN0 + 20, 0, g_hi[:, 20, :], g_lo[:, 20, :], False, False)
                rows(L, DOWN0 + 21, 1, g_hi[:, 21, :], g_lo[:, 21, :], False, True, s["down_projected"])
            norm(DEPTH, 0)


def constants():
    f8 = np.float64
    i = np.arange(C)
    col = np.zeros((P, N_CONST), np.float32)

    def put(name, a):
        at, n = CONSTS[name]
        col[:, at:at + n] = np.asarray(a, f8).reshape(P, n)

    put("ident", np.eye(C))
    put("mean_model", np.full((P, P), 1.0 / D_MODEL))
    put("ones", np.ones((P, P)))
    block = np.kron(np.eye(2), np.ones((64, 64)))
    put("blocks", block)
    put("mean64", block / 64)
    put("mean128", np.full((P, P), 1.0 / P))
    put("causal", i[:, None] <= i[None, :])
    put("lvl", np.stack([(j0 % 2 == 0) & (i0 == j0 + 1) for half in LEVELS
                         for j0, i0 in [(i[:, None] // half, i[None, :] // half)]], 1))
    log_gamma = np.log1p(-np.exp2(-5.0 - np.arange(HEADS)))
    rel = i[None, :] - i[:, None]
    scale = 64.0 ** -0.5
    put("ret_decay", np.stack([np.where(rel >= 0, np.exp(np.maximum(rel, 0) * lg), 0.0) * scale
                               for lg in log_gamma], 1))
    head = 2 * np.arange(2)[None, :] + (np.arange(P) // 64)[:, None]
    put("ret_q", np.exp((i + 1.0)[None, None, :] * log_gamma[head][:, :, None]))
    head_row = 2 * np.arange(2)[:, None] + (np.arange(P) // 64)[None, :]
    put("ret_k", np.exp((C - 1.0 - i)[:, None, None] * log_gamma[head_row][None]) * scale)
    put("ret_w", np.exp(C * log_gamma[head]))
    rot = np.zeros((P, P))
    for m in range(P):
        if m % 64 < 32:
            rot[m + 32, m] = -1.0
        else:
            rot[m - 32, m] = 1.0
    put("rot", rot)
    half = np.float32(32)
    inv = np.float32(10000.0) ** (-np.arange(32, dtype=np.float32) / half)
    put("inv_freq", np.tile(inv, 4)[:, None])
    return col


def kernel(**inputs):
    import concourse.bacc as bacc
    from concourse.bass_utils import run_bass_kernel_spmd

    a = {k: np.asarray(v) for k, v in inputs.items()}

    def tiles(v):
        return v.reshape(-1, P).T

    starts = ([P * j for j in range(6)] + [1280, 1408, 1536, 1664]
              + [2048 + P * j for j in range(12)]
              + [768, 896, 1792, 1920] + [3592 + P * j for j in range(4)] + [1024, 1152])
    ups = [o for j in range(FT) for o in (P * j, D_FF + P * j)]
    units, params = [], []
    for layer in range(DEPTH):
        w_in, w_up = a["w_in"][layer], a["w_up"][layer]
        for w, cols in ((w_in, starts), (w_up, ups)):
            blocks = [w[:, o:o + P].reshape(KT, P, P).transpose(1, 0, 2).reshape(P, KT * P) for o in cols]
            units += blocks
            if w is w_in:
                units += list(a["w_out"][layer].reshape(KT, P, D_MODEL))
        units += list(a["w_down"][layer].reshape(FT, P, D_MODEL))
        ab = w_in[:, 3584:3592].reshape(KT, P, 8).transpose(1, 0, 2).reshape(P, KT * 8)
        gconv = a["gdn_conv_w"][layer].T.reshape(12, P, 4).transpose(1, 0, 2).reshape(P, 48)
        fconv = a["ffn_conv_w"][layer].T.reshape(2, FT, P, 3).transpose(2, 1, 0, 3).reshape(P, -1)
        fbias = a["ffn_conv_b"][layer].reshape(2, FT, P).transpose(2, 1, 0).reshape(P, -1)
        ones = np.ones((P, 2), np.float32)
        hgn = np.tile(a["hg_norm_w"][layer], 2)[:, None]
        gdn = a["gdn_norm_w"][layer][:, None]
        wide = [np.broadcast_to(a[k][layer][None, :], (P, HEADS)) for k in ("gdn_A_log", "gdn_dt_bias")]
        params.append(np.concatenate([tiles(a["norm1_w"][layer]), tiles(a["norm2_w"][layer]), gconv, fconv, fbias,
                                      ones, hgn, hgn, gdn, gdn, gdn, gdn, *wide, ab], axis=1))
    arrays = {
        "x_t": a["x"][0].T.reshape(KT, P, SEQ).transpose(1, 0, 2),
        "positions": np.broadcast_to(a["positions"][0][None, :], (P, SEQ)),
        "constants": constants(),
        "params": np.stack(params, axis=1),
        "lb_logits": a["hg_lb_logits"].reshape(DEPTH, 2, P).transpose(2, 0, 1),
        "final_norm": tiles(a["final_norm_w"]),
        "weights": np.stack(units),
    }
    arrays = {k: np.ascontiguousarray(v) for k, v in arrays.items()}
    nc = bacc.Bacc("TRN2", target_bir_lowering=False, num_devices=1)
    args = [nc.dram_tensor(k, v.shape, mybir.dt.from_np(v.dtype), kind="ExternalInput").ap()
            for k, v in arrays.items()]
    args.append(nc.dram_tensor("out_t", (P, KT, SEQ), F32, kind="ExternalOutput").ap())
    build(nc, *args)
    r = run_bass_kernel_spmd(nc, [arrays], core_ids=[0])
    return r.results[0]["out_t"].transpose(2, 1, 0).reshape(1, SEQ, D_MODEL)
```

```python
from contextlib import ExitStack

import numpy as np

import concourse.bass as bass
from concourse import mybir

F32 = mybir.dt.float32
F32R = mybir.dt.float32r
I32 = mybir.dt.int32
ACT = mybir.ActivationFunctionType
ALU = mybir.AluOpType

P = 128
D_MODEL = 1024
SEQ = 512
DEPTH = 2
C = 128
NC = SEQ // C
KT = D_MODEL // P
HEADS = 4
D_FF = 2816
FT = D_FF // P
EPS = 1e-6

COPY_UNITS, CONV_UNITS, GATE_UNITS = 10, 12, 10
IN_UNITS = COPY_UNITS + CONV_UNITS + GATE_UNITS
OUT_UNITS = KT
UP_UNITS = 2 * FT
DOWN_UNITS = FT
UNITS = IN_UNITS + OUT_UNITS + UP_UNITS + DOWN_UNITS
CONV0, GATE0 = COPY_UNITS, COPY_UNITS + CONV_UNITS
OUT0, UP0, DOWN0 = IN_UNITS, IN_UNITS + OUT_UNITS, IN_UNITS + OUT_UNITS + UP_UNITS

LEVELS = [1, 2, 4, 8, 16, 32, 64]

JOINS = 4 * (len(LEVELS) - 1)
STEPS = JOINS + 2
GROUPS = HEADS * (len(LEVELS) + 1)
RING = 4


def groups_of(step):
    return range(GROUPS * step // STEPS, GROUPS * (step + 1) // STEPS)


FIRST_STEP = [k for n in range(len(LEVELS)) for k in range(STEPS) if HEADS * n in groups_of(k)]
LEVEL_AFTER = {FIRST_STEP[n - RING + 1]: n for n in range(RING, len(LEVELS))}

CONSTS = {}
_at = 0
for _name, _n in (("ident", C), ("mean_model", P), ("ones", P), ("mean64", P), ("mean128", P), ("causal", C),
                  ("lvl", len(LEVELS) * C), ("ret_decay", HEADS * C), ("ret_q", 2 * C), ("ret_k", 2 * P),
                  ("blocks", P), ("rot", P), ("ret_w", 2), ("inv_freq", 1)):
    CONSTS[_name] = (_at, _n)
    _at += _n
N_CONST = _at
PARAMS = {}
_at = 0
for _name, _n in (("norm1", KT), ("norm2", KT), ("gdn_conv", CONV_UNITS * 4), ("ffn_conv", UP_UNITS * 3),
                  ("ffn_bias", UP_UNITS), ("onorm", KT), ("a_log", HEADS), ("dt_bias", HEADS), ("w_ab", KT * 8)):
    PARAMS[_name] = (_at, _n)
    _at += _n
N_PARAM = _at

PER_LAYER = dict(
    x_after_mixer=8, x_after_ffn=8, x_squared=16, x_mean_square=2, rstd_log=2, rstd_ready=2, x_normed=16, h_hi_ready=16, h_lo_ready=16,
    params_copied=1, wab_hi_ready=1, wab_lo_ready=1, ab_projected=1, ab_copied=1, ab_turned=1, gate_dve_step=14, gate_act_step=8, b_token_major=1, b_spread=4, b_diff_ready=4, exp_b_ready=4, decay_exp=4, decay_masked=4,
    hi_ready=UNITS, lo_ready=UNITS, unit_used=UNITS,
    conv_last_tap=12, conv_mid_taps=24, conv_done=12, qkv_silu=12, bank_copied=20,
    kv_turned=8, kv_turned_read=8, k_out_ready=4, l2_squared=8, l2_summed=8, l2_log=8, l2_rnorm=8, qk_normed=8,
    kk_qk_products=4, kk_decayed=4, g_attn_ready=4, q_in_ready=4, g_smallest=4, inv_first=4, inv_first_turned=4, inv_t_first=4,
    g_level=24, gt_product=24, gt_copied=24, tgt_product=24, inv_t_updated=24, inv_turned=24, inv_r_updated=24, kcd_product=4, kcd_ready=4,
    v_new_product=4, v_new_ready=4, state_sum=3, delta_out=4, state_ready=3, delta_out_copied=4,
    rotated=4, rot_sin=4, rot_cos=4, rot_done=4, ret_scores=4, ret_decayed=4, ret_q_in=2, ret_turned=4, ret_k_out=2, ret_v_copied=2, ret_sums=2, ret_states=6, ret_out=2, ret_out_copied=2,
    hg_dve_step=14, hg_act_step=8, hg_scores_cleared=1, hg_q_in=1, level_diff=7, level_exp=7, level_qk=7, hg_scores=32, hg_scores_placed=32, hg_turned=4, hg_turned_copied=4, hg_sums=2, hg_states=6, hg_out=2, hg_out_copied=2,
    out_squared=8, out_mean_square=8, out_log=8, out_rstd=8, out_normed=8, out_gated=8, mix_hi_ready=8, mix_lo_ready=8,
    out_projected=7, ffn_last_tap=UP_UNITS, ffn_mid_tap=UP_UNITS, ffn_conv_done=UP_UNITS, ffn_silu=FT, ffn_product=FT, g_hi_ready=FT, g_lo_ready=FT, down_projected=7,
)


def build(nc, x_in, pos_in, const_in, par_in, lb_in, fin_in, w_in, out):
    ctx = ExitStack()
    with ctx:
        def sb(name, shape, dt=F32, where=ctx):
            return where.enter_context(nc.sbuf_tensor(name, shape, dt))

        s = {name: ctx.enter_context(nc.semaphore(name)) for name in PER_LAYER}
        per = PER_LAYER
        setup_loaded = ctx.enter_context(nc.semaphore("setup_loaded"))
        x_loaded = ctx.enter_context(nc.semaphore("x_loaded"))
        loaded = ctx.enter_context(nc.semaphore("loaded"))
        raw_loaded = [ctx.enter_context(nc.semaphore(f"raw_loaded{i}")) for i in range(2)]
        setup_dve = ctx.enter_context(nc.semaphore("setup_dve"))
        SETUP_LB, SETUP_ANGLES = 2, 26
        setup_act = ctx.enter_context(nc.semaphore("setup_act"))
        stored = ctx.enter_context(nc.semaphore("stored"))
        carrier = ctx.enter_context(nc.semaphore("carrier"))

        def apart(eng):
            eng.sem_inc(carrier)

        cst = sb("cst", [P, N_CONST])
        par = sb("par", [P, DEPTH, N_PARAM])
        cur = sb("cur", [P, N_PARAM])
        lb = sb("lb", [P, DEPTH, 4])
        lb_cur = sb("lb_cur", [P, 4])
        fin = sb("fin", [P, KT])
        sin_t = sb("sin_t", [P, SEQ])
        cos_t = sb("cos_t", [P, SEQ])
        x = sb("x", [P, KT, SEQ])
        rstd = sb("rstd", [P, SEQ])
        with ExitStack() as normed_mem:
            h_hi = sb("h_hi", [P, KT, SEQ], F32R, normed_mem)
            h_lo = sb("h_lo", [P, KT, SEQ], F32R, normed_mem)
        between = sb("between", [P, 2 * KT, SEQ])
        raw = sb("raw", [P, 2, KT * P])
        w_hi = sb("w_hi", [P, 2, KT * P], F32R)
        w_lo = sb("w_lo", [P, 2, KT * P], F32R)
        wab_hi = sb("wab_hi", [P, KT, 8], F32R)
        wab_lo = sb("wab_lo", [P, KT, 8], F32R)
        small = sb("small", [P, 16, 16])
        abc = sb("abc", [P, NC, 8])
        lbw = sb("lbw", [P, 8])
        bank = [ctx.enter_context(nc.psum_tensor(f"bank{i}", [P, 512], F32)) for i in range(8)]

        with ExitStack() as mixer_mem:
            gqkv = sb("gqkv", [P, 12, SEQ], F32, mixer_mem)
            gate = sb("gate", [P, GATE_UNITS, SEQ], F32, mixer_mem)
            cp = sb("cp", [P, COPY_UNITS, SEQ], F32, mixer_mem)
            area_a = sb("area_a", [P, 12, SEQ], F32, mixer_mem)
            area_b = sb("area_b", [P, 12, SEQ], F32, mixer_mem)
        with ExitStack() as ffn_mem:
            g_hi = sb("g_hi", [P, FT, SEQ], F32R, ffn_mem)
            g_lo = sb("g_lo", [P, FT, SEQ], F32R, ffn_mem)
            cg = sb("cg", [P, SEQ], F32, ffn_mem)
            cv = sb("cv", [P, SEQ], F32, ffn_mem)
            gt = sb("gt", [P, SEQ], F32, ffn_mem)

        def const(name, i=0, n=None):
            a, _n = CONSTS[name]
            n = _n if n is None else n
            return cst[:, a + i * n:a + (i + 1) * n]

        def param(name, i=0, n=1):
            a, _ = PARAMS[name]
            return cur[:, bass.ds(a + i * n, n)] if not isinstance(i, int) else cur[:, a + i * n:a + (i + 1) * n]

        def chunks(ap):
            return ap.rearrange("p (c i) -> p c i", c=NC)

        def per_chunk(ap):
            return ap.unsqueeze(1).broadcast_to([P, NC, C])

        def even_blocks(ap, half):
            return ap.rearrange("p (g s) -> p g s", s=2 * half)[:, :, 0:half]

        def per_token(ap):
            return ap.unsqueeze(2).broadcast_to([P, ap.shape[1], C])

        ident, causal = const("ident"), const("causal")
        k_out, k_be = (area_a[:, 4 * i:4 * i + 4, :] for i in range(2))
        v_b = between[:, 8:12, :]
        T, R, attn = (area_b[:, 4 * i:4 * i + 4, :] for i in range(3))
        decay, e_b, kcd = T, R, T
        G = gqkv[:, 4:8, :]
        ab_rows = gate[0:8, 9, :]
        ml_ring, p_ring = gqkv[:, 8:10, :], gqkv[:, 10:12, :]
        vn_ring, S_ring = ml_ring, p_ring
        oT = gqkv[:, 0:8, :]
        scratch = gqkv[:, 2:4, :]
        hz, hv = (cp[:, 2 * i:2 * i + 2, :].rearrange("p t n -> p (t n)") for i in range(2))
        rq, rk, rv = (cp[:, 4 + 2 * i:6 + 2 * i, :] for i in range(3))
        rqk = cp[:, 4:8, :]
        PT = area_a[:, 0:4, :]
        k_tok, v_tok = area_a[:, 4:6, :], area_b[:, 6:8, :]
        SU = area_b[:, 8:10, :]
        hE, hs, hl, hf, hg = (gqkv[:, 2 * i:2 * i + 2, :].rearrange("p t n -> p (t n)") for i in range(5))
        hb, hk = (area_a[:, 8 + 2 * i:10 + 2 * i, :].rearrange("p t n -> p (t n)") for i in range(2))
        hq = gate[:, 8:10, :].rearrange("p t n -> p (t n)")
        X_ring = [between[:, 2 * i:2 * i + 2, :].rearrange("p t n -> p (t n)") for i in range(RING)]
        hk_out, hq_in = X_ring[0], X_ring[1]
        hPT = between[:, 12:16, :]
        hk_tok, hv_tok, hSU = (area_b[:, 2 * i:2 * i + 2, :] for i in range(3))
        angles = [area_b[:, 2 * i, :] for i in range(5)]

        za, sp, g_tok, nb, beta, btok, bl, dko, e_tok, ko, w_dec, be, hbl, hw, e_a, abt = (
            small[:, i, :] for i in range(16))

        def hc(ap):
            return ap.rearrange("p (h c) -> p h c", h=HEADS)


        block = ctx.enter_context(nc.Block())

        @block.sync
        def _(sp_):
            freq = CONSTS["ret_w"][0]
            for dst, src in ((angles[0].bitcast(I32), pos_in), (cst[:, freq:], const_in[:, freq:]),
                             (lb[:, :, 0:2], lb_in)):
                sp_.dma_start(dst, src).then_inc(setup_loaded, 16)
            for k in range(KT):
                sp_.dma_start(x[:, k, :], x_in[:, k, :]).then_inc(x_loaded, 16)
            for dst, src in ((par[:, :, :], par_in), (fin[:, :], fin_in), (cst[:, :freq], const_in[:, :freq])):
                sp_.dma_start(dst, src).then_inc(loaded, 16)
            for u in range(2):
                sp_.dma_start(raw[:, u, :], w_in[u]).then_inc(raw_loaded[u], 16)
            with sp_.Fori(1, DEPTH * UNITS // 2) as q:
                for u in range(2):
                    sp_.wait_ge(s["lo_ready"], 2 * q + u - 1)
                    sp_.dma_start(raw[:, u, :], w_in[2 * q + u]).then_inc(raw_loaded[u], 16)
            for k in range(KT):
                sp_.wait_ge(s["x_normed"], DEPTH * 16 + k + 1)
                sp_.dma_start(out[:, k, :], gqkv[:, k, :]).then_inc(stored, 16)
            sp_.wait_ge(stored, 16 * KT)

        @block.gpsimd
        def _(pool):
            tt = nc.gpsimd.tensor_tensor

            def norm_lo(L, which):
                for k in range(KT):
                    pool.wait_ge(s["h_hi_ready"], L * per["h_hi_ready"] + 8 * which + k + 1)
                    tt(h_lo[:, k, :], gqkv[:, k, :], h_hi[:, k, :].bitcast(F32),
                       ALU.subtract).then_inc(s["h_lo_ready"], 1)

            with pool.Fori(0, DEPTH) as L:
                norm_lo(L, 0)
                for h in range(HEADS):
                    pool.wait_ge(s["decay_exp"], L * per["decay_exp"] + h + 1)
                    tt(chunks(decay[:, h, :]), chunks(decay[:, h, :]), per_chunk(causal),
                       ALU.mult).then_inc(s["decay_masked"], 1)
                def level_diff(n):
                    half = LEVELS[n]
                    X = X_ring[n % RING].rearrange("p (g s) -> p g s", s=2 * half)
                    b = hb.rearrange("p (g s) -> p g s", s=2 * half)
                    ref = b[:, :, half - 1:half].broadcast_to([P, 2 * SEQ // (2 * half), half])
                    if n >= RING:
                        pool.wait_ge(s["hg_scores"], L * per["hg_scores"] + 4 * (n - RING + 1))
                    tt(X[:, :, 0:half], ref, b[:, :, 0:half], ALU.subtract)
                    tt(X[:, :, half:], b[:, :, half:], ref, ALU.subtract).then_inc(s["level_diff"], 1)

                pool.wait_ge(s["hg_dve_step"], L * per["hg_dve_step"] + 12)
                pool.wait_ge(s["unit_used"], L * per["unit_used"] + IN_UNITS)
                level_diff(0)
                level_diff(1)
                nc.gpsimd.memset(hPT, 0.0).then_inc(s["hg_scores_cleared"], 1)
                level_diff(2)
                level_diff(3)
                for h in range(HEADS):
                    pool.wait_ge(s["kk_qk_products"], L * per["kk_qk_products"] + h + 1)
                    pool.wait_ge(s["exp_b_ready"], L * per["exp_b_ready"] + h + 1)
                    tt(gqkv[:, h, :], gqkv[:, h, :], e_b[:, h, :], ALU.mult).then_inc(s["q_in_ready"], 1)
                for h in range(HEADS):
                    pool.wait_ge(s["g_attn_ready"], L * per["g_attn_ready"] + h + 1)
                    pool.wait_ge(s["q_in_ready"], L * per["q_in_ready"] + h + 1)
                    tt(chunks(R[:, h, :]), chunks(G[:, h, :]), per_chunk(const("lvl", 0, C)),
                       ALU.mult).then_inc(s["g_smallest"], 1)
                    pool.wait_ge(s["g_smallest"], L * per["g_smallest"] + h + 1)
                    tt(chunks(R[:, h, :]), per_chunk(ident), chunks(R[:, h, :]),
                       ALU.subtract).then_inc(s["inv_first"], 1)
                for k in range(JOINS):
                    if k >= 2:
                        pool.wait_ge(s["gt_product"], L * per["gt_product"] + k - 1)
                    else:
                        pool.wait_ge(s["g_attn_ready"], L * per["g_attn_ready"] + 4)
                        pool.wait_ge(s["kv_turned"], L * per["kv_turned"] + 4)
                    tt(chunks(ml_ring[:, k % 2, :]), chunks(G[:, k % 4, :]), per_chunk(const("lvl", 1 + k // 4, C)),
                       ALU.mult).then_inc(s["g_level"], 1)
                    if k - 1 in LEVEL_AFTER:
                        level_diff(LEVEL_AFTER[k - 1])
                pool.wait_ge(s["hg_act_step"], L * per["hg_act_step"] + 7)
                tt(hq_in, hq_in, hq, ALU.mult).then_inc(s["hg_q_in"], 1)
                for t in range(4):
                    pool.wait_ge(s["rotated"], L * per["rotated"] + t + 1)
                    tt(rqk[:, t, :], rqk[:, t, :], cos_t[:, :], ALU.mult).then_inc(s["rot_cos"], 1)
                for t in range(2):
                    pool.wait_ge(s["ret_scores"], L * per["ret_scores"] + 2 * t + 2)
                    tt(chunks(rq[:, t, :]), chunks(rq[:, t, :]), per_chunk(const("ret_q", t, C)),
                       ALU.mult).then_inc(s["ret_q_in"], 1)
                norm_lo(L, 1)

        @block.scalar
        def _(act):
            A = nc.scalar.activation

            def split_hi(q, u):
                act.wait_ge(raw_loaded[u], 16 * q + 16)
                A(w_hi[:, u, :], raw[:, u, :], ACT.Copy).then_inc(s["hi_ready"], 1)

            def norm(L, which, meanwhile=None):
                nc.scalar.preload_act_table_set("natural_log_exp_and_others")
                for k in range(KT):
                    if which == 0:
                        act.wait_ge(s["x_after_ffn"], L * per["x_after_ffn"] + k + 1)
                    else:
                        act.wait_ge(s["x_after_mixer"], L * per["x_after_mixer"] + k + 1)
                    A(gqkv[:, k, :], x[:, k, :], ACT.Square).then_inc(s["x_squared"], 1)
                if meanwhile:
                    meanwhile()
                act.wait_ge(s["x_mean_square"], L * per["x_mean_square"] + which + 1)
                A(rstd[:, :], bank[2][:, :], ACT.Ln, bias=EPS).then_inc(s["rstd_log"], 1)
                act.wait_ge(s["rstd_log"], L * per["rstd_log"] + which + 1)
                A(rstd[:, :], rstd[:, :], ACT.Exp, scale=-0.5).then_inc(s["rstd_ready"], 1)

            def norm_hi(L, which):
                for k in range(KT):
                    act.wait_ge(s["x_normed"], L * per["x_normed"] + 8 * which + k + 1)
                    A(h_hi[:, k, :], gqkv[:, k, :], ACT.Copy).then_inc(s["h_hi_ready"], 1)

            act.wait_ge(setup_dve, SETUP_LB)
            A(lbw[:, 0:4], lbw[:, 0:4], ACT.Exp).then_inc(setup_act, 1)
            act.wait_ge(setup_dve, SETUP_ANGLES)
            A(sin_t[:, :], sin_t[:, :], ACT.Sin).then_inc(setup_act, 1)
            A(cos_t[:, :], cos_t[:, :], ACT.Sin).then_inc(setup_act, 1)

            with act.Fori(0, DEPTH) as L:
                norm(L, 0, lambda: [split_hi(L * (UNITS // 2), u) for u in range(2)])
                norm_hi(L, 0)
                act.wait_ge(s["params_copied"], L * per["params_copied"] + 1)
                A(wab_hi[:, :, :], param("w_ab", 0, KT * 8).rearrange("p (k n) -> p k n", k=KT),
                  ACT.Copy).then_inc(s["wab_hi_ready"], 1)

                q0 = L * (UNITS // 2)

                def copy_unit(i, u):
                    act.wait_ge(s["unit_used"], L * per["unit_used"] + 2 * i + u + 1)
                    split_hi(q0 + i + 1, u)
                    A(cp[:, 2 * i + u, :], bank[u][:, :], ACT.Copy).then_inc(s["bank_copied"], 1)

                def spread_exps(h):
                    act.wait_ge(s["b_diff_ready"], L * per["b_diff_ready"] + h + 1)
                    A(e_b[:, h, :], bank[2 + h][:, :], ACT.Exp).then_inc(s["exp_b_ready"], 1)
                    A(decay[:, h, :], decay[:, h, :], ACT.Exp).then_inc(s["decay_exp"], 1)

                copy_unit(0, 0)
                copy_unit(0, 1)
                act.wait_ge(s["gate_dve_step"], L * per["gate_dve_step"] + 2)
                A(sp, za, ACT.Abs).then_inc(s["gate_act_step"], 1)
                act.wait_ge(s["gate_act_step"], L * per["gate_act_step"] + 1)
                A(sp, sp, ACT.Exp, scale=-1.0).then_inc(s["gate_act_step"], 1)
                act.wait_ge(s["gate_act_step"], L * per["gate_act_step"] + 2)
                A(sp, sp, ACT.Ln, bias=1.0).then_inc(s["gate_act_step"], 1)
                A(e_a[:, 0:4], param("a_log", 0, 4), ACT.Exp).then_inc(s["gate_act_step"], 1)
                act.wait_ge(s["gate_dve_step"], L * per["gate_dve_step"] + 3)
                A(nb, nb, ACT.Exp).then_inc(s["gate_act_step"], 1)
                copy_unit(1, 0)
                act.wait_ge(s["gate_dve_step"], L * per["gate_dve_step"] + 8)
                A(e_tok, btok, ACT.Exp).then_inc(s["gate_act_step"], 1)
                spread_exps(0)
                spread_exps(1)
                copy_unit(1, 1)
                spread_exps(2)
                spread_exps(3)
                act.wait_ge(s["gate_dve_step"], L * per["gate_dve_step"] + 13)
                A(ko, dko, ACT.Exp).then_inc(s["gate_act_step"], 1)
                A(w_dec, bl, ACT.Exp).then_inc(s["gate_act_step"], 1)
                copy_unit(2, 0)
                act.wait_ge(s["hg_dve_step"], L * per["hg_dve_step"] + 1)
                A(hE, hE, ACT.Exp).then_inc(s["hg_act_step"], 1)
                act.wait_ge(s["hg_act_step"], L * per["hg_act_step"] + 1)
                A(hl, hE, ACT.Ln, bias=1.0).then_inc(s["hg_act_step"], 1)
                copy_unit(2, 1)
                act.wait_ge(s["hg_dve_step"], L * per["hg_dve_step"] + 3)
                A(hf, hs, ACT.Exp, scale=-1.0).then_inc(s["hg_act_step"], 1)
                copy_unit(3, 0)
                act.wait_ge(s["hg_dve_step"], L * per["hg_dve_step"] + 6)
                A(hk, hk, ACT.Exp).then_inc(s["hg_act_step"], 1)
                copy_unit(3, 1)
                act.wait_ge(s["hg_dve_step"], L * per["hg_dve_step"] + 9)
                A(hf, hf, ACT.Ln).then_inc(s["hg_act_step"], 1)
                copy_unit(4, 0)
                copy_unit(4, 1)

                nc.scalar.preload_act_table_set("silu_and_others")
                act.wait_ge(s["hg_dve_step"], L * per["hg_dve_step"] + 12)
                with act.Fori(0, CONV_UNITS // 2) as i:
                    for u in range(2):
                        act.wait_ge(s["unit_used"], L * per["unit_used"] + CONV0 + 2 * i + u + 1)
                        apart(act)
                        A(gqkv[:, 2 * i + u, :], bank[u][:, :], ACT.Copy,
                          scale=param("gdn_conv", (2 * i + u) * 4 + 3)).then_inc(s["conv_last_tap"], 1)
                        split_hi(q0 + CONV0 // 2 + i + 1, u)
                        act.wait_ge(s["conv_done"], L * per["conv_done"] + 2 * i + u + 1)
                        apart(act)
                        A(gqkv[:, 2 * i + u, :], gqkv[:, 2 * i + u, :], ACT.Silu).then_inc(s["qkv_silu"], 1)
                with act.Fori(0, GATE_UNITS // 2) as i:
                    for u in range(2):
                        act.wait_ge(s["unit_used"], L * per["unit_used"] + GATE0 + 2 * i + u + 1)
                        split_hi(q0 + GATE0 // 2 + i + 1, u)
                        A(gate[:, 2 * i + u, :], bank[u][:, :], ACT.Silu).then_inc(s["bank_copied"], 1)

                nc.scalar.preload_act_table_set("natural_log_exp_and_others")
                act.wait_ge(s["qkv_silu"], L * per["qkv_silu"] + 12)
                act.wait_ge(s["x_normed"], L * per["x_normed"] + 8)
                for t in range(8):
                    A(area_a[:, t, :], gqkv[:, t, :], ACT.Square).then_inc(s["l2_squared"], 1)
                def level_exp(n):
                    act.wait_ge(s["level_diff"], L * per["level_diff"] + n + 1)
                    A(X_ring[n % RING], X_ring[n % RING], ACT.Exp).then_inc(s["level_exp"], 1)

                for t in range(8):
                    if t in (3, 6):
                        level_exp(t // 3 - 1)
                    act.wait_ge(s["l2_summed"], L * per["l2_summed"] + t + 1)
                    A(area_a[:, t, :], bank[t % 2][:, :], ACT.Ln, bias=EPS).then_inc(s["l2_log"], 1)
                    act.wait_ge(s["l2_log"], L * per["l2_log"] + t + 1)
                    A(area_a[:, t, :], area_a[:, t, :], ACT.Exp, scale=-0.5).then_inc(s["l2_rnorm"], 1)
                level_exp(2)
                level_exp(3)
                for h in range(HEADS):
                    act.wait_ge(s["inv_first_turned"], L * per["inv_first_turned"] + h + 1)
                    A(T[:, h, :], bank[4 + h % 2][:, :], ACT.Copy).then_inc(s["inv_t_first"], 1)
                for k in range(STEPS):
                    if k < JOINS:
                        act.wait_ge(s["gt_product"], L * per["gt_product"] + k + 1)
                        if k >= 2:
                            act.wait_ge(s["tgt_product"], L * per["tgt_product"] + k - 1)
                        A(p_ring[:, k % 2, :], bank[k % 2][:, :], ACT.Copy).then_inc(s["gt_copied"], 1)
                    if k >= 2:
                        act.wait_ge(s["inv_turned"], L * per["inv_turned"] + k - 1)
                        A(R[:, (k - 2) % 4, :], bank[4 + k % 2][:, :], ACT.Copy).then_inc(s["inv_r_updated"], 1)
                    if k - 4 in LEVEL_AFTER:
                        level_exp(LEVEL_AFTER[k - 4])
                for h in range(HEADS):
                    act.wait_ge(s["kcd_product"], L * per["kcd_product"] + h + 1)
                    A(kcd[:, h, :], bank[6 + h % 2][:, :], ACT.Copy, scale=-1.0).then_inc(s["kcd_ready"], 1)
                act.wait_ge(s["hg_dve_step"], L * per["hg_dve_step"] + 13)
                A(hk_out, hk_out, ACT.Exp).then_inc(s["hg_act_step"], 1)
                A(hq_in, hb, ACT.Exp).then_inc(s["hg_act_step"], 1)
                A(hw[:, 0:8], hbl[:, 0:8], ACT.Exp).then_inc(s["hg_act_step"], 1)
                for c in range(NC):
                    act.wait_ge(s["v_new_product"], L * per["v_new_product"] + c + 1)
                    if c >= 2:
                        act.wait_ge(s["delta_out"], L * per["delta_out"] + c - 1)
                    A(vn_ring[:, c % 2, :], bank[c % 2][:, :], ACT.Copy).then_inc(s["v_new_ready"], 1)
                act.wait_ge(s["delta_out"], L * per["delta_out"] + 4)
                for h in range(HEADS):
                    A(oT[:, 4 + h, :], bank[2 + h][:, :], ACT.Copy).then_inc(s["delta_out_copied"], 1)

                for t in range(4):
                    act.wait_ge(s["hg_turned"], L * per["hg_turned"] + t + 1)
                    dst = hk_tok if t < 2 else hv_tok
                    A(dst[:, t % 2, :], bank[4 + t][:, :], ACT.Copy).then_inc(s["hg_turned_copied"], 1)
                for t in range(2):
                    act.wait_ge(s["ret_turned"], L * per["ret_turned"] + 3 + t)
                    A(v_tok[:, t, :], bank[6 + t][:, :], ACT.Copy).then_inc(s["ret_v_copied"], 1)
                for t in range(2):
                    act.wait_ge(s["hg_out"], L * per["hg_out"] + t + 1)
                    A(oT[:, 2 + t, :], bank[6 + t][:, :], ACT.Copy).then_inc(s["hg_out_copied"], 1)
                for t in range(2):
                    act.wait_ge(s["ret_out"], L * per["ret_out"] + t + 1)
                    A(oT[:, t, :], bank[2 + t][:, :], ACT.Copy).then_inc(s["ret_out_copied"], 1)

                for t in range(8):
                    if t == 0:
                        act.wait_ge(s["ret_out_copied"], L * per["ret_out_copied"] + 2)
                        act.wait_ge(s["delta_out_copied"], L * per["delta_out_copied"] + 4)
                        act.wait_ge(s["hg_out_copied"], L * per["hg_out_copied"] + 2)
                        act.wait_ge(s["hg_out"], L * per["hg_out"] + 2)
                    A(area_a[:, t, :], oT[:, t, :], ACT.Square).then_inc(s["out_squared"], 1)
                for t in range(8):
                    act.wait_ge(s["out_mean_square"], L * per["out_mean_square"] + t + 1)
                    A(area_a[:, t, :], bank[t % 2][:, :], ACT.Ln, bias=EPS).then_inc(s["out_log"], 1)
                    act.wait_ge(s["out_log"], L * per["out_log"] + t + 1)
                    A(area_a[:, t, :], area_a[:, t, :], ACT.Exp, scale=-0.5).then_inc(s["out_rstd"], 1)
                for t in range(8):
                    act.wait_ge(s["out_gated"], L * per["out_gated"] + t + 1)
                    A(h_hi[:, t, :], oT[:, t, :], ACT.Copy).then_inc(s["mix_hi_ready"], 1)

                with act.Fori(0, OUT_UNITS // 2) as i:
                    for u in range(2):
                        act.wait_ge(s["unit_used"], L * per["unit_used"] + OUT0 + 2 * i + u + 1)
                        split_hi(q0 + OUT0 // 2 + i + 1, u)

                norm(L, 1)
                norm_hi(L, 1)

                nc.scalar.preload_act_table_set("silu_and_others")
                with act.Fori(0, FT) as i:
                    for u, dst in ((0, cg), (1, cv)):
                        act.wait_ge(s["unit_used"], L * per["unit_used"] + UP0 + 2 * i + u + 1)
                        split_hi(q0 + UP0 // 2 + i + 1, u)
                        A(dst[:, :], bank[u][:, :], ACT.Identity,
                          scale=param("ffn_conv", (2 * i + u) * 3 + 2),
                          bias=param("ffn_bias", 2 * i + u)).then_inc(s["ffn_last_tap"], 1)
                        if u == 0:
                            act.wait_ge(s["ffn_conv_done"], L * per["ffn_conv_done"] + 2 * i + 1)
                            A(cg[:, :], cg[:, :], ACT.Silu).then_inc(s["ffn_silu"], 1)
                    act.wait_ge(s["ffn_product"], L * per["ffn_product"] + i + 1)
                    A(g_hi[:, bass.ds(i, 1), :], gt[:, :].unsqueeze(1), ACT.Copy).then_inc(s["g_hi_ready"], 1)

                with act.Fori(0, DOWN_UNITS // 2 - 1) as i:
                    for u in range(2):
                        act.wait_ge(s["unit_used"], L * per["unit_used"] + DOWN0 + 2 * i + u + 1)
                        split_hi(q0 + DOWN0 // 2 + i + 1, u)
            norm(DEPTH, 0)

        @block.vector
        def _(dve):
            tt, ts, stt = nc.vector.tensor_tensor, nc.vector.tensor_scalar, nc.vector.scalar_tensor_tensor

            def split_lo(L, k, u):
                dve.wait_ge(s["hi_ready"], L * per["hi_ready"] + k + 1)
                tt(w_lo[:, u, :], raw[:, u, :], w_hi[:, u, :].bitcast(F32),
                   ALU.subtract).then_inc(s["lo_ready"], 1)

            def norm(L, which, weight):
                dve.wait_ge(s["rstd_ready"], L * per["rstd_ready"] + which + 1)
                for k in range(KT):
                    stt(gqkv[:, k, :], x[:, k, :], weight(k), rstd[:, :], ALU.mult,
                        ALU.mult).then_inc(s["x_normed"], 1)

            steps = [0]
            dve.wait_ge(setup_loaded, 48)

            def once(ins):
                ins.then_inc(setup_dve, 1)
                steps[0] += 1
                dve.wait_ge(setup_dve, steps[0])

            l0, l1 = lb[:, 0, 0:2], lb[:, 1, 0:2]
            once(tt(lbw[:, 4:6], l0, l1, ALU.max))
            once(tt(lbw[:, 0:4].rearrange("p (l t) -> p l t", l=DEPTH), lb[:, :, 0:2],
                    lbw[:, 4:6].unsqueeze(1).broadcast_to([P, DEPTH, 2]), ALU.subtract))
            dve.wait_ge(setup_act, 1)
            once(tt(lbw[:, 4:6], lbw[:, 0:2], lbw[:, 2:4], ALU.add))
            once(nc.vector.reciprocal(lbw[:, 6:8], lbw[:, 4:6]))
            once(tt(lbw[:, 0:4].rearrange("p (l t) -> p l t", l=DEPTH),
                    lbw[:, 0:4].rearrange("p (l t) -> p l t", l=DEPTH),
                    lbw[:, 6:8].unsqueeze(1).broadcast_to([P, DEPTH, 2]), ALU.mult))
            once(tt(lbw[:, 2:4], lbw[:, 0:2], lbw[:, 2:4], ALU.add))
            for layer in range(DEPTH):
                once(tt(lb[:, layer, 0:2], lbw[:, 2 * layer:2 * layer + 2], lbw[:, 0:2], ALU.subtract))
            once(ts(lb[:, :, 0:2], lb[:, :, 0:2], 0.0, None, ALU.max))
            once(ts(lb[:, :, 2:4], lb[:, :, 0:2], -1.0, 1.0, ALU.mult, ALU.add))
            posf, ang, turns, n_turns = angles[1:]
            magic = 12582912.0
            two_pi = [6.28125, float(np.float32(2 * np.pi - 6.28125))]
            two_pi.append(float(2 * np.pi - two_pi[0] - two_pi[1]))
            once(nc.vector.tensor_copy(posf, angles[0].bitcast(I32)))
            once(ts(ang, posf, const("inv_freq"), None, ALU.mult))
            for dst, quarter in ((sin_t, 0.0), (cos_t, 0.25)):
                once(ts(turns, ang, float(1 / (2 * np.pi)), quarter, ALU.mult, ALU.add))
                once(ts(n_turns, turns, magic, -magic, ALU.add, ALU.add))
                once(stt(turns, n_turns, -two_pi[0], ang, ALU.mult, ALU.add))
                once(stt(turns, n_turns, -two_pi[1], turns, ALU.mult, ALU.add))
                once(stt(turns, n_turns, -two_pi[2], turns, ALU.mult, ALU.add))
                once(ts(turns, turns, float(2 * np.pi * quarter), 3.1415925, ALU.add, ALU.min))
                once(ts(dst[:, :], turns, -3.1415925, None, ALU.max))
            assert steps[0] == SETUP_ANGLES
            dve.wait_ge(setup_act, 3)
            dve.wait_ge(x_loaded, 16 * KT)
            dve.sem_inc(s["x_after_ffn"], KT)
            dve.wait_ge(loaded, 48)

            with dve.Fori(0, DEPTH) as L:
                nc.vector.tensor_copy(lb_cur[:, :].unsqueeze(1), lb[:, bass.ds(L, 1), :])
                nc.vector.tensor_copy(cur[:, :].unsqueeze(1), par[:, bass.ds(L, 1), :]).then_inc(s["params_copied"], 1)
                dve.wait_ge(s["params_copied"], L * per["params_copied"] + 1)
                norm(L, 0, lambda k: param("norm1", k))
                for u in range(2):
                    split_lo(L, u, u)
                dve.wait_ge(s["wab_hi_ready"], L * per["wab_hi_ready"] + 1)
                tt(wab_lo[:, :, :], param("w_ab", 0, KT * 8).rearrange("p (k n) -> p k n", k=KT),
                   wab_hi[:, :, :].bitcast(F32), ALU.subtract).then_inc(s["wab_lo_ready"], 1)

                dve.wait_ge(s["ab_projected"], L * per["ab_projected"] + 1)
                gd = s["gate_dve_step"]
                nc.vector.tensor_copy(ab_rows, bank[6][0:8, :]).then_inc(s["ab_copied"], 1)
                split_lo(L, 2, 0)
                split_lo(L, 3, 1)
                dve.wait_ge(s["ab_turned"], L * per["ab_turned"] + 1)
                nc.vector.tensor_copy(abc[:, :, :], bank[7][:, 0:32].rearrange("p (c n) -> p c n", c=NC)).then_inc(gd, 1)
                dve.wait_ge(s["gate_dve_step"], L * per["gate_dve_step"] + 1)
                tt(hc(za), abc[:, :, 0:4].rearrange("p c h -> p h c"),
                   param("dt_bias", 0, 4).unsqueeze(2).broadcast_to([P, HEADS, NC]), ALU.add).then_inc(gd, 1)
                ts(hc(nb), abc[:, :, 4:8].rearrange("p c h -> p h c"), -1.0, 80.0, ALU.mult, ALU.min).then_inc(gd, 1)
                dve.wait_ge(s["gate_act_step"], L * per["gate_act_step"] + 3)
                stt(sp, za, 0.0, sp, ALU.max, ALU.add).then_inc(gd, 1)
                dve.wait_ge(s["gate_act_step"], L * per["gate_act_step"] + 4)
                dve.wait_ge(s["gate_dve_step"], L * per["gate_dve_step"] + 4)
                stt(hc(g_tok), hc(sp), -1.0, e_a[:, 0:4].unsqueeze(2).broadcast_to([P, HEADS, NC]),
                    ALU.mult, ALU.mult).then_inc(gd, 1)
                dve.wait_ge(s["gate_act_step"], L * per["gate_act_step"] + 5)
                ts(nb, nb, 1.0, None, ALU.add).then_inc(gd, 1)
                dve.wait_ge(s["gate_dve_step"], L * per["gate_dve_step"] + 6)
                nc.vector.reciprocal(beta, nb).then_inc(gd, 1)
                split_lo(L, 4, 0)
                dve.wait_ge(s["b_token_major"], L * per["b_token_major"] + 1)
                nc.vector.tensor_copy(btok, bank[6][:, 64:80]).then_inc(gd, 1)
                dve.wait_ge(s["gate_dve_step"], L * per["gate_dve_step"] + 8)
                for h in range(HEADS):
                    dve.wait_ge(s["b_spread"], L * per["b_spread"] + h + 1)
                    nc.vector.tensor_copy(hc(bl)[:, h, :], chunks(bank[2 + h][:, :])[:, :, C - 1]).then_inc(gd, 1)
                    for c in range(NC):
                        ins = ts(decay[:, h, c * C:(c + 1) * C], bank[2 + h][:, c * C:(c + 1) * C],
                                 btok[:, h * NC + c:h * NC + c + 1], 0.0, ALU.subtract, ALU.min)
                    ins.then_inc(s["b_diff_ready"], 1)
                    if h == 1:
                        split_lo(L, 5, 1)
                dve.wait_ge(s["gate_dve_step"], L * per["gate_dve_step"] + 12)
                tt(dko, bl, btok, ALU.subtract).then_inc(gd, 1)
                dve.wait_ge(s["gate_act_step"], L * per["gate_act_step"] + 6)
                tt(be, beta, e_tok, ALU.mult).then_inc(gd, 1)

                hd = s["hg_dve_step"]
                split_lo(L, 6, 0)
                dve.wait_ge(s["h_lo_ready"], L * per["h_lo_ready"] + 8)
                dve.wait_ge(s["bank_copied"], L * per["bank_copied"] + 2)
                ts(hE, hz, -1.0, 40.0, ALU.mult, ALU.min).then_inc(hd, 1)
                ts(hs, hz, -1.0, -40.0, ALU.mult, ALU.add).then_inc(hd, 1)
                dve.wait_ge(s["hg_dve_step"], L * per["hg_dve_step"] + 2)
                ts(hs, hs, 0.0, 40.0, ALU.max, ALU.min).then_inc(hd, 1)
                ts(hg, hz, 40.0, 0.0, ALU.add, ALU.min).then_inc(hd, 1)
                split_lo(L, 7, 1)
                dve.wait_ge(s["hg_act_step"], L * per["hg_act_step"] + 2)
                tt(hk, hz, hl, ALU.add).then_inc(hd, 1)
                dve.wait_ge(s["hg_dve_step"], L * per["hg_dve_step"] + 5)
                ts(hk, hk, -1.0, 0.0, ALU.mult, ALU.min).then_inc(hd, 1)
                tt(hg, hg, hl, ALU.subtract).then_inc(hd, 1)
                dve.wait_ge(s["hg_dve_step"], L * per["hg_dve_step"] + 7)
                tt(hg, hg, hs, ALU.add).then_inc(hd, 1)
                split_lo(L, 8, 0)
                dve.wait_ge(s["hg_act_step"], L * per["hg_act_step"] + 3)
                for t in range(2):
                    o = slice(t * SEQ, (t + 1) * SEQ)
                    ins = stt(hf[:, o], hE[:, o], lb_cur[:, t:t + 1], hf[:, o], ALU.mult, ALU.add)
                ins.then_inc(hd, 1)
                split_lo(L, 9, 1)
                dve.wait_ge(s["hg_act_step"], L * per["hg_act_step"] + 4)
                for t in range(2):
                    o = slice(t * SEQ, (t + 1) * SEQ)
                    ins = ts(hk[:, o], hk[:, o], lb_cur[:, 2 + t:3 + t], None, ALU.mult)
                ins.then_inc(hd, 1)
                split_lo(L, 10, 0)
                dve.wait_ge(s["hg_act_step"], L * per["hg_act_step"] + 5)
                dve.wait_ge(s["hg_dve_step"], L * per["hg_dve_step"] + 8)
                tt(hg, hg, hf, ALU.add).then_inc(hd, 1)
                dve.wait_ge(s["hg_dve_step"], L * per["hg_dve_step"] + 11)
                for c in range(2 * NC):
                    o = slice(c * C, (c + 1) * C)
                    ins = nc.vector.tensor_tensor_scan(hb[:, o], const("ones"), hg[:, o], 0.0,
                                                       ALU.mult, ALU.add)
                ins.then_inc(hd, 1)
                split_lo(L, 11, 1)
                with dve.Fori(0, CONV_UNITS // 2) as i:
                    for u in range(2):
                        n = 2 * i + u
                        for tap in range(1, 4):
                            if tap == 1:
                                dve.wait_ge(s["conv_last_tap"], L * per["conv_last_tap"] + n + 1)
                            else:
                                dve.wait_ge(s["conv_mid_taps"], L * per["conv_mid_taps"] + 2 * n + tap - 1)
                            o = gqkv[:, bass.ds(n, 1), tap:SEQ]
                            stt(o, bank[u][:, 0:SEQ - tap].unsqueeze(1), param("gdn_conv", n * 4 + 3 - tap), o,
                                ALU.mult, ALU.add).then_inc(s["conv_mid_taps"] if tap < 3 else s["conv_done"], 1)
                        split_lo(L, CONV0 + n + 2, u)
                with dve.Fori(0, GATE_UNITS // 2) as i:
                    for u in range(2):
                        split_lo(L, GATE0 + 2 * i + 2 + u, u)

                dve.wait_ge(s["gate_dve_step"], L * per["gate_dve_step"] + 14)
                for h in range(HEADS):
                    dve.wait_ge(s["kv_turned"], L * per["kv_turned"] + h + 1)
                    tt(chunks(v_b[:, h, :]), chunks(bank[6 + h % 2][:, :]), per_token(hc(beta)[:, h, :]),
                       ALU.mult).then_inc(s["kv_turned_read"], 1)
                def level_qk(n):
                    half = LEVELS[n]
                    X, k3, q3 = (a.rearrange("p (g s) -> p g s", s=2 * half) for a in (X_ring[n % RING], hk, hq))
                    dve.wait_ge(s["level_exp"], L * per["level_exp"] + n + 1)
                    tt(X[:, :, 0:half], X[:, :, 0:half], k3[:, :, 0:half], ALU.mult)
                    tt(X[:, :, half:], X[:, :, half:], q3[:, :, half:], ALU.mult).then_inc(s["level_qk"], 1)

                def place(g):
                    n, h = g // HEADS, g % HEADS
                    mask = const("lvl", n, C) if n < len(LEVELS) else ident
                    dve.wait_ge(s["hg_scores"], L * per["hg_scores"] + g + 1)
                    if n:
                        dve.wait_ge(s["hg_scores_placed"], L * per["hg_scores_placed"] + g - HEADS + 1)
                    else:
                        dve.wait_ge(s["hg_scores_cleared"], L * per["hg_scores_cleared"] + 1)
                    apart(dve)
                    to, src, mask4 = chunks(hPT[:, h, :]), chunks(bank[6 + g % 2][:, :]), per_chunk(mask.bitcast(I32))
                    if n < len(LEVELS):
                        to, src, mask4 = (a.rearrange("p c (g s) -> p c g s", s=2 * LEVELS[n])[:, :, :, LEVELS[n]:]
                                          for a in (to, src, mask4))
                    nc.vector.copy_predicated(to, mask4, src).then_inc(s["hg_scores_placed"], 1)

                for t in range(8):
                    dve.wait_ge(s["l2_rnorm"], L * per["l2_rnorm"] + t + 1)
                    stt(gqkv[:, t, :], gqkv[:, t, :], float(P) ** -0.5 if t < 4 else 1.0, area_a[:, t, :],
                        ALU.mult, ALU.mult).then_inc(s["qk_normed"], 1)
                dve.wait_ge(s["qk_normed"], L * per["qk_normed"] + 8)
                dve.wait_ge(s["gate_act_step"], L * per["gate_act_step"] + 8)
                for h in range(HEADS):
                    dve.wait_ge(s["kv_turned"], L * per["kv_turned"] + 4 + h + 1)
                    tt(chunks(k_out[:, h, :]), chunks(bank[6 + h % 2][:, :]), per_token(hc(ko)[:, h, :]),
                       ALU.mult).then_inc(s["k_out_ready"], 1)
                    tt(chunks(k_be[:, h, :]), chunks(bank[6 + h % 2][:, :]), per_token(hc(be)[:, h, :]),
                       ALU.mult).then_inc(s["kv_turned_read"], 1)
                level_qk(0)
                level_qk(1)
                dve.wait_ge(s["decay_masked"], L * per["decay_masked"] + 4)
                for h in range(HEADS):
                    e = h % 2
                    dve.wait_ge(s["kk_qk_products"], L * per["kk_qk_products"] + h + 1)
                    tt(attn[:, h, :], bank[2 + e][:, :], decay[:, h, :], ALU.mult)
                    tt(G[:, h, :], bank[e][:, :], decay[:, h, :], ALU.mult).then_inc(s["kk_decayed"], 1)
                    dve.wait_ge(s["kk_decayed"], L * per["kk_decayed"] + h + 1)
                    tt(G[:, h, :], bank[4 + e][:, :], G[:, h, :], ALU.mult).then_inc(s["g_attn_ready"], 1)
                level_qk(2)
                for k in range(STEPS):
                    if 1 <= k < JOINS + 1:
                        dve.wait_ge(s["tgt_product"], L * per["tgt_product"] + k)
                        if k < 5:
                            dve.wait_ge(s["inv_t_first"], L * per["inv_t_first"] + k)
                        else:
                            dve.wait_ge(s["inv_t_updated"], L * per["inv_t_updated"] + k - 4)
                        half = LEVELS[1 + (k - 1) // 4]
                        to_join = even_blocks(T[:, (k - 1) % 4, :], half)
                        tt(to_join, to_join, even_blocks(bank[2 + (k - 1) % 2][:, :], half),
                           ALU.subtract).then_inc(s["inv_t_updated"], 1)
                    for g in groups_of(k):
                        place(g)
                    if k == 4:
                        level_qk(3)
                    if k - 5 in LEVEL_AFTER:
                        level_qk(LEVEL_AFTER[k - 5])
                bc = hb.rearrange("p (c i) -> p c i", i=C)
                nc.vector.tensor_copy(hbl[:, 0:8].unsqueeze(2), bc[:, :, C - 1:C])
                tt(hk_out.rearrange("p (c i) -> p c i", i=C), bc[:, :, C - 1:C].broadcast_to([P, 2 * NC, C]), bc,
                   ALU.subtract).then_inc(hd, 1)
                for c in range(NC - 1):
                    dve.wait_ge(s["state_sum"], L * per["state_sum"] + c + 1)
                    if c == 0:
                        nc.vector.tensor_copy(S_ring[:, 0, :], bank[6][:, :]).then_inc(s["state_ready"], 1)
                        dve.wait_ge(s["hg_act_step"], L * per["hg_act_step"] + 6)
                        tt(hk_out, hk_out, hk, ALU.mult).then_inc(hd, 1)
                        continue
                    dve.wait_ge(s["state_ready"], L * per["state_ready"] + c)
                    if c >= 2:
                        dve.wait_ge(s["delta_out"], L * per["delta_out"] + c)
                    for h in range(HEADS):
                        o = slice(h * P, (h + 1) * P)
                        ins = stt(S_ring[:, c % 2, o], S_ring[:, (c - 1) % 2, o], w_dec[:, h * NC + c:h * NC + c + 1],
                                  bank[6 + c % 2][:, o], ALU.mult, ALU.add)
                    ins.then_inc(s["state_ready"], 1)

                def states(to, first_bank, w_of, summed, per_sum, done, per_done):
                    for t in range(2):
                        dve.wait_ge(summed, L * per_sum + t + 1)
                        st = to[:, t, 0:3 * P].rearrange("p (c n) -> p c n", c=3)
                        tt(st, bank[first_bank + t][:, 0:3 * P].rearrange("p (c n) -> p c n", c=3),
                           const("blocks").unsqueeze(1).broadcast_to([P, 3, P]), ALU.mult).then_inc(done, 1)
                        for c in range(1, 3):
                            dve.wait_ge(done, L * per_done + 3 * t + c)
                            stt(st[:, c, :], st[:, c - 1, :], w_of(t, c), st[:, c, :], ALU.mult,
                                ALU.add).then_inc(done, 1)

                for t in range(4):
                    dve.wait_ge(s["rotated"], L * per["rotated"] + t + 1)
                    if t >= 2:
                        dve.wait_ge(s["rot_done"], L * per["rot_done"] + t - 1)
                    tt(scratch[:, t % 2, :], bank[t % 2][:, :], sin_t[:, :], ALU.mult).then_inc(s["rot_sin"], 1)
                    dve.wait_ge(s["rot_sin"], L * per["rot_sin"] + t + 1)
                    dve.wait_ge(s["rot_cos"], L * per["rot_cos"] + t + 1)
                    tt(rqk[:, t, :], rqk[:, t, :], scratch[:, t % 2, :], ALU.add).then_inc(s["rot_done"], 1)
                for h in range(HEADS):
                    dve.wait_ge(s["ret_scores"], L * per["ret_scores"] + h + 1)
                    tt(chunks(PT[:, h, :]), chunks(bank[2 + h % 2][:, :]), per_chunk(const("ret_decay", h, C)),
                       ALU.mult).then_inc(s["ret_decayed"], 1)
                for t in range(2):
                    dve.wait_ge(s["ret_turned"], L * per["ret_turned"] + t + 1)
                    tt(chunks(k_tok[:, t, :]), chunks(bank[4 + t][:, :]), per_chunk(const("ret_k", t, P)),
                       ALU.mult).then_inc(s["ret_k_out"], 1)
                states(hSU, 0, lambda t, c: hw[:, t * NC + c:t * NC + c + 1], s["hg_sums"], per["hg_sums"],
                       s["hg_states"], per["hg_states"])
                states(SU, 4, lambda t, c: const("ret_w", t, 1), s["ret_sums"], per["ret_sums"],
                       s["ret_states"], per["ret_states"])

                for t in range(8 + 1):
                    if t < 8:
                        dve.wait_ge(s["out_rstd"], L * per["out_rstd"] + t + 1)
                        stt(oT[:, t, :], oT[:, t, :], param("onorm", t), area_a[:, t, :], ALU.mult,
                            ALU.mult).then_inc(s["out_normed"], 1)
                        dve.wait_ge(s["out_normed"], L * per["out_normed"] + t + 1)
                        tt(oT[:, t, :], oT[:, t, :], gate[:, t, :], ALU.mult).then_inc(s["out_gated"], 1)
                    if t:
                        dve.wait_ge(s["mix_hi_ready"], L * per["mix_hi_ready"] + t)
                        tt(h_lo[:, t - 1, :], oT[:, t - 1, :], h_hi[:, t - 1, :].bitcast(F32),
                           ALU.subtract).then_inc(s["mix_lo_ready"], 1)

                with dve.Fori(0, OUT_UNITS // 2) as i:
                    for u in range(2):
                        split_lo(L, OUT0 + 2 + 2 * i + u, u)
                for m in range(KT):
                    if m < KT - 1:
                        dve.wait_ge(s["out_projected"], L * per["out_projected"] + m + 1)
                    else:
                        dve.wait_ge(s["unit_used"], L * per["unit_used"] + OUT0 + 8)
                    tt(x[:, m, :], x[:, m, :], bank[(m + 2) % 8][:, :], ALU.add).then_inc(s["x_after_mixer"], 1)
                dve.wait_ge(s["x_after_mixer"], L * per["x_after_mixer"] + 8)
                norm(L, 1, lambda k: param("norm2", k))

                with dve.Fori(0, FT) as i:
                    for u, dst in ((0, cg), (1, cv)):
                        split_lo(L, UP0 + 2 + 2 * i + u, u)
                        n = 2 * i + u
                        dve.wait_ge(s["ffn_last_tap"], L * per["ffn_last_tap"] + n + 1)
                        stt(dst[:, 1:SEQ], bank[u][:, 0:SEQ - 1], param("ffn_conv", n * 3 + 1), dst[:, 1:SEQ],
                            ALU.mult, ALU.add).then_inc(s["ffn_mid_tap"], 1)
                        dve.wait_ge(s["ffn_mid_tap"], L * per["ffn_mid_tap"] + n + 1)
                        stt(dst[:, 2:SEQ], bank[u][:, 0:SEQ - 2], param("ffn_conv", n * 3), dst[:, 2:SEQ],
                            ALU.mult, ALU.add).then_inc(s["ffn_conv_done"], 1)
                    dve.wait_ge(s["ffn_conv_done"], L * per["ffn_conv_done"] + 2 * i + 2)
                    dve.wait_ge(s["ffn_silu"], L * per["ffn_silu"] + i + 1)
                    tt(gt[:, :], cg[:, :], cv[:, :], ALU.mult).then_inc(s["ffn_product"], 1)
                    dve.wait_ge(s["g_hi_ready"], L * per["g_hi_ready"] + i + 1)
                    tt(g_lo[:, bass.ds(i, 1), :], gt[:, :].unsqueeze(1), g_hi[:, bass.ds(i, 1), :].bitcast(F32),
                       ALU.subtract).then_inc(s["g_lo_ready"], 1)

                with dve.Fori(0, DOWN_UNITS // 2 - 1) as i:
                    for u in range(2):
                        split_lo(L, DOWN0 + 2 + 2 * i + u, u)
                for m in range(KT):
                    if m < KT - 1:
                        dve.wait_ge(s["down_projected"], L * per["down_projected"] + m + 1)
                    else:
                        dve.wait_ge(s["unit_used"], L * per["unit_used"] + UNITS)
                    tt(x[:, m, :], x[:, m, :], bank[(m + 2) % 8][:, :], ALU.add).then_inc(s["x_after_ffn"], 1)
                dve.wait_ge(s["x_after_ffn"], 8 * L + 16)

            norm(DEPTH, 0, lambda k: fin[:, k:k + 1])

        @block.tensor
        def _(pe):
            mm = nc.tensor.matmul

            def norm(L, which):
                for k in range(KT):
                    pe.wait_ge(s["x_squared"], L * per["x_squared"] + 8 * which + k + 1)
                    ins = mm(bank[2][:, :], const("mean_model"), gqkv[:, k, :], start=k == 0, stop=k == KT - 1)
                ins.then_inc(s["x_mean_square"], 1)

            def three(dst, hi, lo, b_hi, b_lo, start, stop):
                mm(dst, hi, b_hi, start=start, stop=False)
                mm(dst, hi, b_lo, start=False, stop=False)
                return mm(dst, lo, b_hi, start=False, stop=stop)

            def unit(L, k, u, normed_before=None):
                pe.wait_ge(s["lo_ready"], L * per["lo_ready"] + k + 1)
                for kt in range(KT):
                    if normed_before is not None:
                        pe.wait_ge(s["h_lo_ready"], L * per["h_lo_ready"] + normed_before + kt + 1)
                    o = slice(kt * P, (kt + 1) * P)
                    ins = three(bank[u][:, :], w_hi[:, u, o], w_lo[:, u, o], h_hi[:, kt, :], h_lo[:, kt, :],
                                kt == 0, kt == KT - 1)
                ins.then_inc(s["unit_used"], 1)
                return ins

            def rows(L, k, u, b_hi, b_lo, start, stop, last=None, over_up=False):
                pe.wait_ge(s["lo_ready"], L * per["lo_ready"] + k + 1)
                for m in range(KT):
                    if over_up and m >= KT - 2:
                        pe.wait_ge(s["ffn_conv_done"], L * per["ffn_conv_done"] + UP_UNITS - (KT - 1 - m))
                    o = slice(m * P, (m + 1) * P)
                    ins = three(bank[(m + 2) % 8][:, :], w_hi[:, u, o], w_lo[:, u, o], b_hi, b_lo, start, stop)
                    if last and m < KT - 1:
                        ins.then_inc(last, 1)
                ins.then_inc(s["unit_used"], 1)

            pe.wait_ge(loaded, 48)
            with pe.Fori(0, DEPTH) as L:
                norm(L, 0)
                unit(L, 0, 0, normed_before=0)
                pe.wait_ge(s["wab_lo_ready"], L * per["wab_lo_ready"] + 1)
                for kt in range(KT):
                    ins = three(bank[6][0:8, :], wab_hi[:, kt, :], wab_lo[:, kt, :], h_hi[:, kt, :], h_lo[:, kt, :],
                                kt == 0, kt == KT - 1)
                ins.then_inc(s["ab_projected"], 1)
                unit(L, 1, 1)
                pe.wait_ge(s["ab_copied"], L * per["ab_copied"] + 1)
                apart(pe)
                for c in range(NC):
                    ins = nc.tensor.transpose(bank[7][:, c * 8:c * 8 + 8], ab_rows[:, c * C:(c + 1) * C], ident[0:8, 0:8])
                ins.then_inc(s["ab_turned"], 1)
                pe.wait_ge(s["bank_copied"], L * per["bank_copied"] + 1)
                unit(L, 2, 0)
                pe.wait_ge(s["gate_dve_step"], L * per["gate_dve_step"] + 5)
                mm(bank[6][:, 64:80], causal, g_tok, start=True, stop=True).then_inc(s["b_token_major"], 1)
                for h in range(HEADS):
                    for c in range(NC):
                        ins = mm(bank[2 + h][:, c * C:(c + 1) * C],
                                 g_tok[:, h * NC + c:h * NC + c + 1].broadcast_to([P, C]), causal,
                                 start=True, stop=True)
                    ins.then_inc(s["b_spread"], 1)
                pe.wait_ge(s["bank_copied"], L * per["bank_copied"] + 2)
                unit(L, 3, 1)
                with pe.Fori(2, COPY_UNITS // 2) as i:
                    for u in range(2):
                        pe.wait_ge(s["bank_copied"], L * per["bank_copied"] + 2 * i + u - 1)
                        unit(L, 2 * i + u, u)
                for u in range(2):
                    pe.wait_ge(s["bank_copied"], L * per["bank_copied"] + COPY_UNITS - 1 + u)
                    unit(L, CONV0 + u, u)
                with pe.Fori(1, CONV_UNITS // 2) as i:
                    for u in range(2):
                        pe.wait_ge(s["conv_done"], L * per["conv_done"] + 2 * i + u - 1)
                        unit(L, CONV0 + 2 * i + u, u)
                for u in range(2):
                    pe.wait_ge(s["conv_done"], L * per["conv_done"] + CONV_UNITS - 1 + u)
                    unit(L, GATE0 + u, u)
                with pe.Fori(1, GATE_UNITS // 2) as i:
                    for u in range(2):
                        pe.wait_ge(s["bank_copied"], L * per["bank_copied"] + COPY_UNITS + 2 * i + u - 1)
                        unit(L, GATE0 + 2 * i + u, u)

                def turn(dst, src):
                    for c in range(NC):
                        o = slice(c * C, (c + 1) * C)
                        ins = nc.tensor.transpose(dst[:, o], src[:, o], ident)
                    return ins

                pe.wait_ge(s["qkv_silu"], L * per["qkv_silu"] + 12)
                pe.wait_ge(s["gate_dve_step"], L * per["gate_dve_step"] + 8)
                for h in range(HEADS):
                    if h >= 2:
                        pe.wait_ge(s["kv_turned_read"], L * per["kv_turned_read"] + h - 1)
                    turn(bank[6 + h % 2], gqkv[:, 8 + h, :]).then_inc(s["kv_turned"], 1)
                pe.wait_ge(s["bank_copied"], L * per["bank_copied"] + GATE_UNITS + COPY_UNITS)
                for t in range(8):
                    pe.wait_ge(s["l2_squared"], L * per["l2_squared"] + t + 1)
                    if t >= 2:
                        pe.wait_ge(s["l2_log"], L * per["l2_log"] + t - 1)
                    mm(bank[t % 2][:, :], const("ones"), area_a[:, t, :], start=True,
                       stop=True).then_inc(s["l2_summed"], 1)
                for h in range(HEADS):
                    pe.wait_ge(s["qk_normed"], L * per["qk_normed"] + 4 + h + 1)
                    pe.wait_ge(s["kv_turned_read"], L * per["kv_turned_read"] + 4 + h - 1)
                    turn(bank[6 + h % 2], gqkv[:, 4 + h, :]).then_inc(s["kv_turned"], 1)
                pe.wait_ge(s["l2_log"], L * per["l2_log"] + 8)
                pe.wait_ge(s["exp_b_ready"], L * per["exp_b_ready"] + 4)
                pe.wait_ge(s["gate_dve_step"], L * per["gate_dve_step"] + 12)
                for h in range(HEADS):
                    e = h % 2
                    if h >= 2:
                        pe.wait_ge(s["g_attn_ready"], L * per["g_attn_ready"] + h - 1)
                    for c in range(NC):
                        o = slice(c * C, (c + 1) * C)
                        mm(bank[2 + e][:, o], gqkv[:, 4 + h, o], gqkv[:, h, o], start=True, stop=True)
                        mm(bank[e][:, o], gqkv[:, 4 + h, o], gqkv[:, 4 + h, o], start=True, stop=True)
                        ins = mm(bank[4 + e][:, o], beta[:, h * NC + c:h * NC + c + 1].broadcast_to([P, C]), ident,
                                 start=True, stop=True)
                    ins.then_inc(s["kk_qk_products"], 1)
                pe.wait_ge(s["g_attn_ready"], L * per["g_attn_ready"] + 4)
                for h in range(HEADS):
                    pe.wait_ge(s["inv_first"], L * per["inv_first"] + h + 1)
                    if h >= 2:
                        pe.wait_ge(s["inv_t_first"], L * per["inv_t_first"] + h - 1)
                    turn(bank[4 + h % 2], R[:, h, :]).then_inc(s["inv_first_turned"], 1)

                def join_p(k):
                    h = k % 4
                    pe.wait_ge(s["g_level"], L * per["g_level"] + k + 1)
                    if k < 4:
                        pe.wait_ge(s["inv_t_first"], L * per["inv_t_first"] + h + 1)
                    else:
                        pe.wait_ge(s["inv_t_updated"], L * per["inv_t_updated"] + k - 3)
                    if k >= 2:
                        pe.wait_ge(s["gt_copied"], L * per["gt_copied"] + k - 1)
                    for c in range(NC):
                        o = slice(c * C, (c + 1) * C)
                        ins = mm(bank[k % 2][:, o], ml_ring[:, k % 2, o], T[:, h, o], start=True, stop=True)
                    ins.then_inc(s["gt_product"], 1)

                def join_tp(k):
                    h = k % 4
                    pe.wait_ge(s["gt_copied"], L * per["gt_copied"] + k + 1)
                    if k >= 4:
                        pe.wait_ge(s["inv_r_updated"], L * per["inv_r_updated"] + k - 3)
                    if k >= 2:
                        pe.wait_ge(s["inv_t_updated"], L * per["inv_t_updated"] + k - 1)
                    for c in range(NC):
                        o = slice(c * C, (c + 1) * C)
                        ins = mm(bank[2 + k % 2][:, o], R[:, h, o], p_ring[:, k % 2, o], start=True, stop=True)
                    ins.then_inc(s["tgt_product"], 1)

                def join_x(k):
                    pe.wait_ge(s["inv_t_updated"], L * per["inv_t_updated"] + k + 1)
                    if k >= 2:
                        pe.wait_ge(s["inv_r_updated"], L * per["inv_r_updated"] + k - 1)
                    else:
                        pe.wait_ge(s["inv_t_first"], L * per["inv_t_first"] + 4)
                    turn(bank[4 + k % 2], T[:, k % 4, :]).then_inc(s["inv_turned"], 1)

                def scores(g):
                    n, h = g // HEADS, g % HEADS
                    if n < len(LEVELS):
                        pe.wait_ge(s["level_qk"], L * per["level_qk"] + n + 1)
                    if g >= 2:
                        pe.wait_ge(s["hg_scores_placed"], L * per["hg_scores_placed"] + g - 1)
                    X = X_ring[n % RING]
                    r = slice(64 * (h % 2), 64 * (h % 2) + 64)
                    for c in range(NC):
                        a = (h // 2) * SEQ + c * C
                        dst = bank[6 + g % 2][:, c * C:(c + 1) * C]
                        if n < len(LEVELS):
                            ins = mm(dst, X[r, a:a + C], X[r, a:a + C], start=True, stop=True)
                        else:
                            ins = mm(dst, hk[r, a:a + C], hq[r, a:a + C], start=True, stop=True)
                    ins.then_inc(s["hg_scores"], 1)

                pe.wait_ge(s["kv_turned_read"], L * per["kv_turned_read"] + 8)
                for k in range(STEPS):
                    if k < JOINS:
                        join_p(k)
                    if 1 <= k < JOINS + 1:
                        join_tp(k - 1)
                    if k >= 2:
                        join_x(k - 2)
                    for g in groups_of(k):
                        scores(g)
                pe.wait_ge(s["hg_scores_placed"], L * per["hg_scores_placed"] + GROUPS)
                for h in range(HEADS):
                    pe.wait_ge(s["inv_r_updated"], L * per["inv_r_updated"] + 20 + h + 1)
                    if h >= 2:
                        pe.wait_ge(s["kcd_ready"], L * per["kcd_ready"] + h - 1)
                    for c in range(NC):
                        o = slice(c * C, (c + 1) * C)
                        ins = mm(bank[6 + h % 2][:, o], k_be[:, h, o], R[:, h, o], start=True, stop=True)
                    ins.then_inc(s["kcd_product"], 1)
                pe.wait_ge(s["gt_copied"], L * per["gt_copied"] + 24)
                pe.wait_ge(s["kcd_ready"], L * per["kcd_ready"] + 4)
                pe.wait_ge(s["inv_t_updated"], L * per["inv_t_updated"] + 24)
                pe.wait_ge(s["q_in_ready"], L * per["q_in_ready"] + 4)
                for c in range(NC):
                    o = slice(c * C, (c + 1) * C)
                    before = S_ring[:, (c - 1) % 2, :]
                    if c:
                        pe.wait_ge(s["state_ready"], L * per["state_ready"] + c)
                    if c >= 2:
                        pe.wait_ge(s["v_new_ready"], L * per["v_new_ready"] + c - 1)
                    for h in range(HEADS):
                        ho = slice(h * P, (h + 1) * P)
                        ins = mm(bank[c % 2][:, ho], R[:, h, o], v_b[:, h, o], start=True, stop=c == 0)
                        if c:
                            ins = mm(bank[c % 2][:, ho], kcd[:, h, o], before[:, ho], start=False, stop=True)
                    ins.then_inc(s["v_new_product"], 1)
                    pe.wait_ge(s["v_new_ready"], L * per["v_new_ready"] + c + 1)
                    if c < NC - 1:
                        if c >= 2:
                            pe.wait_ge(s["state_ready"], L * per["state_ready"] + c - 1)
                        for h in range(HEADS):
                            ho = slice(h * P, (h + 1) * P)
                            ins = mm(bank[6 + c % 2][:, ho], k_out[:, h, o], vn_ring[:, c % 2, ho],
                                     start=True, stop=True)
                        ins.then_inc(s["state_sum"], 1)
                    for h in range(HEADS):
                        ho = slice(h * P, (h + 1) * P)
                        if c:
                            mm(bank[2 + h][:, o], before[:, ho], gqkv[:, h, o], start=True, stop=False)
                        ins = mm(bank[2 + h][:, o], vn_ring[:, c % 2, ho], attn[:, h, o], start=c == 0, stop=True)
                    ins.then_inc(s["delta_out"], 1)

                def sums(first_bank, k_of, v_of, done):
                    for t in range(2):
                        for c in range(NC - 1):
                            o = slice(c * C, (c + 1) * C)
                            ins = mm(bank[first_bank + t][:, c * P:(c + 1) * P], k_of[:, t, o], v_of[:, t, o],
                                     start=True, stop=True)
                        ins.then_inc(done, 1)

                def outputs(first_bank, states, q_of, v_of, p_of, ready, per_ready, done):
                    for t in range(2):
                        pe.wait_ge(ready, L * per_ready + 3 * t + 3)
                        for c in range(NC):
                            o = slice(c * C, (c + 1) * C)
                            if c:
                                mm(bank[first_bank + t][:, o], states[:, t, (c - 1) * P:c * P], q_of(t, o), start=True, stop=False,
                                   skip_group_check=True)
                            for e in range(2):
                                ins = mm(bank[first_bank + t][64 * e:64 * e + 64, o],
                                         v_of[:, t, c * C + 64 * e:c * C + 64 * e + 64],
                                         p_of[:, 2 * t + e, o], start=c == 0, stop=True, skip_group_check=True)
                        ins.then_inc(done, 1)

                pe.wait_ge(s["v_new_ready"], L * per["v_new_ready"] + 4)
                for t in range(4):
                    if t >= 2:
                        pe.wait_ge(s["rot_sin"], L * per["rot_sin"] + t - 1)
                    mm(bank[t % 2][:, :], const("rot"), rqk[:, t, :], start=True, stop=True).then_inc(s["rotated"], 1)
                pe.wait_ge(s["state_ready"], L * per["state_ready"] + 3)
                pe.wait_ge(s["delta_out_copied"], L * per["delta_out_copied"] + 4)
                pe.wait_ge(s["hg_dve_step"], L * per["hg_dve_step"] + 14)
                for t in range(4):
                    turn(bank[4 + t], hk_out[:, t * SEQ:(t + 1) * SEQ] if t < 2 else
                         hv[:, (t - 2) * SEQ:(t - 1) * SEQ]).then_inc(s["hg_turned"], 1)
                for h in range(HEADS):
                    pe.wait_ge(s["rot_done"], L * per["rot_done"] + 3 + h // 2)
                    if h >= 2:
                        pe.wait_ge(s["ret_decayed"], L * per["ret_decayed"] + h - 1)
                    r = slice(64 * (h % 2), 64 * (h % 2) + 64)
                    for c in range(NC):
                        o = slice(c * C, (c + 1) * C)
                        ins = mm(bank[2 + h % 2][:, o], rk[r, h // 2, o], rq[r, h // 2, o], start=True, stop=True)
                    ins.then_inc(s["ret_scores"], 1)
                pe.wait_ge(s["hg_turned_copied"], L * per["hg_turned_copied"] + 4)
                for t in range(4):
                    turn(bank[4 + t], (rk if t < 2 else rv)[:, t % 2, :]).then_inc(s["ret_turned"], 1)
                sums(0, hk_tok, hv_tok, s["hg_sums"])
                pe.wait_ge(s["ret_k_out"], L * per["ret_k_out"] + 2)
                pe.wait_ge(s["ret_v_copied"], L * per["ret_v_copied"] + 2)
                sums(4, k_tok, v_tok, s["ret_sums"])
                pe.wait_ge(s["hg_q_in"], L * per["hg_q_in"] + 1)
                outputs(6, hSU, lambda t, o: hq_in[:, t * SEQ + o.start:t * SEQ + o.stop], hv_tok, hPT,
                        s["hg_states"], per["hg_states"], s["hg_out"])
                pe.wait_ge(s["ret_decayed"], L * per["ret_decayed"] + 4)
                pe.wait_ge(s["ret_q_in"], L * per["ret_q_in"] + 2)
                outputs(2, SU, lambda t, o: rq[:, t, o], v_tok, PT, s["ret_states"], per["ret_states"], s["ret_out"])

                for t in range(8):
                    pe.wait_ge(s["out_squared"], L * per["out_squared"] + t + 1)
                    if t >= 2:
                        pe.wait_ge(s["out_log"], L * per["out_log"] + t - 1)
                    mm(bank[t % 2][:, :], const("mean64" if t < 4 else "mean128"), area_a[:, t, :], start=True,
                       stop=True).then_inc(s["out_mean_square"], 1)

                pe.wait_ge(s["out_log"], L * per["out_log"] + 8)
                for u in range(2):
                    pe.wait_ge(s["mix_lo_ready"], L * per["mix_lo_ready"] + u + 1)
                    rows(L, OUT0 + u, u, h_hi[:, u, :], h_lo[:, u, :], u == 0, False)
                pe.wait_ge(s["mix_lo_ready"], L * per["mix_lo_ready"] + 8)
                apart(pe)
                with pe.Fori(1, OUT_UNITS // 2 - 1) as i:
                    for u in range(2):
                        rows(L, OUT0 + 2 * i + u, u, h_hi[:, bass.ds(2 * i + u, 1), :],
                             h_lo[:, bass.ds(2 * i + u, 1), :], False, False)
                rows(L, OUT0 + 6, 0, h_hi[:, 6, :], h_lo[:, 6, :], False, False)
                rows(L, OUT0 + 7, 1, h_hi[:, 7, :], h_lo[:, 7, :], False, True, s["out_projected"])

                pe.wait_ge(s["x_after_mixer"], L * per["x_after_mixer"] + 8)
                norm(L, 1)

                unit(L, UP0, 0, normed_before=8)
                unit(L, UP0 + 1, 1)
                with pe.Fori(1, FT) as i:
                    for u in range(2):
                        pe.wait_ge(s["ffn_conv_done"], L * per["ffn_conv_done"] + 2 * i + u - 1)
                        unit(L, UP0 + 2 * i + u, u)

                pe.wait_ge(s["g_lo_ready"], L * per["g_lo_ready"] + 2)
                for u in range(2):
                    rows(L, DOWN0 + u, u, g_hi[:, u, :], g_lo[:, u, :], u == 0, False, over_up=u == 0)
                pe.wait_ge(s["g_lo_ready"], L * per["g_lo_ready"] + FT)
                apart(pe)
                with pe.Fori(1, DOWN_UNITS // 2 - 1) as i:
                    for u in range(2):
                        rows(L, DOWN0 + 2 * i + u, u, g_hi[:, bass.ds(2 * i + u, 1), :],
                             g_lo[:, bass.ds(2 * i + u, 1), :], False, False)
                rows(L, DOWN0 + 20, 0, g_hi[:, 20, :], g_lo[:, 20, :], False, False)
                rows(L, DOWN0 + 21, 1, g_hi[:, 21, :], g_lo[:, 21, :], False, True, s["down_projected"])
            norm(DEPTH, 0)


def constants():
    f8 = np.float64
    i = np.arange(C)
    col = np.zeros((P, N_CONST), np.float32)

    def put(name, a):
        at, n = CONSTS[name]
        col[:, at:at + n] = np.asarray(a, f8).reshape(P, n)

    put("ident", np.eye(C))
    put("mean_model", np.full((P, P), 1.0 / D_MODEL))
    put("ones", np.ones((P, P)))
    block = np.kron(np.eye(2), np.ones((64, 64)))
    put("blocks", block)
    put("mean64", block / 64)
    put("mean128", np.full((P, P), 1.0 / P))
    put("causal", i[:, None] <= i[None, :])
    put("lvl", np.stack([(j0 % 2 == 0) & (i0 == j0 + 1) for half in LEVELS
                         for j0, i0 in [(i[:, None] // half, i[None, :] // half)]], 1))
    log_gamma = np.log1p(-np.exp2(-5.0 - np.arange(HEADS)))
    rel = i[None, :] - i[:, None]
    scale = 64.0 ** -0.5
    put("ret_decay", np.stack([np.where(rel >= 0, np.exp(np.maximum(rel, 0) * lg), 0.0) * scale
                               for lg in log_gamma], 1))
    head = 2 * np.arange(2)[None, :] + (np.arange(P) // 64)[:, None]
    put("ret_q", np.exp((i + 1.0)[None, None, :] * log_gamma[head][:, :, None]))
    head_row = 2 * np.arange(2)[:, None] + (np.arange(P) // 64)[None, :]
    put("ret_k", np.exp((C - 1.0 - i)[:, None, None] * log_gamma[head_row][None]) * scale)
    put("ret_w", np.exp(C * log_gamma[head]))
    rot = np.zeros((P, P))
    for m in range(P):
        if m % 64 < 32:
            rot[m + 32, m] = -1.0
        else:
            rot[m - 32, m] = 1.0
    put("rot", rot)
    half = np.float32(32)
    inv = np.float32(10000.0) ** (-np.arange(32, dtype=np.float32) / half)
    put("inv_freq", np.tile(inv, 4)[:, None])
    return col


def kernel(**inputs):
    import concourse.bacc as bacc
    from concourse.bass_utils import run_bass_kernel_spmd

    a = {k: np.asarray(v) for k, v in inputs.items()}

    def tiles(v):
        return v.reshape(-1, P).T

    starts = ([1280, 1408, 1536, 1664] + [P * j for j in range(6)]
              + [2048 + P * j for j in range(12)]
              + [768, 896, 1792, 1920] + [3592 + P * j for j in range(4)] + [1024, 1152])
    ups = [o for j in range(FT) for o in (P * j, D_FF + P * j)]
    units, params = [], []
    for layer in range(DEPTH):
        w_in, w_up = a["w_in"][layer], a["w_up"][layer]
        for w, cols in ((w_in, starts), (w_up, ups)):
            blocks = [w[:, o:o + P].reshape(KT, P, P).transpose(1, 0, 2).reshape(P, KT * P) for o in cols]
            units += blocks
            if w is w_in:
                units += list(a["w_out"][layer].reshape(KT, P, D_MODEL))
        units += list(a["w_down"][layer].reshape(FT, P, D_MODEL))
        ab = w_in[:, 3584:3592].reshape(KT, P, 8).transpose(1, 0, 2).reshape(P, KT * 8)
        gconv = a["gdn_conv_w"][layer].T.reshape(12, P, 4).transpose(1, 0, 2).reshape(P, 48)
        fconv = a["ffn_conv_w"][layer].T.reshape(2, FT, P, 3).transpose(2, 1, 0, 3).reshape(P, -1)
        fbias = a["ffn_conv_b"][layer].reshape(2, FT, P).transpose(2, 1, 0).reshape(P, -1)
        ones = np.ones((P, 2), np.float32)
        hgn = np.tile(a["hg_norm_w"][layer], 2)[:, None]
        gdn = a["gdn_norm_w"][layer][:, None]
        wide = [np.broadcast_to(a[k][layer][None, :], (P, HEADS)) for k in ("gdn_A_log", "gdn_dt_bias")]
        params.append(np.concatenate([tiles(a["norm1_w"][layer]), tiles(a["norm2_w"][layer]), gconv, fconv, fbias,
                                      ones, hgn, hgn, gdn, gdn, gdn, gdn, *wide, ab], axis=1))
    arrays = {
        "x_t": a["x"][0].T.reshape(KT, P, SEQ).transpose(1, 0, 2),
        "positions": np.broadcast_to(a["positions"][0][None, :], (P, SEQ)),
        "constants": constants(),
        "params": np.stack(params, axis=1),
        "lb_logits": a["hg_lb_logits"].reshape(DEPTH, 2, P).transpose(2, 0, 1),
        "final_norm": tiles(a["final_norm_w"]),
        "weights": np.stack(units),
    }
    arrays = {k: np.ascontiguousarray(v) for k, v in arrays.items()}
    nc = bacc.Bacc("TRN2", target_bir_lowering=False, num_devices=1)
    args = [nc.dram_tensor(k, v.shape, mybir.dt.from_np(v.dtype), kind="ExternalInput").ap()
            for k, v in arrays.items()]
    args.append(nc.dram_tensor("out_t", (P, KT, SEQ), F32, kind="ExternalOutput").ap())
    build(nc, *args)
    r = run_bass_kernel_spmd(nc, [arrays], core_ids=[0])
    return r.results[0]["out_t"].transpose(2, 1, 0).reshape(1, SEQ, D_MODEL)
```

```python
from contextlib import ExitStack

import numpy as np

import concourse.bass as bass
from concourse import mybir

F32 = mybir.dt.float32
F32R = mybir.dt.float32r
I32 = mybir.dt.int32
ACT = mybir.ActivationFunctionType
ALU = mybir.AluOpType

P = 128
D_MODEL = 1024
SEQ = 512
DEPTH = 2
C = 128
NC = SEQ // C
KT = D_MODEL // P
HEADS = 4
D_FF = 2816
FT = D_FF // P
EPS = 1e-6

COPY_UNITS, CONV_UNITS, GATE_UNITS = 10, 12, 10
IN_UNITS = COPY_UNITS + CONV_UNITS + GATE_UNITS
OUT_UNITS = KT
UP_UNITS = 2 * FT
DOWN_UNITS = FT
UNITS = IN_UNITS + OUT_UNITS + UP_UNITS + DOWN_UNITS
CONV0, GATE0 = COPY_UNITS, COPY_UNITS + CONV_UNITS
OUT0, UP0, DOWN0 = IN_UNITS, IN_UNITS + OUT_UNITS, IN_UNITS + OUT_UNITS + UP_UNITS

LEVELS = [1, 2, 4, 8, 16, 32, 64]

JOINS = 4 * (len(LEVELS) - 1)
STEPS = JOINS + 2
GROUPS = HEADS * (len(LEVELS) + 1)
RING = 4


def groups_of(step):
    first = HEADS
    return range(*(GROUPS * max(k - first, 0) // (STEPS - first) for k in (step, step + 1)))


FIRST_STEP = [k for n in range(len(LEVELS)) for k in range(STEPS) if HEADS * n in groups_of(k)]
LEVEL_AFTER = {FIRST_STEP[n - RING + 1]: n for n in range(RING, len(LEVELS))}

CONSTS = {}
_at = 0
for _name, _n in (("ident", C), ("mean_model", P), ("ones", P), ("mean64", P), ("mean128", P), ("causal", C),
                  ("lvl", len(LEVELS) * C), ("ret_decay", HEADS * C), ("ret_q", 2 * C), ("ret_k", 2 * P),
                  ("blocks", P), ("rot", P), ("ret_w", 2), ("inv_freq", 1)):
    CONSTS[_name] = (_at, _n)
    _at += _n
N_CONST = _at
PARAMS = {}
_at = 0
for _name, _n in (("norm1", KT), ("norm2", KT), ("gdn_conv", CONV_UNITS * 4), ("ffn_conv", UP_UNITS * 3),
                  ("ffn_bias", UP_UNITS), ("onorm", KT), ("a_log", HEADS), ("dt_bias", HEADS), ("w_ab", KT * 8)):
    PARAMS[_name] = (_at, _n)
    _at += _n
N_PARAM = _at

PER_LAYER = dict(
    x_after_mixer=8, x_after_ffn=8, x_squared=16, squares_paired=8, x_mean_square=2, rstd_log=2, rstd_ready=2,
    x_normed=16, h_hi_ready=16, h_lo_even_ready=8, h_lo_odd_ready=8, params_copied=1, wab_hi_ready=1,
    wab_lo_ready=1, ab_projected=1, ab_copied=1, ab_turned=1, ab_hi_copied=1, gate_dve_step=14, gate_act_step=8,
    b_token_major=1, b_spread=4, b_diff_ready=4, exp_b_ready=4, decay_exp=4, decay_masked=4, hi_ready=UNITS,
    lo_ready=UNITS, unit_used=UNITS, conv_last_tap=12, conv_mid_taps=24, conv_done=12, qkv_silu=12,
    bank_copied=20, kv_turned=8, kv_turned_read=8, k_turned_again=4, k_out_ready=4, l2_squared=8, l2_summed=8,
    l2_copied=8, l2_log=8, l2_rnorm=8, qk_normed=8, beta_spread=4, beta_decay_ready=4, kk_qk_products=4,
    kk_decayed=4, g_attn_ready=4, q_in_ready=4, g_smallest=4, inv_even_columns=4, inv_first=4,
    inv_first_turned=4, inv_t_first=4, g_level=24, gt_product=24, gt_copied=24, tgt_product=24,
    inv_t_updated=24, inv_turned=24, inv_r_updated=24, kcd_product=4, kcd_ready=4, v_new_product=4,
    v_new_ready=4, state_sum=3, delta_out=4, state_ready=3, delta_out_copied=4, rotated=4, rot_sin=4, rot_cos=4,
    rot_done=4, ret_scores=4, ret_decayed=4, ret_q_in=2, ret_turned=4, ret_k_out=2, ret_v_copied=2, ret_sums=2,
    ret_states=6, ret_out=2, ret_out_copied=2, hg_dve_step=14, hg_act_step=8, hg_scores_cleared=1, hg_q_in=1,
    level_diff=7, level_exp=7, level_qk=7, hg_scores=32, hg_scores_placed=32, hg_turned=4, hg_turned_copied=4,
    hg_sums=2, hg_states=6, hg_out=2, hg_out_copied=2, out_squared=8, out_mean_square=8, out_log=8, out_rstd=8,
    out_normed=8, out_gated=8, mix_hi_ready=8, mix_lo_ready=8, out_projected=7, ffn_last_tap=UP_UNITS,
    ffn_mid_tap=UP_UNITS, ffn_conv_done=UP_UNITS, ffn_silu=FT, ffn_product=FT, g_hi_ready=FT, g_lo_ready=FT,
    down_projected=7,
)


def build(nc, x_in, pos_in, const_in, par_in, lb_in, fin_in, w_in, out):
    ctx = ExitStack()
    with ctx:
        def sb(name, shape, dt=F32, where=ctx):
            return where.enter_context(nc.sbuf_tensor(name, shape, dt))

        s = {name: ctx.enter_context(nc.semaphore(name)) for name in PER_LAYER}
        per = PER_LAYER
        setup_loaded = ctx.enter_context(nc.semaphore("setup_loaded"))
        x_loaded = ctx.enter_context(nc.semaphore("x_loaded"))
        loaded = ctx.enter_context(nc.semaphore("loaded"))
        raw_loaded = [ctx.enter_context(nc.semaphore(f"raw_loaded{i}")) for i in range(2)]
        setup_dve = ctx.enter_context(nc.semaphore("setup_dve"))
        SETUP_ANGLES, SETUP_LB = 16, 18
        setup_act = ctx.enter_context(nc.semaphore("setup_act"))
        stored = ctx.enter_context(nc.semaphore("stored"))
        carrier = ctx.enter_context(nc.semaphore("carrier"))

        def apart(eng):
            eng.sem_inc(carrier)

        cst = sb("cst", [P, N_CONST])
        par = sb("par", [P, DEPTH, N_PARAM])
        cur = sb("cur", [P, N_PARAM])
        lb = sb("lb", [P, DEPTH, 4])
        lb_cur = sb("lb_cur", [P, 4])
        fin = sb("fin", [P, KT])
        sin_t = sb("sin_t", [P, SEQ])
        cos_t = sb("cos_t", [P, SEQ])
        x = sb("x", [P, KT, SEQ])
        rstd = sb("rstd", [P, SEQ])
        with ExitStack() as normed_mem:
            h_hi = sb("h_hi", [P, KT, SEQ], F32R, normed_mem)
            h_lo = sb("h_lo", [P, KT, SEQ], F32R, normed_mem)
        between = sb("between", [P, 2 * KT, SEQ])
        raw = sb("raw", [P, 2, KT * P])
        w_hi = sb("w_hi", [P, 2, KT * P], F32R)
        w_lo = sb("w_lo", [P, 2, KT * P], F32R)
        wab = sb("wab", [P, KT, 16], F32R)
        small = sb("small", [P, 16, 16])
        abc = sb("abc", [P, NC, 8])
        lbw = sb("lbw", [P, 8])
        bank = [ctx.enter_context(nc.psum_tensor(f"bank{i}", [P, 512], F32)) for i in range(8)]

        with ExitStack() as mixer_mem:
            gqkv = sb("gqkv", [P, 12, SEQ], F32, mixer_mem)
            gate = sb("gate", [P, GATE_UNITS, SEQ], F32, mixer_mem)
            cp = sb("cp", [P, COPY_UNITS, SEQ], F32, mixer_mem)
            area_a = sb("area_a", [P, 12, SEQ], F32, mixer_mem)
            area_b = sb("area_b", [P, 12, SEQ], F32, mixer_mem)
        with ExitStack() as ffn_mem:
            g_hi = sb("g_hi", [P, FT, SEQ], F32R, ffn_mem)
            g_lo = sb("g_lo", [P, FT, SEQ], F32R, ffn_mem)
            cg = sb("cg", [P, SEQ], F32, ffn_mem)
            cv = sb("cv", [P, SEQ], F32, ffn_mem)
            gt = sb("gt", [P, SEQ], F32, ffn_mem)

        def const(name, i=0, n=None):
            a, _n = CONSTS[name]
            n = _n if n is None else n
            return cst[:, a + i * n:a + (i + 1) * n]

        def param(name, i=0, n=1):
            a, _ = PARAMS[name]
            return cur[:, bass.ds(a + i * n, n)] if not isinstance(i, int) else cur[:, a + i * n:a + (i + 1) * n]

        def chunks(ap):
            return ap.rearrange("p (c i) -> p c i", c=NC)

        def per_chunk(ap):
            return ap.unsqueeze(1).broadcast_to([P, NC, C])

        def even_blocks(ap, half):
            return ap.rearrange("p (g s) -> p g s", s=2 * half)[:, :, 0:half]

        def columns(ap, odd):
            return ap.rearrange("p c (i two) -> p c i two", two=2)[:, :, :, odd:odd + 1]

        def per_token(ap):
            return ap.unsqueeze(2).broadcast_to([P, ap.shape[1], C])

        LO, HI = slice(0, C // 2), slice(C // 2, C)
        ident, causal = const("ident"), const("causal")
        k_out, k_be = (area_a[:, 4 * i:4 * i + 4, :] for i in range(2))
        v_b = between[:, 8:12, :]
        T, R, attn = (area_b[:, 4 * i:4 * i + 4, :] for i in range(3))
        decay, e_b, kcd = T, R, T
        beta_decay = attn
        G = k_out
        ab_rows = gate[0:16, 9, :]
        ml_ring, p_ring = gqkv[:, 8:10, :], gqkv[:, 10:12, :]
        vn_ring, S_ring = ml_ring, p_ring
        oT = gqkv[:, 0:8, :]
        scratch = between[:, 0:2, :]
        hz, hv = (cp[:, 2 * i:2 * i + 2, :].rearrange("p t n -> p (t n)") for i in range(2))
        rq, rk, rv = (cp[:, 4 + 2 * i:6 + 2 * i, :] for i in range(3))
        rqk = cp[:, 4:8, :]
        PT = area_a[:, 0:4, :]
        k_tok, v_tok = area_a[:, 4:6, :], area_b[:, 6:8, :]
        SU = area_b[:, 8:10, :]
        hE, hs, hl, hf, hg = (gqkv[:, 2 * i:2 * i + 2, :].rearrange("p t n -> p (t n)") for i in range(5))
        hb, hk = (area_a[:, 8 + 2 * i:10 + 2 * i, :].rearrange("p t n -> p (t n)") for i in range(2))
        hq = gate[:, 8:10, :].rearrange("p t n -> p (t n)")
        X_ring = [between[:, 2 * i:2 * i + 2, :].rearrange("p t n -> p (t n)") for i in range(RING)]
        hk_out, hq_in = X_ring[2], X_ring[3]
        hPT = between[:, 12:16, :]
        sq_ring = area_a[:, 6:10, :]
        rs_ring = [area_a[:, 10, :], area_a[:, 11, :], gqkv[:, 10, :], gqkv[:, 11, :]]
        hk_tok, hv_tok, hSU = (area_b[:, 2 * i:2 * i + 2, :] for i in range(3))
        angles = [area_b[:, i, :] for i in range(7)]

        za, sp, g_tok, nb, beta, btok, bl, dko, e_tok, ko, w_dec, be, hbl, hw, e_a, abt = (
            small[:, i, :] for i in range(16))

        def hc(ap):
            return ap.rearrange("p (h c) -> p h c", h=HEADS)

        block = ctx.enter_context(nc.Block())

        @block.sync
        def _(sp_):
            freq = CONSTS["ret_w"][0]
            for dst, src in ((angles[0].bitcast(I32), pos_in), (cst[:, freq:], const_in[:, freq:]),
                             (lb[:, :, 0:2], lb_in)):
                sp_.dma_start(dst, src).then_inc(setup_loaded, 16)
            for k in range(KT):
                sp_.dma_start(x[:, k, :], x_in[:, k, :]).then_inc(x_loaded, 16)
            for dst, src in ((par[:, :, :], par_in), (fin[:, :], fin_in), (cst[:, :freq], const_in[:, :freq])):
                sp_.dma_start(dst, src).then_inc(loaded, 16)
            for u in range(2):
                sp_.dma_start(raw[:, u, :], w_in[u]).then_inc(raw_loaded[u], 16)
            with sp_.Fori(1, DEPTH * UNITS // 2) as q:
                for u in range(2):
                    sp_.wait_ge(s["lo_ready"], 2 * q + u - 1)
                    sp_.dma_start(raw[:, u, :], w_in[2 * q + u]).then_inc(raw_loaded[u], 16)
            for k in range(KT):
                sp_.wait_ge(s["x_normed"], DEPTH * 16 + k + 1)
                sp_.dma_start(out[:, k, :], gqkv[:, k, :]).then_inc(stored, 16)
            sp_.wait_ge(stored, 16 * KT)

        @block.gpsimd
        def _(pool):
            tt = nc.gpsimd.tensor_tensor

            def pair_squares(L, which):
                for k in range(0, KT, 2):
                    pool.wait_ge(s["x_squared"], L * per["x_squared"] + 8 * which + k + 2)
                    tt(gqkv[:, k, :], gqkv[:, k, :], gqkv[:, k + 1, :], ALU.add).then_inc(s["squares_paired"], 1)

            def norm_lo(L, which):
                for k in range(1, KT, 2):
                    pool.wait_ge(s["h_hi_ready"], L * per["h_hi_ready"] + 8 * which + k + 1)
                    tt(h_lo[:, k, :], gqkv[:, k, :], h_hi[:, k, :].bitcast(F32),
                       ALU.subtract).then_inc(s["h_lo_odd_ready"], 1)

            with pool.Fori(0, DEPTH) as L:
                pair_squares(L, 0)
                norm_lo(L, 0)
                for h in range(HEADS):
                    pool.wait_ge(s["decay_exp"], L * per["decay_exp"] + h + 1)
                    tt(chunks(decay[:, h, :]), chunks(decay[:, h, :]), per_chunk(causal),
                       ALU.mult).then_inc(s["decay_masked"], 1)
                def level_diff(n):
                    half = LEVELS[n]
                    X = X_ring[n % RING].rearrange("p (g s) -> p g s", s=2 * half)
                    b = hb.rearrange("p (g s) -> p g s", s=2 * half)
                    ref = b[:, :, half - 1:half].broadcast_to([P, 2 * SEQ // (2 * half), half])
                    if n >= RING:
                        pool.wait_ge(s["hg_scores"], L * per["hg_scores"] + 4 * (n - RING + 1))
                    tt(X[:, :, 0:half], ref, b[:, :, 0:half], ALU.subtract)
                    tt(X[:, :, half:], b[:, :, half:], ref, ALU.subtract).then_inc(s["level_diff"], 1)

                pool.wait_ge(s["hg_dve_step"], L * per["hg_dve_step"] + 12)
                pool.wait_ge(s["unit_used"], L * per["unit_used"] + IN_UNITS)
                level_diff(0)
                for h in range(HEADS):
                    pool.wait_ge(s["kk_qk_products"], L * per["kk_qk_products"] + h + 1)
                    pool.wait_ge(s["exp_b_ready"], L * per["exp_b_ready"] + h + 1)
                    tt(gqkv[:, h, :], gqkv[:, h, :], e_b[:, h, :], ALU.mult).then_inc(s["q_in_ready"], 1)
                    R3, G3 = chunks(R[:, h, :]), chunks(G[:, h, :])
                    one, smallest = per_chunk(ident), per_chunk(const("lvl", 0, C))
                    pool.wait_ge(s["g_attn_ready"], L * per["g_attn_ready"] + h + 1)
                    pool.wait_ge(s["q_in_ready"], L * per["q_in_ready"] + h + 1)
                    tt(columns(R3, 1), columns(G3, 1), columns(smallest, 1), ALU.mult).then_inc(s["g_smallest"], 1)
                    pool.wait_ge(s["g_smallest"], L * per["g_smallest"] + h + 1)
                    tt(columns(R3, 1), columns(one, 1), columns(R3, 1), ALU.subtract).then_inc(s["inv_first"], 1)
                for k in range(JOINS):
                    if k >= 2:
                        pool.wait_ge(s["gt_product"], L * per["gt_product"] + k - 1)
                    else:
                        pool.wait_ge(s["kv_turned"], L * per["kv_turned"] + 4)
                    tt(chunks(ml_ring[:, k % 2, :]), chunks(G[:, k % 4, :]), per_chunk(const("lvl", 1 + k // 4, C)),
                       ALU.mult).then_inc(s["g_level"], 1)
                    if k in (1, 3, 5):
                        level_diff(k // 2 + 1)
                    if k == 2:
                        nc.gpsimd.memset(hPT, 0.0).then_inc(s["hg_scores_cleared"], 1)
                    if k - 1 in LEVEL_AFTER:
                        level_diff(LEVEL_AFTER[k - 1])
                pool.wait_ge(s["hg_act_step"], L * per["hg_act_step"] + 7)
                tt(hq_in, hq_in, hq, ALU.mult).then_inc(s["hg_q_in"], 1)
                for t in range(4):
                    pool.wait_ge(s["rotated"], L * per["rotated"] + t + 1)
                    tt(rqk[:, t, :], rqk[:, t, :], cos_t[:, :], ALU.mult).then_inc(s["rot_cos"], 1)
                for t in range(2):
                    pool.wait_ge(s["ret_scores"], L * per["ret_scores"] + 2 * t + 2)
                    tt(chunks(rq[:, t, :]), chunks(rq[:, t, :]), per_chunk(const("ret_q", t, C)),
                       ALU.mult).then_inc(s["ret_q_in"], 1)
                for t in range(8):
                    pool.wait_ge(s["mix_hi_ready"], L * per["mix_hi_ready"] + t + 1)
                    tt(h_lo[:, t, :], oT[:, t, :], h_hi[:, t, :].bitcast(F32),
                       ALU.subtract).then_inc(s["mix_lo_ready"], 1)
                pair_squares(L, 1)
                norm_lo(L, 1)
            pair_squares(DEPTH, 0)

        @block.scalar
        def _(act):
            A = nc.scalar.activation

            def split_hi(q, u):
                act.wait_ge(raw_loaded[u], 16 * q + 16)
                A(w_hi[:, u, :], raw[:, u, :], ACT.Copy).then_inc(s["hi_ready"], 1)

            def norm(L, which, meanwhile=None):
                nc.scalar.preload_act_table_set("natural_log_exp_and_others")
                for k in range(KT):
                    if which == 0:
                        act.wait_ge(s["x_after_ffn"], L * per["x_after_ffn"] + k + 1)
                    else:
                        act.wait_ge(s["x_after_mixer"], L * per["x_after_mixer"] + k + 1)
                    A(gqkv[:, k, :], x[:, k, :], ACT.Square).then_inc(s["x_squared"], 1)
                if meanwhile:
                    meanwhile()
                act.wait_ge(s["x_mean_square"], L * per["x_mean_square"] + which + 1)
                A(rstd[:, :], bank[2][:, :], ACT.Ln, bias=EPS).then_inc(s["rstd_log"], 1)
                act.wait_ge(s["rstd_log"], L * per["rstd_log"] + which + 1)
                A(rstd[:, :], rstd[:, :], ACT.Exp, scale=-0.5).then_inc(s["rstd_ready"], 1)

            def norm_hi(L, which):
                for k in range(KT):
                    act.wait_ge(s["x_normed"], L * per["x_normed"] + 8 * which + k + 1)
                    A(h_hi[:, k, :], gqkv[:, k, :], ACT.Copy).then_inc(s["h_hi_ready"], 1)

            act.wait_ge(setup_dve, SETUP_ANGLES)
            A(sin_t[:, :], sin_t[:, :], ACT.Sin).then_inc(setup_act, 1)
            A(cos_t[:, :], cos_t[:, :], ACT.Sin).then_inc(setup_act, 1)
            nc.scalar.preload_act_table_set("natural_log_exp_and_others")
            act.wait_ge(setup_dve, SETUP_LB)
            A(lbw[:, 0:4], lbw[:, 0:4], ACT.Exp).then_inc(setup_act, 1)

            with act.Fori(0, DEPTH) as L:
                def split_first():
                    for u in range(2):
                        split_hi(L * (UNITS // 2), u)
                    act.wait_ge(s["params_copied"], L * per["params_copied"] + 1)
                    A(wab[:, :, 0:8], param("w_ab", 0, KT * 8).rearrange("p (k n) -> p k n", k=KT),
                      ACT.Copy).then_inc(s["wab_hi_ready"], 1)

                norm(L, 0, split_first)
                norm_hi(L, 0)

                q0 = L * (UNITS // 2)

                def copy_unit(i, u):
                    act.wait_ge(s["unit_used"], L * per["unit_used"] + 2 * i + u + 1)
                    split_hi(q0 + i + 1, u)
                    A(cp[:, 2 * i + u, :], bank[u][:, :], ACT.Copy).then_inc(s["bank_copied"], 1)

                def spread_exps(h):
                    act.wait_ge(s["b_diff_ready"], L * per["b_diff_ready"] + h + 1)
                    A(e_b[:, h, :], bank[2 + h][:, :], ACT.Exp).then_inc(s["exp_b_ready"], 1)
                    A(decay[:, h, :], decay[:, h, :], ACT.Exp).then_inc(s["decay_exp"], 1)

                copy_unit(0, 0)
                copy_unit(0, 1)
                act.wait_ge(s["gate_dve_step"], L * per["gate_dve_step"] + 2)
                A(sp, za, ACT.Abs).then_inc(s["gate_act_step"], 1)
                act.wait_ge(s["gate_act_step"], L * per["gate_act_step"] + 1)
                A(sp, sp, ACT.Exp, scale=-1.0).then_inc(s["gate_act_step"], 1)
                act.wait_ge(s["gate_act_step"], L * per["gate_act_step"] + 2)
                A(sp, sp, ACT.Ln, bias=1.0).then_inc(s["gate_act_step"], 1)
                A(e_a[:, 0:4], param("a_log", 0, 4), ACT.Exp).then_inc(s["gate_act_step"], 1)
                act.wait_ge(s["gate_dve_step"], L * per["gate_dve_step"] + 3)
                A(nb, nb, ACT.Exp).then_inc(s["gate_act_step"], 1)
                copy_unit(1, 0)
                act.wait_ge(s["gate_dve_step"], L * per["gate_dve_step"] + 8)
                A(e_tok, btok, ACT.Exp).then_inc(s["gate_act_step"], 1)
                spread_exps(0)
                spread_exps(1)
                copy_unit(1, 1)
                spread_exps(2)
                spread_exps(3)
                act.wait_ge(s["gate_dve_step"], L * per["gate_dve_step"] + 13)
                A(ko, dko, ACT.Exp).then_inc(s["gate_act_step"], 1)
                A(w_dec, bl, ACT.Exp).then_inc(s["gate_act_step"], 1)
                copy_unit(2, 0)
                act.wait_ge(s["hg_dve_step"], L * per["hg_dve_step"] + 1)
                A(hE, hE, ACT.Exp).then_inc(s["hg_act_step"], 1)
                act.wait_ge(s["hg_act_step"], L * per["hg_act_step"] + 1)
                A(hl, hE, ACT.Ln, bias=1.0).then_inc(s["hg_act_step"], 1)
                copy_unit(2, 1)
                act.wait_ge(s["hg_dve_step"], L * per["hg_dve_step"] + 3)
                A(hf, hs, ACT.Exp, scale=-1.0).then_inc(s["hg_act_step"], 1)
                copy_unit(3, 0)
                act.wait_ge(s["hg_dve_step"], L * per["hg_dve_step"] + 6)
                A(hk, hk, ACT.Exp).then_inc(s["hg_act_step"], 1)
                copy_unit(3, 1)
                act.wait_ge(s["hg_dve_step"], L * per["hg_dve_step"] + 9)
                A(hf, hf, ACT.Ln).then_inc(s["hg_act_step"], 1)
                copy_unit(4, 0)
                copy_unit(4, 1)

                nc.scalar.preload_act_table_set("silu_and_others")
                act.wait_ge(s["hg_dve_step"], L * per["hg_dve_step"] + 12)
                with act.Fori(0, CONV_UNITS // 2) as i:
                    for u in range(2):
                        act.wait_ge(s["unit_used"], L * per["unit_used"] + CONV0 + 2 * i + u + 1)
                        apart(act)
                        A(gqkv[:, 2 * i + u, :], bank[u][:, :], ACT.Copy,
                          scale=param("gdn_conv", (2 * i + u) * 4 + 3)).then_inc(s["conv_last_tap"], 1)
                        split_hi(q0 + CONV0 // 2 + i + 1, u)
                        act.wait_ge(s["conv_done"], L * per["conv_done"] + 2 * i + u + 1)
                        apart(act)
                        A(gqkv[:, 2 * i + u, :], gqkv[:, 2 * i + u, :], ACT.Silu).then_inc(s["qkv_silu"], 1)
                with act.Fori(0, 4) as i:
                    for u in range(2):
                        act.wait_ge(s["unit_used"], L * per["unit_used"] + GATE0 + 2 * i + u + 1)
                        split_hi(q0 + GATE0 // 2 + i + 1, u)
                        A(gate[:, 2 * i + u, :], bank[u][:, :], ACT.Silu).then_inc(s["bank_copied"], 1)
                        act.wait_ge(s["qkv_silu"], L * per["qkv_silu"] + 2 * i + u + 1)
                        apart(act)
                        A(area_a[:, bass.ds(2 * i + u, 1), :], gqkv[:, bass.ds(2 * i + u, 1), :],
                          ACT.Square).then_inc(s["l2_squared"], 1)

                def l2_rnorm(h):
                    for t in (h, 4 + h):
                        A(area_a[:, t, :], area_a[:, t, :], ACT.Ln, bias=EPS).then_inc(s["l2_log"], 1)
                    for n, t in enumerate((h, 4 + h)):
                        act.wait_ge(s["l2_log"], L * per["l2_log"] + 2 * h + n + 1)
                        A(area_a[:, t, :], area_a[:, t, :], ACT.Exp, scale=-0.5).then_inc(s["l2_rnorm"], 1)

                for u in range(2):
                    if u:
                        nc.scalar.preload_act_table_set("natural_log_exp_and_others")
                        act.wait_ge(s["l2_copied"], L * per["l2_copied"] + 8)
                        l2_rnorm(0)
                        l2_rnorm(1)
                        nc.scalar.preload_act_table_set("silu_and_others")
                    act.wait_ge(s["unit_used"], L * per["unit_used"] + GATE0 + 8 + u + 1)
                    split_hi(q0 + GATE0 // 2 + 5, u)
                    A(gate[:, 8 + u, :], bank[u][:, :], ACT.Silu).then_inc(s["bank_copied"], 1)

                nc.scalar.preload_act_table_set("natural_log_exp_and_others")
                def level_exp(n):
                    act.wait_ge(s["level_diff"], L * per["level_diff"] + n + 1)
                    A(X_ring[n % RING], X_ring[n % RING], ACT.Exp).then_inc(s["level_exp"], 1)

                l2_rnorm(2)
                l2_rnorm(3)
                level_exp(0)
                for h in range(HEADS):
                    act.wait_ge(s["q_in_ready"], L * per["q_in_ready"] + h + 1)
                    A(columns(chunks(R[:, h, :]), 0), columns(per_chunk(ident), 0),
                      ACT.Copy).then_inc(s["inv_even_columns"], 1)
                for h in range(HEADS):
                    act.wait_ge(s["inv_first_turned"], L * per["inv_first_turned"] + h + 1)
                    A(T[:, h, :], bank[4 + h % 2][:, :], ACT.Copy).then_inc(s["inv_t_first"], 1)
                for k in range(STEPS):
                    if k < JOINS:
                        act.wait_ge(s["gt_product"], L * per["gt_product"] + k + 1)
                        if k >= 2:
                            act.wait_ge(s["tgt_product"], L * per["tgt_product"] + k - 1)
                        if k < JOINS - HEADS:
                            ins = A(p_ring[:, k % 2, :], bank[k % 2][:, :], ACT.Copy)
                        else:
                            ins = A(even_blocks(p_ring[HI, k % 2, :], C // 2),
                                    even_blocks(bank[k % 2][HI, :], C // 2), ACT.Copy)
                        ins.then_inc(s["gt_copied"], 1)
                    if k >= 2:
                        act.wait_ge(s["inv_turned"], L * per["inv_turned"] + k - 1)
                        A(R[:, (k - 2) % 4, :], bank[4 + k % 2][:, :], ACT.Copy).then_inc(s["inv_r_updated"], 1)
                    if k in (3, 5, 7):
                        level_exp(k // 2)
                    if k - 4 in LEVEL_AFTER:
                        level_exp(LEVEL_AFTER[k - 4])
                for h in range(HEADS):
                    act.wait_ge(s["kcd_product"], L * per["kcd_product"] + h + 1)
                    A(kcd[:, h, :], bank[6 + h % 2][:, :], ACT.Copy, scale=-1.0).then_inc(s["kcd_ready"], 1)
                act.wait_ge(s["hg_dve_step"], L * per["hg_dve_step"] + 13)
                A(hk_out, hk_out, ACT.Exp).then_inc(s["hg_act_step"], 1)
                A(hq_in, hb, ACT.Exp).then_inc(s["hg_act_step"], 1)
                A(hw[:, 0:8], hbl[:, 0:8], ACT.Exp).then_inc(s["hg_act_step"], 1)
                for c in range(NC):
                    act.wait_ge(s["v_new_product"], L * per["v_new_product"] + c + 1)
                    if c >= 2:
                        act.wait_ge(s["delta_out"], L * per["delta_out"] + c - 1)
                    A(vn_ring[:, c % 2, :], bank[c % 2][:, :], ACT.Copy).then_inc(s["v_new_ready"], 1)
                act.wait_ge(s["delta_out"], L * per["delta_out"] + 4)
                for h in range(HEADS):
                    A(oT[:, h, :], bank[2 + h][:, :], ACT.Copy).then_inc(s["delta_out_copied"], 1)

                def square_out(t):
                    A(sq_ring[:, t % 4, :], oT[:, t, :], ACT.Square).then_inc(s["out_squared"], 1)

                def out_rstd(t):
                    act.wait_ge(s["out_mean_square"], L * per["out_mean_square"] + t + 1)
                    A(rs_ring[t % 4], bank[t % 2][:, :], ACT.Ln, bias=EPS).then_inc(s["out_log"], 1)
                    act.wait_ge(s["out_log"], L * per["out_log"] + t + 1)
                    A(rs_ring[t % 4], rs_ring[t % 4], ACT.Exp, scale=-0.5).then_inc(s["out_rstd"], 1)

                def out_hi(t):
                    act.wait_ge(s["out_gated"], L * per["out_gated"] + t + 1)
                    A(h_hi[:, t, :], oT[:, t, :], ACT.Copy).then_inc(s["mix_hi_ready"], 1)

                act.wait_ge(s["delta_out_copied"], L * per["delta_out_copied"] + 4)
                for t in range(4):
                    square_out(t)
                for t in range(4):
                    act.wait_ge(s["hg_turned"], L * per["hg_turned"] + t + 1)
                    dst = hk_tok if t < 2 else hv_tok
                    A(dst[:, t % 2, :], bank[4 + t][:, :], ACT.Copy).then_inc(s["hg_turned_copied"], 1)
                out_rstd(0)
                out_rstd(1)
                for t in range(2):
                    act.wait_ge(s["ret_turned"], L * per["ret_turned"] + 3 + t)
                    A(v_tok[:, t, :], bank[6 + t][:, :], ACT.Copy).then_inc(s["ret_v_copied"], 1)
                out_rstd(2)
                out_rstd(3)
                for t in range(2):
                    act.wait_ge(s["hg_out"], L * per["hg_out"] + t + 1)
                    A(oT[:, 4 + t, :], bank[6 + t][:, :], ACT.Copy).then_inc(s["hg_out_copied"], 1)
                    act.wait_ge(s["hg_out_copied"], L * per["hg_out_copied"] + t + 1)
                    square_out(4 + t)
                for t in range(2):
                    act.wait_ge(s["ret_out"], L * per["ret_out"] + t + 1)
                    A(oT[:, 6 + t, :], bank[2 + t][:, :], ACT.Copy).then_inc(s["ret_out_copied"], 1)
                    act.wait_ge(s["ret_out_copied"], L * per["ret_out_copied"] + t + 1)
                    square_out(6 + t)
                    out_hi(t)
                for t in range(4, 8):
                    out_rstd(t)
                    out_hi(t - 2)
                out_hi(6)
                out_hi(7)

                with act.Fori(0, OUT_UNITS // 2 - 1) as i:
                    for u in range(2):
                        act.wait_ge(s["unit_used"], L * per["unit_used"] + OUT0 + 2 * i + u + 1)
                        split_hi(q0 + OUT0 // 2 + i + 1, u)

                norm(L, 1, lambda: [split_hi(q0 + UP0 // 2, u) for u in range(2)])
                norm_hi(L, 1)

                nc.scalar.preload_act_table_set("silu_and_others")
                with act.Fori(0, FT) as i:
                    for u, dst in ((0, cg), (1, cv)):
                        act.wait_ge(s["unit_used"], L * per["unit_used"] + UP0 + 2 * i + u + 1)
                        split_hi(q0 + UP0 // 2 + i + 1, u)
                        A(dst[:, :], bank[u][:, :], ACT.Identity,
                          scale=param("ffn_conv", (2 * i + u) * 3 + 2),
                          bias=param("ffn_bias", 2 * i + u)).then_inc(s["ffn_last_tap"], 1)
                        if u == 0:
                            act.wait_ge(s["ffn_conv_done"], L * per["ffn_conv_done"] + 2 * i + 1)
                            A(cg[:, :], cg[:, :], ACT.Silu).then_inc(s["ffn_silu"], 1)
                    act.wait_ge(s["ffn_product"], L * per["ffn_product"] + i + 1)
                    A(g_hi[:, bass.ds(i, 1), :], gt[:, :].unsqueeze(1), ACT.Copy).then_inc(s["g_hi_ready"], 1)

                with act.Fori(0, DOWN_UNITS // 2 - 1) as i:
                    for u in range(2):
                        act.wait_ge(s["unit_used"], L * per["unit_used"] + DOWN0 + 2 * i + u + 1)
                        split_hi(q0 + DOWN0 // 2 + i + 1, u)
            norm(DEPTH, 0)

        @block.vector
        def _(dve):
            tt, ts, stt = nc.vector.tensor_tensor, nc.vector.tensor_scalar, nc.vector.scalar_tensor_tensor

            def split_lo(L, k, u):
                dve.wait_ge(s["hi_ready"], L * per["hi_ready"] + k + 1)
                tt(w_lo[:, u, :], raw[:, u, :], w_hi[:, u, :].bitcast(F32),
                   ALU.subtract).then_inc(s["lo_ready"], 1)

            def norm(L, which, weight, meanwhile=None, split=True):
                if meanwhile:
                    meanwhile()
                dve.wait_ge(s["rstd_ready"], L * per["rstd_ready"] + which + 1)
                for k in range(KT):
                    stt(gqkv[:, k, :], x[:, k, :], weight(k), rstd[:, :], ALU.mult,
                        ALU.mult).then_inc(s["x_normed"], 1)
                    if k % 2 and split:
                        dve.wait_ge(s["h_hi_ready"], L * per["h_hi_ready"] + 8 * which + k)
                        tt(h_lo[:, k - 1, :], gqkv[:, k - 1, :], h_hi[:, k - 1, :].bitcast(F32),
                           ALU.subtract).then_inc(s["h_lo_even_ready"], 1)

            steps = [0]
            dve.wait_ge(setup_loaded, 48)

            def once(ins):
                ins.then_inc(setup_dve, 1)
                steps[0] += 1
                dve.wait_ge(setup_dve, steps[0])

            posf, ang = angles[1], angles[2]
            magic = 12582912.0
            two_pi = [6.28125, float(np.float32(2 * np.pi - 6.28125))]
            two_pi.append(float(2 * np.pi - two_pi[0] - two_pi[1]))
            once(nc.vector.tensor_copy(posf, angles[0].bitcast(I32)))
            once(ts(ang, posf, const("inv_freq"), None, ALU.mult))

            def in_turn(ins):
                ins.then_inc(setup_dve, 1)
                steps[0] += 1
                dve.wait_ge(setup_dve, steps[0] - 1)

            chains = ((sin_t, 0.0, angles[3], angles[4]), (cos_t, 0.25, angles[5], angles[6]))
            for dst, quarter, turns, n_turns in chains:
                in_turn(ts(turns, ang, float(1 / (2 * np.pi)), quarter, ALU.mult, ALU.add))
            for dst, quarter, turns, n_turns in chains:
                in_turn(ts(n_turns, turns, magic, -magic, ALU.add, ALU.add))
            for dst, quarter, turns, n_turns in chains:
                in_turn(stt(turns, n_turns, -two_pi[0], ang, ALU.mult, ALU.add))
            for step in (1, 2):
                for dst, quarter, turns, n_turns in chains:
                    in_turn(stt(turns, n_turns, -two_pi[step], turns, ALU.mult, ALU.add))
            for dst, quarter, turns, n_turns in chains:
                in_turn(ts(turns, turns, float(2 * np.pi * quarter), 3.1415925, ALU.add, ALU.min))
            for dst, quarter, turns, n_turns in chains:
                in_turn(ts(dst[:, :], turns, -3.1415925, None, ALU.max))
            assert steps[0] == SETUP_ANGLES
            l0, l1 = lb[:, 0, 0:2], lb[:, 1, 0:2]
            once(tt(lbw[:, 4:6], l0, l1, ALU.max))
            once(tt(lbw[:, 0:4].rearrange("p (l t) -> p l t", l=DEPTH), lb[:, :, 0:2],
                    lbw[:, 4:6].unsqueeze(1).broadcast_to([P, DEPTH, 2]), ALU.subtract))
            assert steps[0] == SETUP_LB
            dve.wait_ge(x_loaded, 16 * KT)
            dve.sem_inc(s["x_after_ffn"], KT)
            dve.wait_ge(setup_act, 3)
            once(tt(lbw[:, 4:6], lbw[:, 0:2], lbw[:, 2:4], ALU.add))
            once(nc.vector.reciprocal(lbw[:, 6:8], lbw[:, 4:6]))
            once(tt(lbw[:, 0:4].rearrange("p (l t) -> p l t", l=DEPTH),
                    lbw[:, 0:4].rearrange("p (l t) -> p l t", l=DEPTH),
                    lbw[:, 6:8].unsqueeze(1).broadcast_to([P, DEPTH, 2]), ALU.mult))
            once(tt(lbw[:, 2:4], lbw[:, 0:2], lbw[:, 2:4], ALU.add))
            for layer in range(DEPTH):
                once(tt(lb[:, layer, 0:2], lbw[:, 2 * layer:2 * layer + 2], lbw[:, 0:2], ALU.subtract))
            once(ts(lb[:, :, 0:2], lb[:, :, 0:2], 0.0, None, ALU.max))
            once(ts(lb[:, :, 2:4], lb[:, :, 0:2], -1.0, 1.0, ALU.mult, ALU.add))
            dve.wait_ge(loaded, 48)

            with dve.Fori(0, DEPTH) as L:
                nc.vector.tensor_copy(lb_cur[:, :].unsqueeze(1), lb[:, bass.ds(L, 1), :])
                nc.vector.tensor_copy(cur[:, :].unsqueeze(1), par[:, bass.ds(L, 1), :]).then_inc(s["params_copied"], 1)
                dve.wait_ge(s["params_copied"], L * per["params_copied"] + 1)
                for u in range(2):
                    split_lo(L, u, u)
                dve.wait_ge(s["wab_hi_ready"], L * per["wab_hi_ready"] + 1)
                tt(wab[:, :, 8:16], param("w_ab", 0, KT * 8).rearrange("p (k n) -> p k n", k=KT),
                   wab[:, :, 0:8].bitcast(F32), ALU.subtract).then_inc(s["wab_lo_ready"], 1)
                norm(L, 0, lambda k: param("norm1", k))
                dve.wait_ge(s["ab_projected"], L * per["ab_projected"] + 1)
                gd = s["gate_dve_step"]
                nc.vector.tensor_copy(ab_rows, bank[6][0:16, :]).then_inc(s["ab_copied"], 1)
                split_lo(L, 2, 0)
                split_lo(L, 3, 1)
                dve.wait_ge(s["ab_turned"], L * per["ab_turned"] + 1)
                both = bank[7][:, 0:64].rearrange("p (c n) -> p c n", c=NC)
                nc.vector.tensor_copy(abc[:, :, :], both[:, :, 0:8]).then_inc(s["ab_hi_copied"], 1)
                dve.wait_ge(s["ab_hi_copied"], L * per["ab_hi_copied"] + 1)
                tt(abc[:, :, :], abc[:, :, :], both[:, :, 8:16], ALU.add).then_inc(gd, 1)
                dve.wait_ge(s["gate_dve_step"], L * per["gate_dve_step"] + 1)
                tt(hc(za), abc[:, :, 0:4].rearrange("p c h -> p h c"),
                   param("dt_bias", 0, 4).unsqueeze(2).broadcast_to([P, HEADS, NC]), ALU.add).then_inc(gd, 1)
                ts(hc(nb), abc[:, :, 4:8].rearrange("p c h -> p h c"), -1.0, 80.0, ALU.mult, ALU.min).then_inc(gd, 1)
                dve.wait_ge(s["gate_act_step"], L * per["gate_act_step"] + 3)
                stt(sp, za, 0.0, sp, ALU.max, ALU.add).then_inc(gd, 1)
                dve.wait_ge(s["gate_act_step"], L * per["gate_act_step"] + 4)
                dve.wait_ge(s["gate_dve_step"], L * per["gate_dve_step"] + 4)
                stt(hc(g_tok), hc(sp), -1.0, e_a[:, 0:4].unsqueeze(2).broadcast_to([P, HEADS, NC]),
                    ALU.mult, ALU.mult).then_inc(gd, 1)
                dve.wait_ge(s["gate_act_step"], L * per["gate_act_step"] + 5)
                ts(nb, nb, 1.0, None, ALU.add).then_inc(gd, 1)
                dve.wait_ge(s["gate_dve_step"], L * per["gate_dve_step"] + 6)
                nc.vector.reciprocal(beta, nb).then_inc(gd, 1)
                split_lo(L, 4, 0)
                dve.wait_ge(s["b_token_major"], L * per["b_token_major"] + 1)
                nc.vector.tensor_copy(btok, bank[6][:, 64:80]).then_inc(gd, 1)
                dve.wait_ge(s["gate_dve_step"], L * per["gate_dve_step"] + 8)
                for h in range(HEADS):
                    dve.wait_ge(s["b_spread"], L * per["b_spread"] + h + 1)
                    nc.vector.tensor_copy(hc(bl)[:, h, :], chunks(bank[2 + h][:, :])[:, :, C - 1]).then_inc(gd, 1)
                    for c in range(NC):
                        ins = ts(decay[:, h, c * C:(c + 1) * C], bank[2 + h][:, c * C:(c + 1) * C],
                                 btok[:, h * NC + c:h * NC + c + 1], 0.0, ALU.subtract, ALU.min)
                    ins.then_inc(s["b_diff_ready"], 1)
                    if h == 1:
                        split_lo(L, 5, 1)
                dve.wait_ge(s["gate_dve_step"], L * per["gate_dve_step"] + 12)
                tt(dko, bl, btok, ALU.subtract).then_inc(gd, 1)
                dve.wait_ge(s["gate_act_step"], L * per["gate_act_step"] + 6)
                tt(be, beta, e_tok, ALU.mult).then_inc(gd, 1)

                hd = s["hg_dve_step"]
                split_lo(L, 6, 0)
                dve.wait_ge(s["h_lo_odd_ready"], L * per["h_lo_odd_ready"] + 4)
                dve.wait_ge(s["bank_copied"], L * per["bank_copied"] + 2)
                ts(hE, hz, -1.0, 40.0, ALU.mult, ALU.min).then_inc(hd, 1)
                ts(hs, hz, -1.0, -40.0, ALU.mult, ALU.add).then_inc(hd, 1)
                dve.wait_ge(s["hg_dve_step"], L * per["hg_dve_step"] + 2)
                ts(hs, hs, 0.0, 40.0, ALU.max, ALU.min).then_inc(hd, 1)
                ts(hg, hz, 40.0, 0.0, ALU.add, ALU.min).then_inc(hd, 1)
                split_lo(L, 7, 1)
                dve.wait_ge(s["hg_act_step"], L * per["hg_act_step"] + 2)
                tt(hk, hz, hl, ALU.add).then_inc(hd, 1)
                dve.wait_ge(s["hg_dve_step"], L * per["hg_dve_step"] + 5)
                ts(hk, hk, -1.0, 0.0, ALU.mult, ALU.min).then_inc(hd, 1)
                tt(hg, hg, hl, ALU.subtract).then_inc(hd, 1)
                dve.wait_ge(s["hg_dve_step"], L * per["hg_dve_step"] + 7)
                tt(hg, hg, hs, ALU.add).then_inc(hd, 1)
                split_lo(L, 8, 0)
                dve.wait_ge(s["hg_act_step"], L * per["hg_act_step"] + 3)
                for t in range(2):
                    o = slice(t * SEQ, (t + 1) * SEQ)
                    ins = stt(hf[:, o], hE[:, o], lb_cur[:, t:t + 1], hf[:, o], ALU.mult, ALU.add)
                ins.then_inc(hd, 1)
                split_lo(L, 9, 1)
                dve.wait_ge(s["hg_act_step"], L * per["hg_act_step"] + 4)
                for t in range(2):
                    o = slice(t * SEQ, (t + 1) * SEQ)
                    ins = ts(hk[:, o], hk[:, o], lb_cur[:, 2 + t:3 + t], None, ALU.mult)
                ins.then_inc(hd, 1)
                split_lo(L, 10, 0)
                dve.wait_ge(s["hg_act_step"], L * per["hg_act_step"] + 5)
                dve.wait_ge(s["hg_dve_step"], L * per["hg_dve_step"] + 8)
                tt(hg, hg, hf, ALU.add).then_inc(hd, 1)
                dve.wait_ge(s["hg_dve_step"], L * per["hg_dve_step"] + 11)
                for c in range(2 * NC):
                    o = slice(c * C, (c + 1) * C)
                    ins = nc.vector.tensor_tensor_scan(hb[:, o], const("ones"), hg[:, o], 0.0,
                                                       ALU.mult, ALU.add)
                ins.then_inc(hd, 1)
                split_lo(L, 11, 1)
                with dve.Fori(0, CONV_UNITS // 2) as i:
                    for u in range(2):
                        n = 2 * i + u
                        for tap in range(1, 4):
                            if tap == 1:
                                dve.wait_ge(s["conv_last_tap"], L * per["conv_last_tap"] + n + 1)
                            else:
                                dve.wait_ge(s["conv_mid_taps"], L * per["conv_mid_taps"] + 2 * n + tap - 1)
                            o = gqkv[:, bass.ds(n, 1), tap:SEQ]
                            stt(o, bank[u][:, 0:SEQ - tap].unsqueeze(1), param("gdn_conv", n * 4 + 3 - tap), o,
                                ALU.mult, ALU.add).then_inc(s["conv_mid_taps"] if tap < 3 else s["conv_done"], 1)
                        split_lo(L, CONV0 + n + 2, u)
                with dve.Fori(0, 4) as i:
                    for u in range(2):
                        split_lo(L, GATE0 + 2 * i + 2 + u, u)
                    for u in range(2):
                        dve.wait_ge(s["l2_summed"], L * per["l2_summed"] + 2 * i + u + 1)
                        apart(dve)
                        nc.vector.tensor_copy(area_a[:, bass.ds(2 * i + u, 1), :],
                                              bank[2 + u][:, :].unsqueeze(1)).then_inc(s["l2_copied"], 1)
                split_lo(L, GATE0 + 10, 0)
                dve.wait_ge(s["decay_masked"], L * per["decay_masked"] + 4)
                for h in range(HEADS):
                    dve.wait_ge(s["beta_spread"], L * per["beta_spread"] + h + 1)
                    tt(beta_decay[:, h, :], bank[4 + h][:, :], decay[:, h, :],
                       ALU.mult).then_inc(s["beta_decay_ready"], 1)

                def norm_qk(h):
                    for n, t in enumerate((h, 4 + h)):
                        dve.wait_ge(s["l2_rnorm"], L * per["l2_rnorm"] + 2 * h + n + 1)
                        stt(gqkv[:, t, :], gqkv[:, t, :], float(P) ** -0.5 if t < 4 else 1.0, area_a[:, t, :],
                            ALU.mult, ALU.mult).then_inc(s["qk_normed"], 1)

                norm_qk(0)
                norm_qk(1)
                split_lo(L, GATE0 + 11, 1)

                dve.wait_ge(s["gate_dve_step"], L * per["gate_dve_step"] + 14)
                def level_qk(n):
                    half = LEVELS[n]
                    X, k3, q3 = (a.rearrange("p (g s) -> p g s", s=2 * half) for a in (X_ring[n % RING], hk, hq))
                    dve.wait_ge(s["level_exp"], L * per["level_exp"] + n + 1)
                    tt(X[:, :, 0:half], X[:, :, 0:half], k3[:, :, 0:half], ALU.mult)
                    tt(X[:, :, half:], X[:, :, half:], q3[:, :, half:], ALU.mult).then_inc(s["level_qk"], 1)

                def place(g):
                    n, h = g // HEADS, g % HEADS
                    mask = const("lvl", n, C) if n < len(LEVELS) else ident
                    dve.wait_ge(s["hg_scores"], L * per["hg_scores"] + g + 1)
                    if n:
                        dve.wait_ge(s["hg_scores_placed"], L * per["hg_scores_placed"] + g - HEADS + 1)
                    else:
                        dve.wait_ge(s["hg_scores_cleared"], L * per["hg_scores_cleared"] + 1)
                    apart(dve)
                    to, src, mask4 = chunks(hPT[:, h, :]), chunks(bank[6 + g % 2][:, :]), per_chunk(mask.bitcast(I32))
                    if n < len(LEVELS):
                        if n == len(LEVELS) - 1:
                            to, src, mask4 = to[LO], src[LO], mask4[LO]
                        to, src, mask4 = (a.rearrange("p c (g s) -> p c g s", s=2 * LEVELS[n])[:, :, :, LEVELS[n]:]
                                          for a in (to, src, mask4))
                    nc.vector.copy_predicated(to, mask4, src).then_inc(s["hg_scores_placed"], 1)

                for h in range(HEADS):
                    e = h % 2
                    dve.wait_ge(s["kk_qk_products"], L * per["kk_qk_products"] + h + 1)
                    dve.wait_ge(s["qk_normed"], L * per["qk_normed"] + 2 * h + 2)
                    dve.wait_ge(s["beta_decay_ready"], L * per["beta_decay_ready"] + h + 1)
                    tt(G[:, h, :], bank[e][:, :], beta_decay[:, h, :], ALU.mult).then_inc(s["kk_decayed"], 1)
                    dve.wait_ge(s["kk_decayed"], L * per["kk_decayed"] + h + 1)
                    tt(attn[:, h, :], bank[2 + e][:, :], decay[:, h, :], ALU.mult).then_inc(s["g_attn_ready"], 1)
                    if h < 2:
                        norm_qk(h + 2)
                    if h % 2:
                        for g in (h - 1, h):
                            dve.wait_ge(s["kv_turned"], L * per["kv_turned"] + g + 1)
                            tt(chunks(v_b[:, g, :]), chunks(bank[4 + g][:, :]), per_token(hc(beta)[:, g, :]),
                               ALU.mult).then_inc(s["kv_turned_read"], 1)
                level_qk(0)
                for k in range(STEPS):
                    if 1 <= k < JOINS + 1:
                        dve.wait_ge(s["tgt_product"], L * per["tgt_product"] + k)
                        if k < 5:
                            dve.wait_ge(s["inv_t_first"], L * per["inv_t_first"] + k)
                        else:
                            dve.wait_ge(s["inv_t_updated"], L * per["inv_t_updated"] + k - 4)
                        half = LEVELS[1 + (k - 1) // 4]
                        rows_of = slice(0, P) if half < C // 2 else HI
                        to_join = even_blocks(T[rows_of, (k - 1) % 4, :], half)
                        tt(to_join, to_join, even_blocks(bank[2 + (k - 1) % 2][rows_of, :], half),
                           ALU.subtract).then_inc(s["inv_t_updated"], 1)
                    for g in groups_of(k):
                        place(g)
                    if k < HEADS:
                        dve.wait_ge(s["kv_turned"], L * per["kv_turned"] + 4 + k + 1)
                        tt(chunks(k_be[:, k, :]), chunks(bank[6 + k % 2][:, :]), per_token(hc(be)[:, k, :]),
                           ALU.mult).then_inc(s["kv_turned_read"], 1)
                    if k in (4, 6, 8):
                        level_qk(k // 2 - 1)
                    if k - 5 in LEVEL_AFTER:
                        level_qk(LEVEL_AFTER[k - 5])
                bc = hb.rearrange("p (c i) -> p c i", i=C)
                nc.vector.tensor_copy(hbl[:, 0:8].unsqueeze(2), bc[:, :, C - 1:C])
                tt(hk_out.rearrange("p (c i) -> p c i", i=C), bc[:, :, C - 1:C].broadcast_to([P, 2 * NC, C]), bc,
                   ALU.subtract).then_inc(hd, 1)
                dve.wait_ge(s["gate_act_step"], L * per["gate_act_step"] + 8)
                for h in range(HEADS):
                    dve.wait_ge(s["k_turned_again"], L * per["k_turned_again"] + h + 1)
                    tt(chunks(k_out[:, h, :]), chunks(bank[2 + h][:, :]), per_token(hc(ko)[:, h, :]),
                       ALU.mult).then_inc(s["k_out_ready"], 1)
                for c in range(NC):
                    dve.wait_ge(s["rotated"], L * per["rotated"] + c + 1)
                    if c >= 2:
                        dve.wait_ge(s["rot_done"], L * per["rot_done"] + c - 1)
                    tt(scratch[:, c % 2, :], bank[7][:, :], sin_t[:, :], ALU.mult).then_inc(s["rot_sin"], 1)
                    if c == NC - 1:
                        break
                    dve.wait_ge(s["state_sum"], L * per["state_sum"] + c + 1)
                    if c == 0:
                        nc.vector.tensor_copy(S_ring[:, 0, :], bank[6][:, :]).then_inc(s["state_ready"], 1)
                        dve.wait_ge(s["hg_act_step"], L * per["hg_act_step"] + 6)
                        tt(hk_out, hk_out, hk, ALU.mult).then_inc(hd, 1)
                    else:
                        dve.wait_ge(s["state_ready"], L * per["state_ready"] + c)
                        if c >= 2:
                            dve.wait_ge(s["delta_out"], L * per["delta_out"] + c)
                        for h in range(HEADS):
                            o = slice(h * P, (h + 1) * P)
                            ins = stt(S_ring[:, c % 2, o], S_ring[:, (c - 1) % 2, o],
                                      w_dec[:, h * NC + c:h * NC + c + 1], bank[6][:, o], ALU.mult, ALU.add)
                        ins.then_inc(s["state_ready"], 1)
                    dve.wait_ge(s["rot_sin"], L * per["rot_sin"] + c + 1)
                    dve.wait_ge(s["rot_cos"], L * per["rot_cos"] + c + 1)
                    tt(rqk[:, c, :], rqk[:, c, :], scratch[:, c % 2, :], ALU.add).then_inc(s["rot_done"], 1)
                dve.wait_ge(s["rot_sin"], L * per["rot_sin"] + NC)
                dve.wait_ge(s["rot_cos"], L * per["rot_cos"] + NC)
                tt(rqk[:, 3, :], rqk[:, 3, :], scratch[:, 1, :], ALU.add).then_inc(s["rot_done"], 1)

                def states(to, first_bank, w_of, summed, per_sum, done, per_done):
                    for t in range(2):
                        dve.wait_ge(summed, L * per_sum + t + 1)
                        st = to[:, t, 0:3 * P].rearrange("p (c n) -> p c n", c=3)
                        tt(st, bank[first_bank + t][:, 0:3 * P].rearrange("p (c n) -> p c n", c=3),
                           const("blocks").unsqueeze(1).broadcast_to([P, 3, P]), ALU.mult).then_inc(done, 1)
                        for c in range(1, 3):
                            dve.wait_ge(done, L * per_done + 3 * t + c)
                            stt(st[:, c, :], st[:, c - 1, :], w_of(t, c), st[:, c, :], ALU.mult,
                                ALU.add).then_inc(done, 1)

                for h in range(HEADS):
                    dve.wait_ge(s["ret_scores"], L * per["ret_scores"] + h + 1)
                    tt(chunks(PT[:, h, :]), chunks(bank[h % 2][:, :]), per_chunk(const("ret_decay", h, C)),
                       ALU.mult).then_inc(s["ret_decayed"], 1)
                for t in range(2):
                    dve.wait_ge(s["ret_turned"], L * per["ret_turned"] + t + 1)
                    tt(chunks(k_tok[:, t, :]), chunks(bank[4 + t][:, :]), per_chunk(const("ret_k", t, P)),
                       ALU.mult).then_inc(s["ret_k_out"], 1)
                states(hSU, 2, lambda t, c: hw[:, t * NC + c:t * NC + c + 1], s["hg_sums"], per["hg_sums"],
                       s["hg_states"], per["hg_states"])
                states(SU, 4, lambda t, c: const("ret_w", t, 1), s["ret_sums"], per["ret_sums"],
                       s["ret_states"], per["ret_states"])

                for t in range(8):
                    dve.wait_ge(s["out_rstd"], L * per["out_rstd"] + t + 1)
                    stt(oT[:, t, :], oT[:, t, :], param("onorm", t), rs_ring[t % 4], ALU.mult,
                        ALU.mult).then_inc(s["out_normed"], 1)
                    dve.wait_ge(s["out_normed"], L * per["out_normed"] + t + 1)
                    tt(oT[:, t, :], oT[:, t, :], gate[:, t, :], ALU.mult).then_inc(s["out_gated"], 1)

                with dve.Fori(0, OUT_UNITS // 2 - 1) as i:
                    for u in range(2):
                        split_lo(L, OUT0 + 2 + 2 * i + u, u)
                for m in range(KT):
                    if m < KT - 1:
                        dve.wait_ge(s["out_projected"], L * per["out_projected"] + m + 1)
                    else:
                        dve.wait_ge(s["unit_used"], L * per["unit_used"] + OUT0 + 8)
                    tt(x[:, m, :], x[:, m, :], bank[(m + 2) % 8][:, :], ALU.add).then_inc(s["x_after_mixer"], 1)
                dve.wait_ge(s["x_after_mixer"], L * per["x_after_mixer"] + 8)
                norm(L, 1, lambda k: param("norm2", k), lambda: [split_lo(L, UP0 + u, u) for u in range(2)])

                with dve.Fori(0, FT) as i:
                    for u, dst in ((0, cg), (1, cv)):
                        split_lo(L, UP0 + 2 + 2 * i + u, u)
                        n = 2 * i + u
                        dve.wait_ge(s["ffn_last_tap"], L * per["ffn_last_tap"] + n + 1)
                        stt(dst[:, 1:SEQ], bank[u][:, 0:SEQ - 1], param("ffn_conv", n * 3 + 1), dst[:, 1:SEQ],
                            ALU.mult, ALU.add).then_inc(s["ffn_mid_tap"], 1)
                        dve.wait_ge(s["ffn_mid_tap"], L * per["ffn_mid_tap"] + n + 1)
                        stt(dst[:, 2:SEQ], bank[u][:, 0:SEQ - 2], param("ffn_conv", n * 3), dst[:, 2:SEQ],
                            ALU.mult, ALU.add).then_inc(s["ffn_conv_done"], 1)
                    dve.wait_ge(s["ffn_conv_done"], L * per["ffn_conv_done"] + 2 * i + 2)
                    dve.wait_ge(s["ffn_silu"], L * per["ffn_silu"] + i + 1)
                    tt(gt[:, :], cg[:, :], cv[:, :], ALU.mult).then_inc(s["ffn_product"], 1)
                    dve.wait_ge(s["g_hi_ready"], L * per["g_hi_ready"] + i + 1)
                    tt(g_lo[:, bass.ds(i, 1), :], gt[:, :].unsqueeze(1), g_hi[:, bass.ds(i, 1), :].bitcast(F32),
                       ALU.subtract).then_inc(s["g_lo_ready"], 1)

                with dve.Fori(0, DOWN_UNITS // 2 - 1) as i:
                    for u in range(2):
                        split_lo(L, DOWN0 + 2 + 2 * i + u, u)
                for m in range(KT):
                    if m < KT - 1:
                        dve.wait_ge(s["down_projected"], L * per["down_projected"] + m + 1)
                    else:
                        dve.wait_ge(s["unit_used"], L * per["unit_used"] + UNITS)
                    tt(x[:, m, :], x[:, m, :], bank[(m + 2) % 8][:, :], ALU.add).then_inc(s["x_after_ffn"], 1)
                dve.wait_ge(s["x_after_ffn"], 8 * L + 16)

            norm(DEPTH, 0, lambda k: fin[:, k:k + 1], split=False)

        @block.tensor
        def _(pe):
            mm = nc.tensor.matmul

            def norm(L, which):
                for k in range(0, KT, 2):
                    pe.wait_ge(s["squares_paired"], L * per["squares_paired"] + 4 * which + k // 2 + 1)
                    ins = mm(bank[2][:, :], const("mean_model"), gqkv[:, k, :], start=k == 0, stop=k == KT - 2)
                ins.then_inc(s["x_mean_square"], 1)

            def three(dst, hi, lo, b_hi, b_lo, start, stop):
                mm(dst, hi, b_hi, start=start, stop=False)
                mm(dst, hi, b_lo, start=False, stop=False)
                return mm(dst, lo, b_hi, start=False, stop=stop)

            def part(u, kt):
                o = slice(kt * P, (kt + 1) * P)
                return three(bank[u][:, :], w_hi[:, u, o], w_lo[:, u, o], h_hi[:, kt, :], h_lo[:, kt, :],
                             kt == 0, kt == KT - 1)

            def unit(L, k, u):
                pe.wait_ge(s["lo_ready"], L * per["lo_ready"] + k + 1)
                for kt in range(KT):
                    ins = part(u, kt)
                ins.then_inc(s["unit_used"], 1)

            def first_unit(L, k, normed_before, gates=False):
                pe.wait_ge(s["lo_ready"], L * per["lo_ready"] + k + 1)
                if gates:
                    pe.wait_ge(s["wab_lo_ready"], L * per["wab_lo_ready"] + 1)
                for kt in range(KT):
                    if kt % 2:
                        pe.wait_ge(s["h_lo_odd_ready"], L * per["h_lo_odd_ready"] + (normed_before + kt + 1) // 2)
                    else:
                        pe.wait_ge(s["h_lo_even_ready"], L * per["h_lo_even_ready"] + (normed_before + kt) // 2 + 1)
                    if gates:
                        mm(bank[6][0:16, :], wab[:, kt, :], h_hi[:, kt, :], start=kt == 0, stop=False)
                        ab = mm(bank[6][0:16, :], wab[:, kt, :], h_lo[:, kt, :], start=False, stop=kt == KT - 1)
                    ins = part(0, kt)
                if gates:
                    ab.then_inc(s["ab_projected"], 1)
                ins.then_inc(s["unit_used"], 1)

            def rows(L, k, u, b_hi, b_lo, start, stop, last=None, over_up=False, tiles=range(KT)):
                pe.wait_ge(s["lo_ready"], L * per["lo_ready"] + k + 1)
                for m in tiles:
                    if over_up and m >= KT - 2:
                        pe.wait_ge(s["ffn_conv_done"], L * per["ffn_conv_done"] + UP_UNITS - (KT - 1 - m))
                    o = slice(m * P, (m + 1) * P)
                    ins = three(bank[(m + 2) % 8][:, :], w_hi[:, u, o], w_lo[:, u, o], b_hi, b_lo, start, stop)
                    if last and m < KT - 1:
                        ins.then_inc(last, 1)
                if KT - 1 in tiles:
                    ins.then_inc(s["unit_used"], 1)

            pe.wait_ge(loaded, 48)
            with pe.Fori(0, DEPTH) as L:
                norm(L, 0)
                first_unit(L, 0, 0, gates=True)
                unit(L, 1, 1)
                pe.wait_ge(s["ab_copied"], L * per["ab_copied"] + 1)
                apart(pe)
                for c in range(NC):
                    ins = nc.tensor.transpose(bank[7][:, c * 16:c * 16 + 16], ab_rows[:, c * C:(c + 1) * C],
                                              ident[0:16, 0:16])
                ins.then_inc(s["ab_turned"], 1)
                pe.wait_ge(s["bank_copied"], L * per["bank_copied"] + 1)
                unit(L, 2, 0)
                pe.wait_ge(s["gate_dve_step"], L * per["gate_dve_step"] + 5)
                mm(bank[6][:, 64:80], causal, g_tok, start=True, stop=True).then_inc(s["b_token_major"], 1)
                for h in range(HEADS):
                    for c in range(NC):
                        ins = mm(bank[2 + h][:, c * C:(c + 1) * C],
                                 g_tok[:, h * NC + c:h * NC + c + 1].broadcast_to([P, C]), causal,
                                 start=True, stop=True)
                    ins.then_inc(s["b_spread"], 1)
                pe.wait_ge(s["bank_copied"], L * per["bank_copied"] + 2)
                unit(L, 3, 1)
                with pe.Fori(2, COPY_UNITS // 2) as i:
                    for u in range(2):
                        pe.wait_ge(s["bank_copied"], L * per["bank_copied"] + 2 * i + u - 1)
                        unit(L, 2 * i + u, u)
                for u in range(2):
                    pe.wait_ge(s["bank_copied"], L * per["bank_copied"] + COPY_UNITS - 1 + u)
                    unit(L, CONV0 + u, u)
                with pe.Fori(1, CONV_UNITS // 2) as i:
                    for u in range(2):
                        pe.wait_ge(s["conv_done"], L * per["conv_done"] + 2 * i + u - 1)
                        unit(L, CONV0 + 2 * i + u, u)
                for u in range(2):
                    pe.wait_ge(s["conv_done"], L * per["conv_done"] + CONV_UNITS - 1 + u)
                    unit(L, GATE0 + u, u)
                pe.wait_ge(s["exp_b_ready"], L * per["exp_b_ready"] + 4)
                pe.wait_ge(s["gate_dve_step"], L * per["gate_dve_step"] + 12)
                for u in range(2):
                    pe.wait_ge(s["l2_squared"], L * per["l2_squared"] + u + 1)
                    mm(bank[2 + u][:, :], const("ones"), area_a[:, u, :], start=True,
                       stop=True).then_inc(s["l2_summed"], 1)
                with pe.Fori(1, 4) as i:
                    for u in range(2):
                        pe.wait_ge(s["bank_copied"], L * per["bank_copied"] + COPY_UNITS + 2 * i + u - 1)
                        unit(L, GATE0 + 2 * i + u, u)
                    for u in range(2):
                        pe.wait_ge(s["l2_copied"], L * per["l2_copied"] + 2 * i + u - 1)
                        pe.wait_ge(s["l2_squared"], L * per["l2_squared"] + 2 * i + u + 1)
                        mm(bank[2 + u][:, :], const("ones"), area_a[:, bass.ds(2 * i + u, 1), :], start=True,
                           stop=True).then_inc(s["l2_summed"], 1)
                pe.wait_ge(s["bank_copied"], L * per["bank_copied"] + COPY_UNITS + 7)
                unit(L, GATE0 + 8, 0)
                for h in range(HEADS):
                    for c in range(NC):
                        ins = mm(bank[4 + h][:, c * C:(c + 1) * C],
                                 beta[:, h * NC + c:h * NC + c + 1].broadcast_to([P, C]), ident,
                                 start=True, stop=True)
                    ins.then_inc(s["beta_spread"], 1)
                pe.wait_ge(s["bank_copied"], L * per["bank_copied"] + COPY_UNITS + 8)
                unit(L, GATE0 + 9, 1)

                def turn(dst, src):
                    for c in range(NC):
                        o = slice(c * C, (c + 1) * C)
                        ins = nc.tensor.transpose(dst[:, o], src[:, o], ident)
                    return ins

                pe.wait_ge(s["qkv_silu"], L * per["qkv_silu"] + 12)
                pe.wait_ge(s["beta_decay_ready"], L * per["beta_decay_ready"] + 4)
                for h in range(HEADS):
                    turn(bank[4 + h], gqkv[:, 8 + h, :]).then_inc(s["kv_turned"], 1)
                pe.wait_ge(s["bank_copied"], L * per["bank_copied"] + COPY_UNITS + GATE_UNITS)
                pe.wait_ge(s["l2_copied"], L * per["l2_copied"] + 8)
                for h in range(HEADS):
                    e = h % 2
                    pe.wait_ge(s["qk_normed"], L * per["qk_normed"] + 2 * h + 2)
                    if h >= 2:
                        pe.wait_ge(s["g_attn_ready"], L * per["g_attn_ready"] + h - 1)
                    for c in range(NC):
                        o = slice(c * C, (c + 1) * C)
                        mm(bank[2 + e][:, o], gqkv[:, 4 + h, o], gqkv[:, h, o], start=True, stop=True)
                        ins = mm(bank[e][:, o], gqkv[:, 4 + h, o], gqkv[:, 4 + h, o], start=True, stop=True)
                    ins.then_inc(s["kk_qk_products"], 1)
                for h in range(2):
                    pe.wait_ge(s["kv_turned_read"], L * per["kv_turned_read"] + h + 3)
                    turn(bank[6 + h], gqkv[:, 4 + h, :]).then_inc(s["kv_turned"], 1)
                for h in range(HEADS):
                    pe.wait_ge(s["g_attn_ready"], L * per["g_attn_ready"] + min(h + 3, 4))
                    pe.wait_ge(s["inv_first"], L * per["inv_first"] + h + 1)
                    pe.wait_ge(s["inv_even_columns"], L * per["inv_even_columns"] + h + 1)
                    if h >= 2:
                        pe.wait_ge(s["inv_t_first"], L * per["inv_t_first"] + h - 1)
                    turn(bank[4 + h % 2], R[:, h, :]).then_inc(s["inv_first_turned"], 1)

                def join_p(k):
                    h = k % 4
                    pe.wait_ge(s["g_level"], L * per["g_level"] + k + 1)
                    if k < 4:
                        pe.wait_ge(s["inv_t_first"], L * per["inv_t_first"] + h + 1)
                    else:
                        pe.wait_ge(s["inv_t_updated"], L * per["inv_t_updated"] + k - 3)
                    if k >= 2:
                        pe.wait_ge(s["gt_copied"], L * per["gt_copied"] + k - 1)
                    if k >= JOINS - HEADS:
                        apart(pe)
                    for c in range(NC):
                        o = slice(c * C, (c + 1) * C)
                        lo, hi = slice(c * C, c * C + C // 2), slice(c * C + C // 2, c * C + C)
                        if k < JOINS - HEADS:
                            ins = mm(bank[k % 2][:, o], ml_ring[:, k % 2, o], T[:, h, o], start=True, stop=True)
                        else:
                            ins = mm(bank[k % 2][HI, lo], ml_ring[LO, k % 2, hi], T[LO, h, lo], start=True, stop=True)
                    ins.then_inc(s["gt_product"], 1)

                def join_tp(k):
                    h = k % 4
                    pe.wait_ge(s["gt_copied"], L * per["gt_copied"] + k + 1)
                    if k >= 4:
                        pe.wait_ge(s["inv_r_updated"], L * per["inv_r_updated"] + k - 3)
                    if k >= 2:
                        pe.wait_ge(s["inv_t_updated"], L * per["inv_t_updated"] + k - 1)
                    if k >= JOINS - HEADS:
                        apart(pe)
                    for c in range(NC):
                        o = slice(c * C, (c + 1) * C)
                        lo, hi = slice(c * C, c * C + C // 2), slice(c * C + C // 2, c * C + C)
                        if k < JOINS - HEADS:
                            ins = mm(bank[2 + k % 2][:, o], R[:, h, o], p_ring[:, k % 2, o], start=True, stop=True)
                        else:
                            ins = mm(bank[2 + k % 2][HI, lo], R[HI, h, hi], p_ring[HI, k % 2, lo],
                                     start=True, stop=True)
                    ins.then_inc(s["tgt_product"], 1)

                def join_x(k):
                    pe.wait_ge(s["inv_t_updated"], L * per["inv_t_updated"] + k + 1)
                    if k >= 2:
                        pe.wait_ge(s["inv_r_updated"], L * per["inv_r_updated"] + k - 1)
                    else:
                        pe.wait_ge(s["inv_t_first"], L * per["inv_t_first"] + 4)
                    turn(bank[4 + k % 2], T[:, k % 4, :]).then_inc(s["inv_turned"], 1)

                def scores(g):
                    n, h = g // HEADS, g % HEADS
                    if n < len(LEVELS):
                        pe.wait_ge(s["level_qk"], L * per["level_qk"] + n + 1)
                    if g >= 2:
                        pe.wait_ge(s["hg_scores_placed"], L * per["hg_scores_placed"] + g - 1)
                    if n == len(LEVELS) - 1:
                        apart(pe)
                    X = X_ring[n % RING]
                    r = slice(64 * (h % 2), 64 * (h % 2) + 64)
                    for c in range(NC):
                        a = (h // 2) * SEQ + c * C
                        dst = bank[6 + g % 2][:, c * C:(c + 1) * C]
                        if n < len(LEVELS) - 1:
                            ins = mm(dst, X[r, a:a + C], X[r, a:a + C], start=True, stop=True)
                        elif n < len(LEVELS):
                            ins = mm(dst[LO, HI], X[r, a:a + C // 2], X[r, a + C // 2:a + C], start=True, stop=True)
                        else:
                            ins = mm(dst, hk[r, a:a + C], hq[r, a:a + C], start=True, stop=True)
                    ins.then_inc(s["hg_scores"], 1)

                for k in range(STEPS):
                    if k in (2, 3):
                        pe.wait_ge(s["kv_turned_read"], L * per["kv_turned_read"] + 4 + k - 1)
                        turn(bank[6 + k % 2], gqkv[:, 4 + k, :]).then_inc(s["kv_turned"], 1)
                    if k == 4:
                        pe.wait_ge(s["kv_turned_read"], L * per["kv_turned_read"] + 8)
                    if k < JOINS:
                        join_p(k)
                    if 1 <= k < JOINS + 1:
                        join_tp(k - 1)
                    if k >= 2:
                        join_x(k - 2)
                    for g in groups_of(k):
                        scores(g)
                pe.wait_ge(s["inv_t_updated"], L * per["inv_t_updated"] + JOINS)
                pe.wait_ge(s["inv_r_updated"], L * per["inv_r_updated"] + JOINS)
                for h in range(HEADS):
                    turn(bank[2 + h], gqkv[:, 4 + h, :]).then_inc(s["k_turned_again"], 1)
                pe.wait_ge(s["hg_scores_placed"], L * per["hg_scores_placed"] + GROUPS)
                for h in range(HEADS):
                    pe.wait_ge(s["inv_r_updated"], L * per["inv_r_updated"] + 20 + h + 1)
                    if h >= 2:
                        pe.wait_ge(s["kcd_ready"], L * per["kcd_ready"] + h - 1)
                    for c in range(NC):
                        o = slice(c * C, (c + 1) * C)
                        ins = mm(bank[6 + h % 2][:, o], k_be[:, h, o], R[:, h, o], start=True, stop=True)
                    ins.then_inc(s["kcd_product"], 1)
                pe.wait_ge(s["gt_copied"], L * per["gt_copied"] + 24)
                pe.wait_ge(s["kcd_ready"], L * per["kcd_ready"] + 4)
                pe.wait_ge(s["k_out_ready"], L * per["k_out_ready"] + 4)
                pe.wait_ge(s["inv_t_updated"], L * per["inv_t_updated"] + 24)
                pe.wait_ge(s["q_in_ready"], L * per["q_in_ready"] + 4)
                for c in range(NC):
                    o = slice(c * C, (c + 1) * C)
                    before = S_ring[:, (c - 1) % 2, :]
                    if c:
                        pe.wait_ge(s["state_ready"], L * per["state_ready"] + c)
                    if c >= 2:
                        pe.wait_ge(s["v_new_ready"], L * per["v_new_ready"] + c - 1)
                    for h in range(HEADS):
                        ho = slice(h * P, (h + 1) * P)
                        ins = mm(bank[c % 2][:, ho], R[:, h, o], v_b[:, h, o], start=True, stop=c == 0)
                        if c:
                            ins = mm(bank[c % 2][:, ho], kcd[:, h, o], before[:, ho], start=False, stop=True)
                    ins.then_inc(s["v_new_product"], 1)
                    if c:
                        pe.wait_ge(s["rot_sin"], L * per["rot_sin"] + c)
                    mm(bank[7][:, :], const("rot"), rqk[:, c, :], start=True, stop=True).then_inc(s["rotated"], 1)
                    pe.wait_ge(s["v_new_ready"], L * per["v_new_ready"] + c + 1)
                    if c < NC - 1:
                        for h in range(HEADS):
                            ho = slice(h * P, (h + 1) * P)
                            ins = mm(bank[6][:, ho], k_out[:, h, o], vn_ring[:, c % 2, ho],
                                     start=True, stop=True)
                        ins.then_inc(s["state_sum"], 1)
                    for h in range(HEADS):
                        ho = slice(h * P, (h + 1) * P)
                        if c:
                            mm(bank[2 + h][:, o], before[:, ho], gqkv[:, h, o], start=True, stop=False)
                        ins = mm(bank[2 + h][:, o], vn_ring[:, c % 2, ho], attn[:, h, o], start=c == 0, stop=True)
                    ins.then_inc(s["delta_out"], 1)

                def sums(first_bank, k_of, v_of, done):
                    for t in range(2):
                        for c in range(NC - 1):
                            o = slice(c * C, (c + 1) * C)
                            ins = mm(bank[first_bank + t][:, c * P:(c + 1) * P], k_of[:, t, o], v_of[:, t, o],
                                     start=True, stop=True)
                        ins.then_inc(done, 1)

                def outputs(first_bank, states, q_of, v_of, p_of, ready, per_ready, done):
                    for t in range(2):
                        pe.wait_ge(ready, L * per_ready + 3 * t + 3)
                        for c in range(NC):
                            o = slice(c * C, (c + 1) * C)
                            if c:
                                mm(bank[first_bank + t][:, o], states[:, t, (c - 1) * P:c * P], q_of(t, o),
                                   start=True, stop=False, skip_group_check=True)
                            for e in range(2):
                                ins = mm(bank[first_bank + t][64 * e:64 * e + 64, o],
                                         v_of[:, t, c * C + 64 * e:c * C + 64 * e + 64],
                                         p_of[:, 2 * t + e, o], start=c == 0, stop=True, skip_group_check=True)
                        ins.then_inc(done, 1)

                pe.wait_ge(s["v_new_ready"], L * per["v_new_ready"] + 4)
                def ret_scores(h):
                    r = slice(64 * (h % 2), 64 * (h % 2) + 64)
                    for c in range(NC):
                        o = slice(c * C, (c + 1) * C)
                        ins = mm(bank[h % 2][:, o], rk[r, h // 2, o], rq[r, h // 2, o], start=True, stop=True)
                    ins.then_inc(s["ret_scores"], 1)

                pe.wait_ge(s["rot_done"], L * per["rot_done"] + 3)
                for h in range(2):
                    ret_scores(h)
                pe.wait_ge(s["state_ready"], L * per["state_ready"] + 3)
                pe.wait_ge(s["delta_out_copied"], L * per["delta_out_copied"] + 4)
                pe.wait_ge(s["hg_dve_step"], L * per["hg_dve_step"] + 14)
                pe.wait_ge(s["rot_done"], L * per["rot_done"] + 4)
                for t in range(4):
                    turn(bank[4 + t], hk_out[:, t * SEQ:(t + 1) * SEQ] if t < 2 else
                         hv[:, (t - 2) * SEQ:(t - 1) * SEQ]).then_inc(s["hg_turned"], 1)
                for h in range(2, 4):
                    pe.wait_ge(s["ret_decayed"], L * per["ret_decayed"] + h - 1)
                    ret_scores(h)
                def mean_square(t):
                    pe.wait_ge(s["out_squared"], L * per["out_squared"] + t + 1)
                    if t >= 2:
                        pe.wait_ge(s["out_log"], L * per["out_log"] + t - 1)
                    mm(bank[t % 2][:, :], const("mean128" if t < 4 else "mean64"), sq_ring[:, t % 4, :], start=True,
                       stop=True).then_inc(s["out_mean_square"], 1)

                pe.wait_ge(s["hg_turned_copied"], L * per["hg_turned_copied"] + 4)
                for t in range(4):
                    turn(bank[4 + t], (rk if t < 2 else rv)[:, t % 2, :]).then_inc(s["ret_turned"], 1)
                pe.wait_ge(s["ret_decayed"], L * per["ret_decayed"] + 4)
                mean_square(0)
                mean_square(1)
                sums(2, hk_tok, hv_tok, s["hg_sums"])
                mean_square(2)
                mean_square(3)
                pe.wait_ge(s["ret_k_out"], L * per["ret_k_out"] + 2)
                pe.wait_ge(s["ret_v_copied"], L * per["ret_v_copied"] + 2)
                sums(4, k_tok, v_tok, s["ret_sums"])
                pe.wait_ge(s["hg_q_in"], L * per["hg_q_in"] + 1)
                outputs(6, hSU, lambda t, o: hq_in[:, t * SEQ + o.start:t * SEQ + o.stop], hv_tok, hPT,
                        s["hg_states"], per["hg_states"], s["hg_out"])
                pe.wait_ge(s["ret_q_in"], L * per["ret_q_in"] + 2)
                outputs(2, SU, lambda t, o: rq[:, t, o], v_tok, PT, s["ret_states"], per["ret_states"], s["ret_out"])

                mean_square(4)
                mean_square(5)

                pe.wait_ge(s["ret_out_copied"], L * per["ret_out_copied"] + 2)
                pe.wait_ge(s["mix_lo_ready"], L * per["mix_lo_ready"] + 1)
                rows(L, OUT0, 0, h_hi[:, 0, :], h_lo[:, 0, :], True, False, tiles=range(KT - 2))
                mean_square(6)
                mean_square(7)
                pe.wait_ge(s["out_log"], L * per["out_log"] + 8)
                rows(L, OUT0, 0, h_hi[:, 0, :], h_lo[:, 0, :], True, False, tiles=range(KT - 2, KT))
                pe.wait_ge(s["mix_lo_ready"], L * per["mix_lo_ready"] + 2)
                rows(L, OUT0 + 1, 1, h_hi[:, 1, :], h_lo[:, 1, :], False, False)
                pe.wait_ge(s["mix_lo_ready"], L * per["mix_lo_ready"] + 8)
                apart(pe)
                with pe.Fori(1, OUT_UNITS // 2 - 1) as i:
                    for u in range(2):
                        rows(L, OUT0 + 2 * i + u, u, h_hi[:, bass.ds(2 * i + u, 1), :],
                             h_lo[:, bass.ds(2 * i + u, 1), :], False, False)
                rows(L, OUT0 + 6, 0, h_hi[:, 6, :], h_lo[:, 6, :], False, False)
                rows(L, OUT0 + 7, 1, h_hi[:, 7, :], h_lo[:, 7, :], False, True, s["out_projected"])

                norm(L, 1)

                first_unit(L, UP0, 8)
                unit(L, UP0 + 1, 1)
                with pe.Fori(1, FT) as i:
                    for u in range(2):
                        pe.wait_ge(s["ffn_conv_done"], L * per["ffn_conv_done"] + 2 * i + u - 1)
                        unit(L, UP0 + 2 * i + u, u)

                pe.wait_ge(s["g_lo_ready"], L * per["g_lo_ready"] + 2)
                for u in range(2):
                    rows(L, DOWN0 + u, u, g_hi[:, u, :], g_lo[:, u, :], u == 0, False, over_up=u == 0)
                pe.wait_ge(s["g_lo_ready"], L * per["g_lo_ready"] + FT)
                apart(pe)
                with pe.Fori(1, DOWN_UNITS // 2 - 1) as i:
                    for u in range(2):
                        rows(L, DOWN0 + 2 * i + u, u, g_hi[:, bass.ds(2 * i + u, 1), :],
                             g_lo[:, bass.ds(2 * i + u, 1), :], False, False)
                rows(L, DOWN0 + 20, 0, g_hi[:, 20, :], g_lo[:, 20, :], False, False)
                rows(L, DOWN0 + 21, 1, g_hi[:, 21, :], g_lo[:, 21, :], False, True, s["down_projected"])
            norm(DEPTH, 0)


def constants():
    f8 = np.float64
    i = np.arange(C)
    col = np.zeros((P, N_CONST), np.float32)

    def put(name, a):
        at, n = CONSTS[name]
        col[:, at:at + n] = np.asarray(a, f8).reshape(P, n)

    put("ident", np.eye(C))
    put("mean_model", np.full((P, P), 1.0 / D_MODEL))
    put("ones", np.ones((P, P)))
    block = np.kron(np.eye(2), np.ones((64, 64)))
    put("blocks", block)
    put("mean64", block / 64)
    put("mean128", np.full((P, P), 1.0 / P))
    put("causal", i[:, None] <= i[None, :])
    put("lvl", np.stack([(j0 % 2 == 0) & (i0 == j0 + 1) for half in LEVELS
                         for j0, i0 in [(i[:, None] // half, i[None, :] // half)]], 1))
    log_gamma = np.log1p(-np.exp2(-5.0 - np.arange(HEADS)))
    rel = i[None, :] - i[:, None]
    scale = 64.0 ** -0.5
    put("ret_decay", np.stack([np.where(rel >= 0, np.exp(np.maximum(rel, 0) * lg), 0.0) * scale
                               for lg in log_gamma], 1))
    head = 2 * np.arange(2)[None, :] + (np.arange(P) // 64)[:, None]
    put("ret_q", np.exp((i + 1.0)[None, None, :] * log_gamma[head][:, :, None]))
    head_row = 2 * np.arange(2)[:, None] + (np.arange(P) // 64)[None, :]
    put("ret_k", np.exp((C - 1.0 - i)[:, None, None] * log_gamma[head_row][None]) * scale)
    put("ret_w", np.exp(C * log_gamma[head]))
    rot = np.zeros((P, P))
    for m in range(P):
        if m % 64 < 32:
            rot[m + 32, m] = -1.0
        else:
            rot[m - 32, m] = 1.0
    put("rot", rot)
    half = np.float32(32)
    inv = np.float32(10000.0) ** (-np.arange(32, dtype=np.float32) / half)
    put("inv_freq", np.tile(inv, 4)[:, None])
    return col


def kernel(**inputs):
    import concourse.bacc as bacc
    from concourse.bass_utils import run_bass_kernel_spmd

    a = {k: np.asarray(v) for k, v in inputs.items()}

    def tiles(v):
        return v.reshape(-1, P).T

    starts = ([1280, 1408, 1536, 1664] + [P * j for j in range(6)]
              + [2048 + P * j for j in range(12)]
              + [3592 + P * j for j in range(4)] + [1792, 1920, 768, 896, 1024, 1152])
    ups = [o for j in range(FT) for o in (P * j, D_FF + P * j)]
    units, params = [], []
    for layer in range(DEPTH):
        w_in, w_up = a["w_in"][layer], a["w_up"][layer]
        for w, cols in ((w_in, starts), (w_up, ups)):
            blocks = [w[:, o:o + P].reshape(KT, P, P).transpose(1, 0, 2).reshape(P, KT * P) for o in cols]
            units += blocks
            if w is w_in:
                units += [a["w_out"][layer].reshape(KT, P, D_MODEL)[t] for t in (4, 5, 6, 7, 2, 3, 0, 1)]
        units += list(a["w_down"][layer].reshape(FT, P, D_MODEL))
        ab = w_in[:, 3584:3592].reshape(KT, P, 8).transpose(1, 0, 2).reshape(P, KT * 8)
        gconv = a["gdn_conv_w"][layer].T.reshape(12, P, 4).transpose(1, 0, 2).reshape(P, 48)
        fconv = a["ffn_conv_w"][layer].T.reshape(2, FT, P, 3).transpose(2, 1, 0, 3).reshape(P, -1)
        fbias = a["ffn_conv_b"][layer].reshape(2, FT, P).transpose(2, 1, 0).reshape(P, -1)
        ones = np.ones((P, 2), np.float32)
        hgn = np.tile(a["hg_norm_w"][layer], 2)[:, None]
        gdn = a["gdn_norm_w"][layer][:, None]
        wide = [np.broadcast_to(a[k][layer][None, :], (P, HEADS)) for k in ("gdn_A_log", "gdn_dt_bias")]
        params.append(np.concatenate([tiles(a["norm1_w"][layer]), tiles(a["norm2_w"][layer]), gconv, fconv, fbias,
                                      gdn, gdn, gdn, gdn, hgn, hgn, ones, *wide, ab], axis=1))
    arrays = {
        "x_t": a["x"][0].T.reshape(KT, P, SEQ).transpose(1, 0, 2),
        "positions": np.broadcast_to(a["positions"][0][None, :], (P, SEQ)),
        "constants": constants(),
        "params": np.stack(params, axis=1),
        "lb_logits": a["hg_lb_logits"].reshape(DEPTH, 2, P).transpose(2, 0, 1),
        "final_norm": tiles(a["final_norm_w"]),
        "weights": np.stack(units),
    }
    arrays = {k: np.ascontiguousarray(v) for k, v in arrays.items()}
    nc = bacc.Bacc("TRN2", target_bir_lowering=False, num_devices=1)
    args = [nc.dram_tensor(k, v.shape, mybir.dt.from_np(v.dtype), kind="ExternalInput").ap()
            for k, v in arrays.items()]
    args.append(nc.dram_tensor("out_t", (P, KT, SEQ), F32, kind="ExternalOutput").ap())
    build(nc, *args)
    r = run_bass_kernel_spmd(nc, [arrays], core_ids=[0])
    return r.results[0]["out_t"].transpose(2, 1, 0).reshape(1, SEQ, D_MODEL)
```
